# Optimizing a Trainium2 kernel written in Bass

```python
import jax, jax.numpy as jnp
from jax import lax
import numpy as np

D_MODEL = 2048
BATCH = 1
SEQ = 256
DEPTH = 1

HEAD_DIM = 128
N_SB_HEADS = 8
N_DSA_HEADS = 8
N_IDX_HEADS = 16
IDX_DIM = 64
ROPE_THETA = 500000.0
ROPE_DIM = HEAD_DIM // 4
IDX_ROPE_DIM = IDX_DIM // 4
MAX_TOPK = 256
D_FF = 5632
CONV_WIDTH = 3
Q_BLOCK = 128
EPS = 1e-6

SB_W = N_SB_HEADS * HEAD_DIM
DSA_W = N_DSA_HEADS * HEAD_DIM
IDX_QW = N_IDX_HEADS * IDX_DIM
IN_SPLITS = (SB_W, SB_W, SB_W, DSA_W, DSA_W, DSA_W, IDX_QW, IDX_DIM, N_IDX_HEADS, D_MODEL, D_MODEL)
IN_COLS = sum(IN_SPLITS)
IN_OFFSETS = tuple(int(v) for v in np.cumsum(IN_SPLITS)[:-1])

kernel_name = "hybrid_stickbreak_dsa_convffn"

def rms_norm(x, g):
    xf = x.astype(jnp.float32)
    y = xf * lax.rsqrt(jnp.mean(xf * xf, axis=-1, keepdims=True) + EPS)
    return (y * g.astype(jnp.float32)).astype(x.dtype)

def partial_rope(x, positions, rot_dim):
    half = rot_dim // 2
    freqs = ROPE_THETA ** (-jnp.arange(0, rot_dim, 2, dtype=jnp.float32) / rot_dim)
    ang = positions.astype(jnp.float32)[..., None] * freqs
    cos = jnp.cos(ang)[:, :, None, :].astype(x.dtype)
    sin = jnp.sin(ang)[:, :, None, :].astype(x.dtype)
    x1, x2, rest = x[..., :half], x[..., half:rot_dim], x[..., rot_dim:]
    return jnp.concatenate([x1 * cos - x2 * sin, x1 * sin + x2 * cos, rest], axis=-1)

def to_blocks(a):
    b, s = a.shape[:2]
    return a.reshape(b, s // Q_BLOCK, Q_BLOCK, *a.shape[2:]).swapaxes(0, 1)

def from_blocks(a):
    nb, b, qb = a.shape[:3]
    return a.swapaxes(0, 1).reshape(b, nb * qb, *a.shape[3:])

def stick_breaking_attention(q, k, v):
    S = q.shape[1]
    scale = HEAD_DIM ** -0.5
    key_pos = jnp.arange(S)
    starts = jnp.arange(S // Q_BLOCK, dtype=jnp.int32) * Q_BLOCK

    def block(args):
        qb, start = args
        z = jnp.einsum('bqhd,bshd->bhqs', qb, k).astype(jnp.float32) * scale
        t = start + jnp.arange(Q_BLOCK)
        mask = key_pos[None, :] < t[:, None]
        log_beta = jax.nn.log_sigmoid(z)
        log_1mb = jnp.where(mask, jax.nn.log_sigmoid(-z), 0.0)
        suffix = lax.cumsum(log_1mb, axis=3, reverse=True) - log_1mb
        a = jnp.where(mask, jnp.exp(log_beta + suffix), 0.0)
        return jnp.einsum('bhqs,bshd->bqhd', a.astype(v.dtype), v)

    out = lax.map(block, (to_blocks(q), starts))
    return from_blocks(out)

def indexed_sparse_attention(q, k, v, iq, ik, iw, topk):
    B, S = q.shape[:2]
    scale = HEAD_DIM ** -0.5
    idx_scale = IDX_DIM ** -0.5 * N_IDX_HEADS ** -0.5
    key_pos = jnp.arange(S)
    bidx = jnp.arange(B)[:, None, None]
    starts = jnp.arange(S // Q_BLOCK, dtype=jnp.int32) * Q_BLOCK

    def block(args):
        qb, iqb, iwb, start = args
        t = start + jnp.arange(Q_BLOCK)
        sc = jnp.einsum('bqhd,bsd->bqhs', iqb, ik).astype(jnp.float32)
        score = jnp.einsum('bqhs,bqh->bqs', jax.nn.relu(sc), iwb.astype(jnp.float32) * idx_scale)
        causal = key_pos[None, :] <= t[:, None]
        score = jnp.where(causal[None], score, -jnp.inf)
        _, sel = lax.top_k(score, topk)
        valid = sel <= t[None, :, None]
        k_sel = k[bidx, sel]
        v_sel = v[bidx, sel]
        logits = jnp.einsum('bqhd,bqkhd->bhqk', qb, k_sel).astype(jnp.float32) * scale
        logits = jnp.where(valid[:, None], logits, -jnp.inf)
        p = jax.nn.softmax(logits, axis=-1)
        return jnp.einsum('bhqk,bqkhd->bqhd', p.astype(v.dtype), v_sel)

    out = lax.map(block, (to_blocks(q), to_blocks(iq), to_blocks(iw), starts))
    return from_blocks(out)

def causal_depthwise_conv(u, w, b):
    C = u.shape[-1]
    y = lax.conv_general_dilated(u, w[:, None, :].astype(u.dtype), window_strides=(1,),
                                 padding=[(CONV_WIDTH - 1, 0)],
                                 dimension_numbers=('NWC', 'WIO', 'NWC'),
                                 feature_group_count=C)
    return y + b

def setup_inputs(seed: int = 0) -> dict:
    key = jax.random.key(seed)
    ks = jax.random.split(key, 13)
    f32 = jnp.float32
    x = jax.random.normal(ks[0], (BATCH, SEQ, D_MODEL), f32)
    positions = jnp.broadcast_to(jnp.arange(SEQ, dtype=jnp.int32), (BATCH, SEQ))
    attn_norm_g = 1.0 + 0.02 * jax.random.normal(ks[1], (D_MODEL,), f32)
    w_in = jax.random.normal(ks[2], (D_MODEL, IN_COLS), f32) * D_MODEL ** -0.5
    q_norm_g = 1.0 + 0.02 * jax.random.normal(ks[3], (HEAD_DIM,), f32)
    k_norm_g = 1.0 + 0.02 * jax.random.normal(ks[4], (HEAD_DIM,), f32)
    w_branch = jax.random.normal(ks[5], (SB_W + DSA_W, D_MODEL), f32) * SB_W ** -0.5
    w_out = jax.random.normal(ks[6], (D_MODEL, D_MODEL), f32) * D_MODEL ** -0.5
    ffn_norm_g = 1.0 + 0.02 * jax.random.normal(ks[7], (D_MODEL,), f32)
    w_up = jax.random.normal(ks[8], (D_MODEL, 2 * D_FF), f32) * D_MODEL ** -0.5
    conv_w = jax.random.normal(ks[9], (CONV_WIDTH, 2 * D_FF), f32) * CONV_WIDTH ** -0.5
    conv_b = 0.01 * jax.random.normal(ks[10], (2 * D_FF,), f32)
    w_down = jax.random.normal(ks[11], (D_FF, D_MODEL), f32) * D_FF ** -0.5
    return {"x": x, "positions": positions, "attn_norm_g": attn_norm_g, "w_in": w_in,
            "q_norm_g": q_norm_g, "k_norm_g": k_norm_g, "w_branch": w_branch, "w_out": w_out,
            "ffn_norm_g": ffn_norm_g, "w_up": w_up, "conv_w": conv_w, "conv_b": conv_b,
            "w_down": w_down}

def reference(x, positions, attn_norm_g, w_in, q_norm_g, k_norm_g, w_branch, w_out,
              ffn_norm_g, w_up, conv_w, conv_b, w_down):
    B, S, _ = x.shape
    topk = min(MAX_TOPK, S // 4)
    for _layer in range(DEPTH):
        h = rms_norm(x, attn_norm_g)
        proj = h @ w_in
        (q_sb, k_sb, v_sb, q_ds, k_ds, v_ds, q_ix, k_ix, w_ix, g_sb, g_ds) = jnp.split(proj, IN_OFFSETS, axis=-1)
        heads = lambda a, n, d: a.reshape(B, S, n, d)

        o_sb = stick_breaking_attention(heads(q_sb, N_SB_HEADS, HEAD_DIM),
                                        heads(k_sb, N_SB_HEADS, HEAD_DIM),
                                        heads(v_sb, N_SB_HEADS, HEAD_DIM)).reshape(B, S, SB_W)

        qd = partial_rope(rms_norm(heads(q_ds, N_DSA_HEADS, HEAD_DIM), q_norm_g), positions, ROPE_DIM)
        kd = partial_rope(rms_norm(heads(k_ds, N_DSA_HEADS, HEAD_DIM), k_norm_g), positions, ROPE_DIM)
        vd = heads(v_ds, N_DSA_HEADS, HEAD_DIM)
        iq = partial_rope(heads(q_ix, N_IDX_HEADS, IDX_DIM), positions, IDX_ROPE_DIM)
        ik = partial_rope(k_ix[:, :, None, :], positions, IDX_ROPE_DIM)[:, :, 0, :]
        o_ds = indexed_sparse_attention(qd, kd, vd, iq, ik, w_ix, topk).reshape(B, S, DSA_W)

        merged = (jax.nn.sigmoid(g_sb) * (o_sb @ w_branch[:SB_W])
                  + jax.nn.sigmoid(g_ds) * (o_ds @ w_branch[SB_W:]))
        x = x + merged @ w_out

        h = rms_norm(x, ffn_norm_g)
        u = causal_depthwise_conv(h @ w_up, conv_w, conv_b)
        gate, val = jnp.split(u, 2, axis=-1)
        x = x + (jax.nn.silu(gate) * val) @ w_down
    return x


_drawn_inputs = setup_inputs


def setup_inputs(seed=0):
    import zlib

    import numpy as np

    out = dict(_drawn_inputs(seed))
    spreads = {}
    factors = {'attn_norm_g': 3.152, 'q_norm_g': 8.0, 'k_norm_g': 8.0, 'ffn_norm_g': 3.947, 'conv_b': 8.0}
    for name, (base, spread) in spreads.items():
        noise = np.random.default_rng([zlib.crc32(name.encode()), seed]).standard_normal(out[name].shape)
        drawn = base * np.exp(spread * noise) if base else spread * noise
        out[name] = __import__('jax').numpy.asarray(drawn.astype(out[name].dtype))
    for name, factor in factors.items():
        out[name] = (out[name] * factor).astype(out[name].dtype)
    return out
```

```python
import math

import numpy as np

import concourse.bass as bass
from concourse import mybir
from contextlib import ExitStack


def hybrid_layer(nc, x, positions, attn_norm_g, w_in, q_norm_g, k_norm_g, w_branch, w_out,
                 ffn_norm_g, w_up, conv_w, conv_b, w_down, out):
    f32 = mybir.dt.float32
    f32r = mybir.dt.float32r
    i32 = mybir.dt.int32
    ACT = mybir.ActivationFunctionType
    ALU = mybir.AluOpType
    AX = mybir.AxisListType
    ds = bass.ds

    P = 128
    S, D = x.shape[1], x.shape[2]
    TH = S // P
    KT = D // P
    HD = 128
    NH = 8
    NI, ID = 16, 64
    FF = w_down.shape[0]
    FT = FF // P
    TOPK = min(256, S // 4)
    EPS = 1e-6
    SCALE = HD ** -0.5
    IDX_SCALE = ID ** -0.5 * NI ** -0.5
    HALF = HD // 4 // 2
    IHALF = ID // 4 // 2
    GRP = 512
    CK = 2
    CPG = KT // CK
    BLOCK = 2 * GRP
    SLOTS = 4
    AHEAD = 3
    NB = 5
    TAIL_AT = 7 * BLOCK
    TAIL = ID + NI
    TAIL_CK = 4
    GATE_AT = TAIL_AT + TAIL
    KEYS = P + S

    C_ROWS = KT // TAIL_CK
    C_HEADS = C_ROWS + NB * 2 * CPG
    C_GATES = C_HEADS + 4 * CPG
    C_BRANCH = C_GATES + 8 * CPG
    C_OUT = C_BRANCH + 4 * CPG
    C_UP = C_OUT + 4 * CPG
    NU = FF // GRP
    C_DOWN = C_UP + NU * 2 * CPG
    for first in (C_ROWS, C_HEADS, C_GATES, C_BRANCH, C_OUT, C_UP, C_DOWN):
        assert first % SLOTS == 0

    NONCAUSAL, TAKEN, MASKED = -1e38, -3e38, -1e30
    ROUND = 1.5 * 2.0 ** 23
    TWO_PI_A, TWO_PI_B = 6.28125, 0.00193500518798828125
    TWO_PI_C = 2 * math.pi - TWO_PI_A - TWO_PI_B
    SIN_MAX = 3.1415925
    FREQS = [float(np.float32(500000.0) ** np.float32(-i / HALF)) for i in range(HALF)]

    ctx = ExitStack()
    with ctx:
        KB = 1024
        ARENA = 206 * KB
        arena = ctx.enter_context(nc.sbuf_tensor("arena", [P, ARENA // 4], f32))
        base = nc.lookup_mloc(arena).addr

        def at(name, shape, offset, dtype=f32):
            assert offset + 4 * int(np.prod(shape)) <= ARENA
            return nc.alloc_sbuf_tensor_at(name, [P, *shape], dtype, offset=base + offset)

        def sem(name):
            return ctx.enter_context(nc.semaphore(name))

        hT = at("hT", [KT, 2 * S], 0, f32r)
        mT = at("mT", [KT, 2 * S], 0, f32r)
        tok = at("tok", [NB, TH, BLOCK], 32 * KB)
        gates = at("gates", [2 * KT, S], 72 * KB)
        xn = at("xn", [TH, D], 72 * KB)
        y = at("y", [TH, D], 88 * KB)
        ffT = at("ffT", [FT, 2 * S], 0, f32r)
        qkT = at("qkT", [2 * NH, 2 * S], 104 * KB)
        oT = at("oT", [2 * NH, 2 * S], 104 * KB, f32r)
        h2T = at("h2T", [KT, 2 * S], 104 * KB, f32r)
        raw = [at(f"raw{i}", [2 * GRP], (136 + 4 * i) * KB) for i in range(SLOTS)]
        hi = [at(f"hi{i}", [2 * GRP], (152 + 4 * i) * KB, f32r) for i in range(SLOTS)]
        lo = [at(f"lo{i}", [2 * GRP], (168 + 4 * i) * KB, f32r) for i in range(SLOTS)]
        ident = at("ident", [P], 184 * KB)
        params = at("params", [2 * KT + 4 * 2 * FT], 184 * KB + 512)
        A0 = 186 * KB
        neg_tri = at("neg_tri", [P], A0)
        neg_one = at("neg_one", [P], A0 + 512)
        qk_gain = at("qk_gain", [2, HD], A0 + 1024)
        tail = at("tail", [TH, TAIL], A0 + 2048)
        wix = at("wix", [TH, NI], A0 + 2688)
        cos_d = at("cos_d", [4, 2 * HALF], A0 + 2816)
        sin_d = at("sin_d", [4, 2 * HALF], A0 + 3328)
        cos_i = at("cos_i", [TH, 2 * IHALF], A0 + 3840)
        sin_i = at("sin_i", [TH, 2 * IHALF], A0 + 3968)
        bias = at("bias", [KEYS], A0 + 4096)
        scores = at("scores", [KEYS], A0 + 5632)
        probT = at("probT", [KEYS], A0 + 5632)
        W0 = A0 + 7 * KB
        part = [at(f"part{i}", [S], W0 + i * KB) for i in range(4)]
        sb_q = at("sb_q", [S], W0 + 4 * KB)
        sb_k = at("sb_k", [S], W0 + 5 * KB)
        ds_qk = at("ds_qk", [2 * S], W0 + 6 * KB)
        sb_v = at("sb_v", [TH, HD], W0 + 8 * KB)
        ds_v = at("ds_v", [TH, HD], W0 + 9 * KB)
        partb = [at(f"partb{i}", [S], W0 + (4 + i) * KB) for i in range(4)]
        Z0 = A0 + 19 * KB
        ss = at("ss", [TH, 4], Z0)
        var2 = at("var2", [TH], Z0 + 32)
        inv2 = at("inv2", [TH], Z0 + 64)
        rstd2 = at("rstd2", [TH], Z0 + 96)
        top = at("top", [2], Z0 + 128)
        ntop = at("ntop", [2], Z0 + 160)
        psum_e = at("psum_e", [2], Z0 + 192)
        pinv = at("pinv", [2], Z0 + 224)
        ikT = at("ikT", [2, S], 104 * KB)
        iq = at("iq", [TH, 4, ID], 106 * KB)
        iqT = at("iqT", [2, S], 108 * KB)
        relu = [at(f"relu{i}", [2, KEYS], (110 + 3 * i) * KB) for i in range(2)]
        rot_i = at("rot_i", [2, TH, 4, 2 * IHALF], 116 * KB)
        rows_in = at("rows_in", [6, P], 118 * KB)
        freq = at("freq", [HALF], 121 * KB)
        ang = at("ang", [2, TH, HALF], 121 * KB + 256)
        turn = at("turn", [2, TH, HALF], 121 * KB + 512)
        trig = at("trig", [2, TH, HALF], 121 * KB + 768)
        pos_i = at("pos_i", [TH], 122 * KB, i32)
        pos_f = at("pos_f", [TH], 122 * KB + 64)
        k_ix = at("k_ix", [TH, 2, ID], 123 * KB)
        rot_k = at("rot_k", [2, TH, 2, 2 * IHALF], 124 * KB)
        junk = at("junk", [TH, D], 32 * KB)
        sq = at("sq", [4, 2, HD], 72 * KB)
        qn = at("qn", [4, 2, HD], 76 * KB)
        rot_d = at("rot_d", [2, 4, 2, 2 * HALF], 80 * KB)
        ms = at("ms", [8], 82 * KB)
        inv = at("inv", [8], 82 * KB + 64)
        rstd = at("rstd", [8], 82 * KB + 128)
        best = at("best", [2, 8], 82 * KB + 192)
        soft = at("soft", [KEYS], 64 * KB)
        stay = at("stay", [KEYS], 64 * KB + 1536)
        stick = at("stick", [KEYS], 64 * KB + 3072)
        logit = at("logit", [KEYS], 64 * KB + 4608)
        prob = at("prob", [KEYS], 64 * KB + 6144)
        sig = [[at(f"sig{b}{i}", [S], (32 + 4 * b + i) * KB) for i in range(4)] for b in range(2)]
        br = [[at(f"br{b}{i}", [S], (40 + 4 * b + i) * KB) for i in range(4)] for b in range(2)]
        junk2 = at("junk2", [TH, GRP], 40 * KB)
        U0 = A0
        uprt = [[at(f"uprt{b}{i}", [S], U0 + (2 * b + i) * KB) for i in range(2)] for b in range(2)]
        u = [[at(f"u{b}{i}", [S + 2], U0 + 4 * KB + (2 * b + i) * 1056) for i in range(2)]
             for b in range(2)]
        conv = [[at(f"conv{b}{i}", [S], U0 + 9 * KB + (2 * b + i) * KB) for i in range(2)]
                for b in range(2)]
        silu = [at(f"silu{i}", [S], U0 + (13 + i) * KB) for i in range(4)]

        banks = [ctx.enter_context(nc.psum_tensor(f"bank{i}", [P, 512], f32)) for i in range(8)]
        A, B = banks[:4], banks[4:]

        w_landed = [sem(f"w_landed{i}") for i in range(SLOTS)]
        hi_done = sem("hi_done")
        lo_done = sem("lo_done")
        w_used = sem("w_used")
        x_in = [sem(f"x_in{t}") for t in range(TH)]
        small_in = sem("small_in")
        x_again = sem("x_again")
        const_set = sem("const_set")
        const_sel = sem("const_sel")
        rows_zero = sem("rows_zero")
        freq_set = sem("freq_set")
        pos_done = sem("pos_done")
        trig_step = sem("trig_step")
        angle_done = sem("angle_done")
        sin_done = sem("sin_done")
        cos_set = sem("cos_set")
        ss_done = sem("ss_done")
        var_done = sem("var_done")
        inv_done = sem("inv_done")
        rstd_done = sem("rstd_done")
        xn_done = sem("xn_done")
        params_T = sem("params_T")
        params_done = sem("params_done")
        xT_full = sem("xT_full")
        xT_hi = sem("xT_hi")
        xT_lo = sem("xT_lo")
        tok_full = sem("tok_full")
        tok_done = sem("tok_done")
        wix_done = sem("wix_done")
        kix_a = sem("kix_a")
        kix_b = sem("kix_b")
        kix_done = sem("kix_done")
        kixT_full = sem("kixT_full")
        ikT_zero = sem("ikT_zero")
        ikT_done = sem("ikT_done")
        score_zero = sem("score_zero")
        iq_rot = sem("iq_rot")
        iq_done = sem("iq_done")
        iqT_full = sem("iqT_full")
        iqT_done = sem("iqT_done")
        sc_full = sem("sc_full")
        relu_done = sem("relu_done")
        score_add = sem("score_add")
        score_masked = sem("score_masked")
        best_done = sem("best_done")
        taken_done = sem("taken_done")
        bias_raw = sem("bias_raw")
        bias_done = sem("bias_done")
        sq_done = sem("sq_done")
        ms_done = sem("ms_done")
        msv_done = sem("msv_done")
        hinv_done = sem("hinv_done")
        hrstd_done = sem("hrstd_done")
        qn_scaled = sem("qn_scaled")
        qn_gain = sem("qn_gain")
        qn_rot = sem("qn_rot")
        qn_done = sem("qn_done")
        qn_T = sem("qn_T")
        qkT_done = sem("qkT_done")
        col_full = sem("col_full")
        part_done = sem("part_done")
        col_done = sem("col_done")
        bcol_full = sem("bcol_full")
        bpart_done = sem("bpart_done")
        bcol_done = sem("bcol_done")
        staged_qk = sem("staged_qk")
        staged_v = sem("staged_v")
        sb_k_done = sem("sb_k_done")
        z_full = sem("z_full")
        logit_full = sem("logit_full")
        abs_done = sem("abs_done")
        exp_done = sem("exp_done")
        ln_done = sem("ln_done")
        stay_raw = sem("stay_raw")
        stay_done = sem("stay_done")
        suffix_full = sem("suffix_full")
        stick_raw = sem("stick_raw")
        stick_done = sem("stick_done")
        logit_done = sem("logit_done")
        top_done = sem("top_done")
        ntop_done = sem("ntop_done")
        prob_raw = sem("prob_raw")
        pinv_done = sem("pinv_done")
        prob_done = sem("prob_done")
        probT_full = sem("probT_full")
        probT_done = sem("probT_done")
        sb_full = sem("sb_full")
        ds_full = sem("ds_full")
        sb_hi = sem("sb_hi")
        ds_hi = sem("ds_hi")
        sb_done = sem("sb_done")
        ds_done = sem("ds_done")
        sig_done = sem("sig_done")
        mix_a = sem("mix_a")
        mix_b = sem("mix_b")
        mix_done = sem("mix_done")
        mT_hi = sem("mT_hi")
        mT_done = sem("mT_done")
        row_full = sem("row_full")
        row_done = sem("row_done")
        pad_zero = sem("pad_zero")
        gate_w2 = sem("gate_w2")
        gate_w1 = sem("gate_w1")
        gate_w0 = sem("gate_w0")
        silu_done = sem("silu_done")
        val_w2 = sem("val_w2")
        val_w1 = sem("val_w1")
        val_w0 = sem("val_w0")
        val_bias = sem("val_bias")
        act_done = sem("act_done")
        ffT_hi = sem("ffT_hi")
        ffT_done = sem("ffT_done")
        down_full = sem("down_full")
        out_ready = sem("out_ready")
        stored = sem("stored")
        passed = sem("passed")

        block = ctx.enter_context(nc.Block())

        def wait_alone(engine, semaphore, value):
            engine.wait_ge(semaphore, value)
            engine.sem_inc(passed, 1)

        def prime(engine, *semaphores):
            for s in semaphores:
                engine.sem_inc(s, 1)

        def wait_full(engine, full, group, count, bank, end):
            if bank < count - 1:
                engine.wait_ge(full, (count - 1) * group + bank + 1)
            else:
                engine.wait_ge(w_used, end)

        @block.sync
        def _(sp):
            def load(slot, dst, src):
                sp.dma_start(dst, src).then_inc(w_landed[slot], 16)

            def load_group(c0, w, step, col, n=CPG, width=GRP, per=CK):
                for j in range(n):
                    wait_alone(sp, lo_done, c0 + j - AHEAD + step)
                    rows = w[j * per * P:(j + 1) * per * P, ds(col, width)]
                    load(j % SLOTS, raw[j % SLOTS][:, :].rearrange("p (k c) -> p k c", k=per),
                         rows.rearrange("(k p) c -> p k c", p=P))

            for t in range(TH):
                sp.dma_start(y[:, t, :], x[0, t * P:(t + 1) * P, :]).then_inc(x_in[t], 16)
            for c in range(C_ROWS):
                rows = w_in[c * TAIL_CK * P:(c + 1) * TAIL_CK * P, TAIL_AT:TAIL_AT + TAIL]
                load(c, raw[c][:, 0:TAIL_CK * TAIL].rearrange("p (k c) -> p k c", k=TAIL_CK),
                     rows.rearrange("(k p) c -> p k c", p=P))
            with sp.Fori(0, NB) as b:
                for g in range(2):
                    load_group(C_ROWS + g * CPG, w_in, 2 * CPG * b,
                               2 * BLOCK + (NB - 1) * BLOCK + g * GRP - BLOCK * b)
            with sp.Fori(0, 4) as g:
                load_group(C_HEADS, w_in, CPG * g, GRP * g)
            with sp.Fori(0, 8) as g:
                load_group(C_GATES, w_in, CPG * g, GATE_AT + GRP * g)
            with sp.Fori(0, 4) as g:
                load_group(C_BRANCH, w_branch, CPG * g, GRP * g)
            with sp.Fori(0, 4) as g:
                load_group(C_OUT, w_out, CPG * g, GRP * g)
            with sp.Fori(0, NU) as n:
                for b in range(2):
                    load_group(C_UP + b * CPG, w_up, 2 * CPG * n, b * FF + GRP * n)
            with sp.Fori(0, 2) as m:
                load_group(C_DOWN, w_down, FT * m, BLOCK * m, n=FT, width=BLOCK, per=1)
            for m in range(2):
                for t in range(TH):
                    for h in range(2):
                        cols = slice(m * BLOCK + h * GRP, m * BLOCK + (h + 1) * GRP)
                        sp.wait_ge(out_ready, 4 * m + 2 * t + h + 1)
                        sp.dma_start(out[0, t * P:(t + 1) * P, cols], y[:, t, cols])\
                            .then_inc(stored, 16)
            sp.wait_ge(stored, 16 * 4 * TH)

        @block.scalar
        def _(act):
            def split(c0, step=0, slots=1, width=2 * GRP):
                s = c0 % SLOTS
                act.wait_ge(w_landed[s], 16 * (c0 // SLOTS + 1) + 16 * slots * step)
                if c0 >= SLOTS:
                    act.wait_ge(w_used, c0 - SLOTS + 1 + SLOTS * slots * step)
                act.activation(hi[s][:, 0:width], raw[s][:, 0:width], ACT.Copy)\
                    .then_inc(hi_done, 1)

            def norm_rstd(k):
                act.wait_ge(inv_done, k + 1)
                act.activation(rstd2[:, :], inv2[:, :], ACT.Sqrt).then_inc(rstd_done, 1)

            def transposed_hi(dst, gain, k):
                for kt in range(KT):
                    act.wait_ge(xT_full, k * KT + kt + 1)
                    act.activation(dst[:, kt, 0:S], B[kt % 4][:, 0:S], ACT.Copy,
                                   scale=params[:, gain + kt:gain + kt + 1]).then_inc(xT_hi, 1)

            prime(act, relu_done)
            act.wait_ge(rows_zero, 1)
            act.dma_start(rows_in[0:KT, 0, :], attn_norm_g.rearrange("(t p) -> t p", p=P))\
                .then_inc(small_in, 16)
            act.dma_start(rows_in[0:KT, 1, :], ffn_norm_g.rearrange("(t p) -> t p", p=P))\
                .then_inc(small_in, 16)
            act.dma_start(rows_in[0:2 * FT, 2:5, :], conv_w.rearrange("k (t p) -> t k p", p=P))\
                .then_inc(small_in, 16)
            act.dma_start(rows_in[0:2 * FT, 5, :], conv_b.rearrange("(t p) -> t p", p=P))\
                .then_inc(small_in, 16)
            act.dma_start(qk_gain[:, 0, :], q_norm_g.partition_broadcast(P)).then_inc(small_in, 16)
            act.dma_start(qk_gain[:, 1, :], k_norm_g.partition_broadcast(P)).then_inc(small_in, 16)
            for t in range(TH):
                act.dma_start(pos_i[:, t:t + 1], positions[0, t * P:(t + 1) * P].unsqueeze(1))\
                    .then_inc(small_in, 16)
            for t in range(TH):
                act.wait_ge(x_in[t], 16)
                act.activation(junk[:, t, :], y[:, t, :], ACT.Square, accum_out=ss[:, t, 0:1])\
                    .then_inc(ss_done, 1)
            norm_rstd(0)
            act.wait_ge(params_T, 1)
            act.activation(params[:, :], B[3][:, 0:2 * KT + 8 * FT], ACT.Copy)\
                .then_inc(params_done, 1)
            act.wait_ge(params_done, 1)
            transposed_hi(hT, 0, 0)
            for c in range(C_ROWS):
                split(c, width=TAIL_CK * TAIL)
            for c in range(C_ROWS, C_ROWS + AHEAD):
                split(c)
            act.wait_ge(angle_done, 1)
            act.activation(trig[:, :, :, :], ang[:, :, :, :], ACT.Sin).then_inc(sin_done, 1)
            for t in range(TH):
                wait_full(act, tok_full, 0, TH, t, C_ROWS)
                act.activation(tail[:, t, :], A[t][:, 0:TAIL], ACT.Copy).then_inc(tok_done, 1)
            act.wait_ge(kixT_full, 1)
            act.wait_ge(ikT_zero, 1)
            for h in range(2):
                act.activation(ikT[h * ID:(h + 1) * ID, h, :], B[0][h * ID:(h + 1) * ID, 0:S],
                               ACT.Copy).then_inc(ikT_done, 1)

            def rows_body(b, index):
                for g in range(2):
                    for j in range(CPG):
                        split(C_ROWS + AHEAD + g * CPG + j, b, 2 * CPG // SLOTS)
                        if not index:
                            continue
                        if g == 0 and j == 5:
                            act.wait_ge(iqT_full, 1 + b)
                            act.activation(iqT[:, :, :], B[0][:, :], ACT.Copy)\
                                .then_inc(iqT_done, 1)
                        if g == 1 and j in (1, 5):
                            pair = j // 4
                            at0, at1 = (B[1], B[2]) if pair == 0 else (B[3], B[0])
                            act.wait_ge(sc_full, 4 * (b - 1) + 2 * pair + 1)
                            act.activation(relu[pair][:, :, 0:P],
                                           at0[:, 0:2 * P].rearrange("p (h k) -> p h k", h=2),
                                           ACT.Relu).then_inc(relu_done, 1)
                            act.wait_ge(sc_full, 4 * (b - 1) + 2 * pair + 2)
                            act.activation(relu[pair][:, :, P:KEYS],
                                           at1[:, :].rearrange("p (h k) -> p h k", h=2),
                                           ACT.Relu).then_inc(relu_done, 1)
                    for t in range(TH):
                        wait_full(act, tok_full, 1 + 2 * b + g, TH, t,
                                  C_ROWS + CPG * (g + 1) + 2 * CPG * b)
                        act.activation(tok[:, ds(NB - 1 - b, 1), t, g * GRP:(g + 1) * GRP],
                                       A[2 * g + t][:, :].unsqueeze(1), ACT.Copy)\
                            .then_inc(tok_done, 1)

            rows_body(0, False)
            with act.Fori(1, NB) as b:
                rows_body(b, True)

            def column_halves(full, done, bank, dst, group, end, tiles=range(4)):
                for ct in tiles:
                    wait_full(act, full, group, 4, ct, end)
                    act.activation(dst[ct][:, :], bank[ct][:, S:2 * S], ACT.Copy).then_inc(done, 1)

            def heads_body(qk, half):
                i = 2 * qk + half
                for j in range(CPG):
                    split(C_HEADS + AHEAD + j, i, CPG // SLOTS)
                    if j == 1:
                        act.activation(sq[:, :, :, :].rearrange("p r h d -> p r (h d)"),
                                       tok[:, 1:3, :, ds(2 * HD * i, 2 * HD)]
                                       .rearrange("p b t c -> p (b t) c"),
                                       ACT.Square).then_inc(sq_done, 1)
                    if j == 3:
                        act.wait_ge(hinv_done, i + 1)
                        act.activation(rstd[:, :], inv[:, :], ACT.Sqrt).then_inc(hrstd_done, 1)
                column_halves(col_full, part_done, A, part, i, C_HEADS + CPG + CPG * i)
                for r in range(2):
                    act.wait_ge(qn_T, 2 * i + r + 1)
                    act.activation(qkT[:, ds(NH + 2 * i, 2), r * S:(r + 1) * S],
                                   B[r][:, :].rearrange("p (h s) -> p h s", h=2),
                                   ACT.Copy).then_inc(qkT_done, 1)

            act.wait_ge(tok_done, 2 + 4 * NB)
            with act.Fori(0, 2) as qk:
                with act.Fori(0, 2) as half:
                    heads_body(qk, half)

            def gates_body(h):
                for j in range(CPG):
                    split(C_GATES + AHEAD + j, h, CPG // SLOTS)
                    if j == 1:
                        act.wait_ge(z_full, h + 1)
                        act.activation(soft[:, :], B[0][:, 0:KEYS], ACT.Abs).then_inc(abs_done, 1)
                        act.wait_ge(abs_done, h + 1)
                        act.activation(soft[:, :], soft[:, :], ACT.Exp, scale=-1.0)\
                            .then_inc(exp_done, 1)
                        act.wait_ge(exp_done, h + 1)
                        act.activation(soft[:, :], soft[:, :], ACT.Ln, bias=1.0)\
                            .then_inc(ln_done, 1)
                    if j == 2:
                        act.wait_ge(ntop_done, h + 1)
                        for t, (k0, k1) in enumerate(((0, P), (P, KEYS))):
                            act.activation(prob[:, k0:k1], logit[:, k0:k1], ACT.Exp,
                                           bias=ntop[:, t:t + 1], scale=SCALE,
                                           accum_out=psum_e[:, t:t + 1]).then_inc(prob_raw, 1)
                    if j == 5:
                        act.wait_ge(suffix_full, h + 1)
                        act.activation(stick[:, :], B[0][:, 0:KEYS], ACT.Exp)\
                            .then_inc(stick_raw, 1)
                    if j == 6:
                        act.wait_ge(probT_full, h + 1)
                        act.activation(probT[:, :], B[3][:, 0:KEYS], ACT.Copy)\
                            .then_inc(probT_done, 1)
                column_halves(col_full, part_done, A, part, 4 + h, C_GATES + CPG + CPG * h)
                for full, done, bank, at_head in ((sb_full, sb_hi, B[2], h),
                                                  (ds_full, ds_hi, B[3], NH + h)):
                    act.wait_ge(full, 1 + h + 1)
                    act.activation(oT[:, ds(at_head, 1), 0:S], bank[:, 0:S].unsqueeze(1),
                                   ACT.Copy).then_inc(done, 1)

            with act.Fori(0, NH) as h:
                gates_body(h)

            with act.Fori(0, 4) as n:
                for j in range(CPG):
                    split(C_BRANCH + AHEAD + j, n, CPG // SLOTS)
                    if j >= 4:
                        column_halves(col_full, part_done, A, part, 12 + n,
                                      C_BRANCH + CPG // 2 + CPG * n, [j - 4])
                        act.activation(sig[0][j - 4][:, :].unsqueeze(1),
                                       gates[:, ds(4 * n + j - 4, 1), :],
                                       ACT.Sigmoid).then_inc(sig_done, 1)
                for ct in range(4):
                    column_halves(bcol_full, bpart_done, B, partb, n, C_BRANCH + CPG + CPG * n, [ct])
                    act.activation(sig[1][ct][:, :].unsqueeze(1),
                                   gates[:, ds(KT + 4 * n + ct, 1), :],
                                   ACT.Sigmoid).then_inc(sig_done, 1)
                for ct in range(4):
                    act.wait_ge(mix_done, 4 * n + ct + 1)
                    act.activation(mT[:, ds(4 * n + ct, 1), 0:S], br[0][ct][:, :].unsqueeze(1),
                                   ACT.Copy).then_inc(mT_hi, 1)

            with act.Fori(0, 2) as m:
                for g in range(2):
                    for j in range(CPG):
                        split(C_OUT + AHEAD + g * CPG + j, m, 2 * CPG // SLOTS)
                    for t in range(TH):
                        act.wait_ge(row_done, 4 * m + 2 * g + t + 1)
                        act.wait_ge(ss_done, 4 * m + 2 * g + t + 1)
                        act.activation(junk2[:, t, :],
                                       y[:, t, ds(GRP * 2 * m + GRP * g, GRP)], ACT.Square,
                                       accum_out=ss[:, t, ds(2 * m + g, 1)]).then_inc(ss_done, 1)
            norm_rstd(1)
            transposed_hi(h2T, KT, 1)

            def gate_tile(n, ct, stage):
                e = 4 * n + ct
                if stage == 0:
                    wait_full(act, col_full, 16 + n, 4, ct, C_UP + CPG + 2 * CPG * n)
                    act.wait_ge(col_done, 64 + e - 1)
                    act.activation(uprt[0][ct % 2][:, :], A[ct][:, S:2 * S], ACT.Copy)\
                        .then_inc(part_done, 1)
                else:
                    act.wait_ge(gate_w0, e + 1)
                    act.activation(silu[ct][:, :], conv[0][ct % 2][:, :], ACT.Silu,
                                   bias=params[:, ds(2 * KT + 3 * 2 * FT + e, 1)])\
                        .then_inc(silu_done, 1)

            def val_tile(n, ct, stage):
                e = 4 * n + ct
                if stage == 0:
                    wait_full(act, bcol_full, 4 + n, 4, ct, C_UP + 2 * CPG + 2 * CPG * n)
                    act.wait_ge(bcol_done, 16 + e - 1)
                    act.activation(uprt[1][ct % 2][:, :], B[ct][:, S:2 * S], ACT.Copy)\
                        .then_inc(bpart_done, 1)
                else:
                    act.wait_ge(act_done, e + 1)
                    act.activation(ffT[:, ds(e, 1), 0:S], conv[1][ct % 2][:, :].unsqueeze(1),
                                   ACT.Copy).then_inc(ffT_hi, 1)

            def up_body(n, before):
                for j in range(CPG):
                    split(C_UP + AHEAD + j, n, 2 * CPG // SLOTS)
                    if before:
                        val_tile(n - 1, j // 2, j % 2)
                for j in range(CPG):
                    split(C_UP + AHEAD + CPG + j, n, 2 * CPG // SLOTS)
                    gate_tile(n, j // 2, j % 2)

            up_body(0, False)
            with act.Fori(1, NU) as n:
                up_body(n, True)
            for j in range(CPG):
                split(C_DOWN + AHEAD + j)
                val_tile(NU - 1, j // 2, j % 2)
            left = C_DOWN + 2 * FT - (C_DOWN + AHEAD + CPG)
            with act.Fori(0, left // SLOTS) as r:
                for j in range(SLOTS):
                    split(C_DOWN + AHEAD + CPG + j, r)
            for j in range(left - left % SLOTS, left):
                split(C_DOWN + AHEAD + CPG + j)

        @block.vector
        def _(dve):
            def split(c0, step=0, slots=1, width=2 * GRP):
                s = c0 % SLOTS
                dve.wait_ge(hi_done, c0 + 1 + SLOTS * slots * step)
                dve.tensor_tensor(lo[s][:, 0:width], raw[s][:, 0:width],
                                  hi[s][:, 0:width].bitcast(f32), ALU.subtract)\
                    .then_inc(lo_done, 1)

            def norm_rows(k, parts):
                dve.wait_ge(ss_done, parts)
                if k == 0:
                    dve.tensor_scalar(var2[:, :].unsqueeze(2), ss[:, :, 0:1], 1.0 / D, EPS,
                                      ALU.mult, ALU.add).then_inc(var_done, 1)
                else:
                    dve.tensor_reduce(var2[:, :], ss[:, :, :], AX.X, ALU.add)\
                        .then_inc(var_done, 1)
                    dve.wait_ge(var_done, 2)
                    dve.tensor_scalar(var2[:, :], var2[:, :], 1.0 / D, EPS, ALU.mult, ALU.add)\
                        .then_inc(var_done, 1)
                dve.wait_ge(var_done, 2 * k + 1)
                dve.reciprocal(inv2[:, :], var2[:, :]).then_inc(inv_done, 1)
                dve.wait_ge(rstd_done, k + 1)
                for t in range(TH):
                    dve.tensor_scalar(xn[:, t, :], y[:, t, :], rstd2[:, t:t + 1], None, ALU.mult)\
                        .then_inc(xn_done, 1)

            def transposed_lo(dst, gain, k):
                for kt in range(KT):
                    dve.wait_ge(xT_hi, k * KT + kt + 1)
                    dve.scalar_tensor_tensor(
                        dst[:, kt, S:2 * S], B[kt % 4][:, 0:S],
                        params[:, gain + kt:gain + kt + 1], dst[:, kt, 0:S].bitcast(f32),
                        ALU.mult, ALU.subtract).then_inc(xT_lo, 1)

            prime(dve, score_add, taken_done, sb_done, ds_done)
            norm_rows(0, TH)
            dve.wait_ge(params_done, 1)
            transposed_lo(hT, 0, 0)
            for c in range(C_ROWS):
                split(c, width=TAIL_CK * TAIL)
            for c in range(C_ROWS, C_ROWS + AHEAD):
                split(c)

            steps = [0]

            def then(instruction):
                steps[0] += 1
                instruction.then_inc(trig_step, 1)
                dve.wait_ge(trig_step, steps[0])

            dve.wait_ge(small_in, 16 * 8)
            dve.wait_ge(freq_set, HALF)
            then(dve.tensor_copy(pos_f[:, :], pos_i[:, :]))
            for q in range(2):
                for t in range(TH):
                    then(dve.tensor_scalar(ang[:, q, t, :], freq[:, :], pos_f[:, t:t + 1], None,
                                           ALU.mult))
            for q in range(2):
                then(dve.tensor_scalar(turn[:, q, :, :], ang[:, q, :, :], 1.0 / (2 * math.pi),
                                       0.25 * q, ALU.mult, ALU.add))
            then(dve.tensor_scalar(turn[:, :, :, :], turn[:, :, :, :], ROUND, None, ALU.add))
            then(dve.tensor_scalar(turn[:, :, :, :], turn[:, :, :, :], -ROUND, None, ALU.add))

            def flat(t):
                return t[:, :, :, :].rearrange("p a b c -> p (a b c)")

            for piece in (TWO_PI_A, TWO_PI_B, TWO_PI_C):
                then(dve.scalar_tensor_tensor(flat(ang), flat(turn), -piece, flat(ang),
                                              ALU.mult, ALU.add))
            then(dve.tensor_scalar(ang[:, 1, :, :], ang[:, 1, :, :], math.pi / 2, None, ALU.add))
            dve.tensor_scalar(flat(ang), flat(ang), SIN_MAX, -SIN_MAX, ALU.min, ALU.max)\
                .then_inc(angle_done, 1)
            dve.wait_ge(sin_done, 1)
            for r in range(4):
                for e in range(2):
                    dve.tensor_copy(cos_d[:, r, e * HALF:(e + 1) * HALF], trig[:, 1, r % 2, :])\
                        .then_inc(cos_set, 1)
                    dve.tensor_scalar(sin_d[:, r, e * HALF:(e + 1) * HALF], trig[:, 0, r % 2, :],
                                      (-1.0, 1.0)[e], None, ALU.mult).then_inc(cos_set, 1)
            for e in range(2):
                dve.tensor_copy(cos_i[:, :, e * IHALF:(e + 1) * IHALF], trig[:, 1, :, 0:HALF:2])\
                    .then_inc(cos_set, 1)
                dve.tensor_scalar(sin_i[:, :, e * IHALF:(e + 1) * IHALF], trig[:, 0, :, 0:HALF:2],
                                  (-1.0, 1.0)[e], None, ALU.mult).then_inc(cos_set, 1)
            dve.wait_ge(tok_done, TH)
            dve.tensor_scalar(wix[:, :, :], tail[:, :, ID:TAIL], IDX_SCALE, None, ALU.mult)\
                .then_inc(wix_done, 1)

            halves = ((0, 0, P), (1, P, KEYS))

            def rows_body(b, index):
                for g in range(2):
                    for j in range(CPG):
                        split(C_ROWS + AHEAD + g * CPG + j, b, 2 * CPG // SLOTS)
                        if index and g == 1 and j in (2, 6):
                            pair = j // 4
                            for h in range(2):
                                for t, k0, k1 in halves:
                                    k = 2 * pair + h
                                    dve.wait_ge(relu_done, 1 + 4 * (b - 1) + 2 * pair + t + 1)
                                    dve.wait_ge(score_add, 1 + 8 * (b - 1) + 2 * k + t)
                                    dve.scalar_tensor_tensor(
                                        scores[:, k0:k1], relu[pair][:, h, k0:k1],
                                        wix[:, t, ds(4 * (b - 1) + k, 1)], scores[:, k0:k1],
                                        ALU.mult, ALU.add).then_inc(score_add, 1)

            dve.wait_ge(wix_done, 1)
            dve.wait_ge(score_zero, 1)
            rows_body(0, False)
            with dve.Fori(1, NB) as b:
                rows_body(b, True)

            def column_sums(ready, done, bank, halves_, count, dst, tiles=range(4)):
                for ct in tiles:
                    dve.wait_ge(ready, count + ct + 1)
                    dve.tensor_tensor(dst(ct), bank[ct][:, 0:S].unsqueeze(1),
                                      halves_[ct][:, :].unsqueeze(1), ALU.add).then_inc(done, 1)

            ROUNDS = TOPK // 8 // 4

            def take(i, r):
                for t, k0, k1 in halves:
                    n = 2 * ROUNDS * i + 2 * r + t
                    wait_alone(dve, taken_done, 1 + n)
                    dve.max(best[:, t, :], scores[:, k0:k1]).then_inc(best_done, 1)
                    wait_alone(dve, best_done, n + 1)
                    dve.match_replace(scores[:, k0:k1], best[:, t, :], scores[:, k0:k1], TAKEN)\
                        .then_inc(taken_done, 1)

            def heads_body(qk, half):
                i = 2 * qk + half
                for j in range(CPG):
                    split(C_HEADS + AHEAD + j, i, CPG // SLOTS)
                    if j == 2:
                        dve.wait_ge(sq_done, i + 1)
                        dve.tensor_reduce(ms[:, :], sq[:, :, :, :].rearrange(
                            "p r h d -> p (r h) d"), AX.X, ALU.add).then_inc(ms_done, 1)
                        dve.wait_ge(ms_done, i + 1)
                        dve.tensor_scalar(ms[:, :], ms[:, :], 1.0 / HD, EPS, ALU.mult, ALU.add)\
                            .then_inc(msv_done, 1)
                        dve.wait_ge(msv_done, i + 1)
                        dve.reciprocal(inv[:, :], ms[:, :]).then_inc(hinv_done, 1)
                    if j == 4:
                        dve.wait_ge(hrstd_done, i + 1)
                        for r in range(4):
                            dve.tensor_tensor(
                                qn[:, r, :, :],
                                tok[:, 1 + r // 2, r % 2, ds(2 * HD * i, 2 * HD)]
                                .rearrange("p (h d) -> p h d", h=2),
                                rstd[:, 2 * r:2 * r + 2].unsqueeze(2).to_broadcast([P, 2, HD]),
                                ALU.mult).then_inc(qn_scaled, 1)
                    if j in (3, 5):
                        take(i, j // 4)
                column_sums(part_done, col_done, A, part, 4 * i,
                            lambda ct: qkT[:, ds(4 * half + ct, 1), ds(S * qk, S)])

            dve.wait_ge(score_masked, 1)
            with dve.Fori(0, 2) as qk:
                with dve.Fori(0, 2) as half:
                    heads_body(qk, half)

            dve.wait_ge(taken_done, 1 + 2 * TOPK // 8)
            dve.tensor_scalar(bias[:, :], scores[:, :], (NONCAUSAL + TAKEN) / 2, MASKED,
                              ALU.is_gt, ALU.mult).then_inc(bias_raw, 1)

            def gates_body(h):
                for j in range(CPG):
                    split(C_GATES + AHEAD + j, h, CPG // SLOTS)
                    if j == 1:
                        dve.wait_ge(logit_full, h + 1)
                        dve.wait_ge(bias_done, 1)
                        dve.tensor_tensor(logit[:, :], B[1][:, 0:KEYS], bias[:, :], ALU.add)\
                            .then_inc(logit_done, 1)
                        dve.wait_ge(logit_done, h + 1)
                        for t, k0, k1 in halves:
                            dve.tensor_reduce(top[:, t:t + 1], logit[:, k0:k1], AX.X, ALU.max)\
                                .then_inc(top_done, 1)
                        dve.wait_ge(top_done, 2 * h + 2)
                        dve.tensor_scalar(ntop[:, :], top[:, :], -SCALE, None, ALU.mult)\
                            .then_inc(ntop_done, 1)
                    if j == 2:
                        dve.wait_ge(ln_done, h + 1)
                        dve.scalar_tensor_tensor(stay[:, :], B[0][:, 0:KEYS], 0.0, soft[:, :],
                                                 ALU.max, ALU.add).then_inc(stay_raw, 1)
                    if j == 3:
                        dve.wait_ge(prob_raw, 2 * h + 2)
                        dve.reciprocal(pinv[:, :], psum_e[:, :]).then_inc(pinv_done, 1)
                column_sums(part_done, col_done, A, part, 16 + 4 * h,
                            lambda ct: gates[:, ds(4 * h + ct, 1), :])
                for ready, done, bank, at_head in ((sb_hi, sb_done, B[2], h),
                                                   (ds_hi, ds_done, B[3], NH + h)):
                    dve.wait_ge(ready, h + 1)
                    dve.tensor_tensor(oT[:, ds(at_head, 1), S:2 * S], bank[:, 0:S].unsqueeze(1),
                                      oT[:, ds(at_head, 1), 0:S].bitcast(f32), ALU.subtract)\
                        .then_inc(done, 1)

            with dve.Fori(0, NH) as h:
                gates_body(h)

            with dve.Fori(0, 4) as n:
                for j in range(CPG):
                    split(C_BRANCH + AHEAD + j, n, CPG // SLOTS)
                    if j >= 4:
                        column_sums(part_done, col_done, A, part, 48 + 4 * n,
                                    lambda ct: br[0][ct][:, :].unsqueeze(1), [j - 4])
                column_sums(bpart_done, bcol_done, B, partb, 4 * n,
                            lambda ct: br[1][ct][:, :].unsqueeze(1))
                for ct in range(4):
                    dve.wait_ge(mT_hi, 4 * n + ct + 1)
                    dve.tensor_tensor(mT[:, ds(4 * n + ct, 1), S:2 * S],
                                      br[0][ct][:, :].unsqueeze(1),
                                      mT[:, ds(4 * n + ct, 1), 0:S].bitcast(f32), ALU.subtract)\
                        .then_inc(mT_done, 1)

            dve.wait_ge(x_again, 16)
            with dve.Fori(0, 2) as m:
                for g in range(2):
                    for j in range(CPG):
                        split(C_OUT + AHEAD + g * CPG + j, m, 2 * CPG // SLOTS)
                    for t in range(TH):
                        wait_full(dve, row_full, 2 * m + g, TH, t,
                                  C_OUT + CPG * (g + 1) + 2 * CPG * m)
                        cols = y[:, t, ds(GRP * 2 * m + GRP * g, GRP)]
                        dve.tensor_tensor(cols, A[2 * g + t][:, :], cols, ALU.add)\
                            .then_inc(row_done, 1)
            norm_rows(1, TH + 4 * TH)
            transposed_lo(h2T, KT, 1)
            for b in range(2):
                for i in range(2):
                    dve.memset(u[b][i][:, 0:2], 0.0).then_inc(pad_zero, 1)
            dve.wait_ge(pad_zero, 4)

            def conv_tile(b, n, ct, stage, part_ready, full_at, col_sem, w2, w1, w0):
                e = 4 * n + ct
                s = ct % 2
                bank = (A, B)[b][ct]
                if stage == 0:
                    dve.wait_ge(part_ready, full_at + e + 1)
                    dve.tensor_tensor(u[b][s][:, 2:S + 2], bank[:, 0:S], uprt[b][s][:, :], ALU.add)\
                        .then_inc(col_sem, 1)
                    return
                for k, before, done in ((1, w2, w1), (0, w1, w0)):
                    column = 2 * KT + 2 * FT * k + b * FT
                    dve.wait_ge(before, e + 1)
                    dve.scalar_tensor_tensor(conv[b][s][:, :], u[b][s][:, k:k + S],
                                             params[:, ds(column + e, 1)], conv[b][s][:, :],
                                             ALU.mult, ALU.add).then_inc(done, 1)
                if b == 1:
                    dve.wait_ge(ffT_hi, e + 1)
                    dve.tensor_tensor(ffT[:, ds(e, 1), S:2 * S], conv[1][s][:, :].unsqueeze(1),
                                      ffT[:, ds(e, 1), 0:S].bitcast(f32), ALU.subtract)\
                        .then_inc(ffT_done, 1)

            def gate_tile(n, ct, stage):
                conv_tile(0, n, ct, stage, part_done, 64, col_done, gate_w2, gate_w1, gate_w0)

            def val_tile(n, ct, stage):
                conv_tile(1, n, ct, stage, bpart_done, 16, bcol_done, val_w2, val_w1, val_w0)

            def up_body(n, before):
                for j in range(CPG):
                    split(C_UP + AHEAD + j, n, 2 * CPG // SLOTS)
                    if before:
                        val_tile(n - 1, j // 2, j % 2)
                for j in range(CPG):
                    split(C_UP + AHEAD + CPG + j, n, 2 * CPG // SLOTS)
                    gate_tile(n, j // 2, j % 2)

            up_body(0, False)
            with dve.Fori(1, NU) as n:
                up_body(n, True)
            for j in range(CPG):
                split(C_DOWN + AHEAD + j)
                val_tile(NU - 1, j // 2, j % 2)

            def add_rows(m):
                for t in range(TH):
                    for g in range(2):
                        cols = y[:, t, m * BLOCK + g * GRP:m * BLOCK + (g + 1) * GRP]
                        wait_full(dve, down_full, m, 4, 2 * t + g, C_DOWN + FT * (m + 1))
                        dve.tensor_tensor(cols, A[2 * t + g][:, :], cols, ALU.add)\
                            .then_inc(out_ready, 1)

            first = C_DOWN + AHEAD + CPG
            with dve.Fori(0, (FT - CPG) // SLOTS) as r:
                for j in range(SLOTS):
                    split(first + j, r)
            add_rows(0)
            second = first + FT - CPG
            left = FT - AHEAD
            with dve.Fori(0, left // SLOTS) as r:
                for j in range(SLOTS):
                    split(second + j, r)
            for j in range(left - left % SLOTS, left):
                split(second + j)
            add_rows(1)

        @block.gpsimd
        def _(pool):
            pool.memset(rows_in[:, :, :], 0.0).then_inc(rows_zero, 1)
            pool.memset(ident[:, :], 0.0).then_inc(const_set, 1)
            pool.memset(neg_tri[:, :], -1.0).then_inc(const_set, 1)
            pool.memset(neg_one[:, :], -1.0).then_inc(const_set, 1)
            pool.wait_ge(const_set, 3)
            pool.affine_select(out=ident[:, :], in_=ident[:, :], compare_op=ALU.not_equal,
                               fill=1.0, base=0, pattern=[[-1, P]], channel_multiplier=1)\
                .then_inc(const_sel, 1)
            pool.affine_select(out=neg_tri[:, :], in_=neg_tri[:, :], compare_op=ALU.is_ge,
                               fill=0.0, base=0, pattern=[[-1, P]], channel_multiplier=1)\
                .then_inc(const_sel, 1)
            for i, f in enumerate(FREQS):
                pool.memset(freq[:, i:i + 1], f).then_inc(freq_set, 1)
            pool.memset(ikT[:, :, :], 0.0).then_inc(ikT_zero, 1)
            pool.memset(scores[:, :], 0.0).then_inc(score_zero, 1)

            def rotate(dst, src, rot, cos, sin, heads, half, sem_mid, count, sem_end):
                rows = cos.shape[1]
                c = cos[:, :, :].unsqueeze(2).to_broadcast([P, rows, heads, 2 * half])
                s = sin[:, :, :].unsqueeze(2).to_broadcast([P, rows, heads, 2 * half])
                pool.tensor_tensor(rot[:, 0], src(0, 2 * half), c, ALU.mult).then_inc(sem_mid, 1)
                pool.tensor_tensor(rot[:, 1, :, :, 0:half], src(half, 2 * half),
                                   s[:, :, :, 0:half], ALU.mult).then_inc(sem_mid, 1)
                pool.tensor_tensor(rot[:, 1, :, :, half:2 * half], src(0, half),
                                   s[:, :, :, half:2 * half], ALU.mult).then_inc(sem_mid, 1)
                pool.wait_ge(sem_mid, count)
                pool.tensor_tensor(dst, rot[:, 0], rot[:, 1], ALU.add).then_inc(sem_end, 1)

            pool.wait_ge(tok_done, TH)
            pool.wait_ge(cos_set, 20)
            for e in range(2):
                pool.tensor_copy(k_ix[:, :, e, 2 * IHALF:ID], tail[:, :, 2 * IHALF:ID])\
                    .then_inc(kix_a, 1)
            rotate(k_ix[:, :, :, 0:2 * IHALF],
                   lambda a, b: tail[:, :, a:b].unsqueeze(2).to_broadcast([P, TH, 2, b - a]),
                   rot_k, cos_i, sin_i, 2, IHALF, kix_b, 3, kix_done)

            with pool.Fori(1, NB) as b:
                q4 = tok[:, NB - 1, :, ds(4 * ID * (b - 1), 4 * ID)]\
                    .rearrange("p t (h d) -> p t h d", h=4)
                pool.wait_ge(tok_done, 2 + 4)
                pool.wait_ge(iqT_full, 1 + b - 1)
                for t in range(TH):
                    pool.tensor_copy(iq[:, t, :, 2 * IHALF:ID], q4[:, t, :, 2 * IHALF:ID])\
                        .then_inc(iq_done, 1)
                rotate(iq[:, :, :, 0:2 * IHALF], lambda c0, c1: q4[:, :, :, c0:c1], rot_i, cos_i,
                       sin_i, 4, IHALF, iq_rot, 3 * b, iq_done)

            pool.wait_ge(score_add, 1 + 2 * NI)
            diagonal = lambda t: t[:, :].rearrange("p (b c) -> p b c", b=3)[:, 0:3:2, :]
            pool.affine_select(out=diagonal(scores), in_=diagonal(scores), compare_op=ALU.is_ge,
                               fill=NONCAUSAL, base=0, pattern=[[0, 2], [-1, P]],
                               channel_multiplier=1).then_inc(score_masked, 1)

            with pool.Fori(0, 4) as i:
                pool.wait_ge(qn_scaled, 4 * i + 4)
                for r in range(4):
                    pool.tensor_tensor(
                        qn[:, r, :, :], qn[:, r, :, :],
                        qk_gain[:, r // 2:r // 2 + 1, :].to_broadcast([P, 2, HD]),
                        ALU.mult).then_inc(qn_gain, 1)
                pool.wait_ge(qn_gain, 4 * i + 4)
                rotate(qn[:, :, :, 0:2 * HALF], lambda c0, c1: qn[:, :, :, c0:c1], rot_d, cos_d,
                       sin_d, 2, HALF, qn_rot, 3 * i + 3, qn_done)

            pool.wait_ge(bias_raw, 1)
            pool.affine_select(out=diagonal(bias), in_=diagonal(bias), compare_op=ALU.is_ge,
                               fill=MASKED, base=0, pattern=[[0, 2], [-1, P]],
                               channel_multiplier=1).then_inc(bias_done, 1)

            pool.wait_ge(col_done, 16)
            pool.wait_ge(qkT_done, 8)
            with pool.Fori(0, NH) as h:
                pool.wait_ge(ds_full, 1 + h)
                pool.tensor_copy(sb_q[:, :].unsqueeze(1), qkT[:, ds(h, 1), 0:S])\
                    .then_inc(staged_qk, 1)
                pool.tensor_copy(sb_k[:, :].unsqueeze(1), qkT[:, ds(h, 1), S:2 * S])\
                    .then_inc(sb_k_done, 1)
                pool.tensor_copy(ds_qk[:, :].unsqueeze(1), qkT[:, ds(NH + h, 1), :])\
                    .then_inc(staged_qk, 1)
                wait_alone(pool, sb_k_done, h + 1)
                pool.tensor_scalar(sb_k[:, :], sb_k[:, :], SCALE, None, ALU.mult)\
                    .then_inc(staged_qk, 1)
                pool.tensor_copy(sb_v[:, :, :], tok[:, 0, :, ds(HD * h, HD)]).then_inc(staged_v, 1)
                pool.tensor_copy(ds_v[:, :, :], tok[:, 3, :, ds(HD * h, HD)]).then_inc(staged_v, 1)
                wait_alone(pool, stay_raw, h + 1)
                pool.affine_select(out=diagonal(stay), in_=diagonal(stay), compare_op=ALU.is_gt,
                                   fill=0.0, base=0, pattern=[[0, 2], [1, P]],
                                   channel_multiplier=-1).then_inc(stay_done, 1)
                wait_alone(pool, pinv_done, h + 1)
                for t, (k0, k1) in enumerate(((0, P), (P, KEYS))):
                    pool.tensor_scalar(prob[:, k0:k1], prob[:, k0:k1], pinv[:, t:t + 1], None,
                                       ALU.mult).then_inc(prob_done, 1)
                wait_alone(pool, stick_raw, h + 1)
                pool.affine_select(out=diagonal(stick), in_=diagonal(stick), compare_op=ALU.is_gt,
                                   fill=0.0, base=0, pattern=[[0, 2], [1, P]],
                                   channel_multiplier=-1).then_inc(stick_done, 1)

            with pool.Fori(0, 4) as n:
                for ct in range(4):
                    pool.wait_ge(sig_done, 8 * n + ct + 1)
                    pool.wait_ge(col_done, 48 + 4 * n + ct + 1)
                    pool.tensor_tensor(br[0][ct][:, :], br[0][ct][:, :], sig[0][ct][:, :],
                                       ALU.mult).then_inc(mix_a, 1)
                for ct in range(4):
                    pool.wait_ge(sig_done, 8 * n + 4 + ct + 1)
                    pool.wait_ge(bcol_done, 4 * n + ct + 1)
                    pool.tensor_tensor(br[1][ct][:, :], br[1][ct][:, :], sig[1][ct][:, :],
                                       ALU.mult).then_inc(mix_b, 1)
                    pool.wait_ge(mix_a, 4 * n + ct + 1)
                    pool.wait_ge(mix_b, 4 * n + ct + 1)
                    pool.tensor_tensor(br[0][ct][:, :], br[0][ct][:, :], br[1][ct][:, :],
                                       ALU.add).then_inc(mix_done, 1)
            pool.wait_ge(sig_done, 32)
            pool.dma_start(y[:, :, :], x[0, :, :].rearrange("(t p) d -> p t d", p=P))\
                .then_inc(x_again, 16)

            def column(first, e):
                return params[:, ds(first + e, 1)].to_broadcast([P, S])

            CONV_B = 2 * KT + 3 * 2 * FT

            def begin(b, n, ct, ready, at_, done):
                e = 4 * n + ct
                pool.wait_ge(ready, at_ + e + 1)
                pool.tensor_tensor(conv[b][ct % 2][:, :], u[b][ct % 2][:, 2:S + 2],
                                   column(2 * KT + 2 * FT * 2 + b * FT, e), ALU.mult)\
                    .then_inc(done, 1)

            def gate_tiles(n):
                for ct in range(4):
                    begin(0, n, ct, col_done, 64, gate_w2)

            def val_tiles(n):
                for ct in range(4):
                    e = 4 * n + ct
                    c = conv[1][ct % 2][:, :]
                    begin(1, n, ct, bcol_done, 16, val_w2)
                    pool.wait_ge(val_w0, e + 1)
                    pool.tensor_tensor(c, c, column(CONV_B + FT, e), ALU.add)\
                        .then_inc(val_bias, 1)
                    pool.wait_ge(val_bias, e + 1)
                    pool.wait_ge(silu_done, e + 1)
                    pool.tensor_tensor(c, c, silu[ct][:, :], ALU.mult).then_inc(act_done, 1)

            gate_tiles(0)
            with pool.Fori(1, NU) as n:
                val_tiles(n - 1)
                gate_tiles(n)
            val_tiles(NU - 1)

        @block.tensor
        def _(pe):
            def mm(o, l, r, start, stop):
                return pe.matmul(o, l, r, start=start, stop=stop, skip_group_check=True)

            def rows_chunk(c, slot, src, kts, width, outs, first, last, free, full):
                n = len(kts)
                wh = hi[slot][:, 0:n * width].rearrange("p (k c) -> p k c", k=n)
                wl = lo[slot][:, 0:n * width].rearrange("p (k c) -> p k c", k=n)
                pe.wait_ge(lo_done, c)
                for o, (bank, t, c0, c1) in enumerate(outs):
                    if first and free is not None:
                        free(o)
                    out_ = bank[:, 0:c1 - c0]
                    for j, kt in enumerate(kts):
                        xh = src[:, kt, t * P:(t + 1) * P]
                        xl = src[:, kt, S + t * P:S + (t + 1) * P]
                        mm(out_, xh, wh[:, j, c0:c1], first and j == 0, False)
                        mm(out_, xl, wh[:, j, c0:c1], False, False)
                        i = mm(out_, xh, wl[:, j, c0:c1], False, last and j == n - 1)
                    if last and o < len(outs) - 1:
                        i.then_inc(full, 1)
                i.then_inc(w_used, 1)

            def cols_chunk(c, slot, src, kts, bank, first, last, free, full):
                wh = hi[slot][:, :].rearrange("p (k c) -> p k c", k=CK)
                wl = lo[slot][:, :].rearrange("p (k c) -> p k c", k=CK)
                pe.wait_ge(lo_done, c)
                for ct in range(4):
                    if first and free is not None:
                        free(ct)
                    cs = slice(ct * P, (ct + 1) * P)
                    for j, kt in enumerate(kts):
                        if not (first and j == 0):
                            mm(bank[ct][:, 0:S], wl[:, j, cs], src[:, kt, 0:S], False, False)
                        i = mm(bank[ct][:, :], wh[:, j, cs], src[:, kt, :], first and j == 0,
                               last and j == CK - 1)
                        if first and j == 0:
                            mm(bank[ct][:, 0:S], wl[:, j, cs], src[:, kt, 0:S], False, False)
                    if last and ct < 3:
                        i.then_inc(full, 1)
                i.then_inc(w_used, 1)

            def transposes(k):
                pe.wait_ge(xn_done, TH * (k + 1))
                for kt in range(KT):
                    if kt >= 4:
                        pe.wait_ge(xT_lo, k * KT + kt - 3)
                    for t in range(TH):
                        i = pe.transpose(B[kt % 4][:, t * P:(t + 1) * P],
                                         xn[:, t, kt * P:(kt + 1) * P], ident[:, :])
                    i.then_inc(xT_full, 1)

            prime(pe, iqT_full, sb_full, ds_full)
            pe.wait_ge(const_sel, 2)
            pe.wait_ge(small_in, 16 * 8)
            for r, (n, at_) in enumerate(((KT, 0), (KT, KT), *((2 * FT, 2 * KT + 2 * FT * k)
                                                               for k in range(4)))):
                i = pe.transpose(B[3][:, at_:at_ + n], rows_in[0:n, r, :], ident[0:n, 0:n])
            i.then_inc(params_T, 1)
            pe.wait_ge(params_done, 1)
            transposes(0)
            for c in range(C_ROWS):
                pe.wait_ge(xT_lo, TAIL_CK * (c + 1))
                rows_chunk(c + 1, c, hT, range(TAIL_CK * c, TAIL_CK * (c + 1)), TAIL,
                           [(A[t], t, 0, TAIL) for t in range(TH)], c == 0,
                           c == C_ROWS - 1, None, tok_full)
            pe.wait_ge(kix_a, 2)
            pe.wait_ge(kix_done, 1)
            for t in range(TH):
                i = pe.transpose(B[0][:, t * P:(t + 1) * P],
                                 k_ix[:, t, :, :].rearrange("p e d -> p (e d)"), ident[:, :])
            i.then_inc(kixT_full, 1)

            def rows_body(b, index):
                for g in range(2):
                    def free(t):
                        if index:
                            pe.wait_ge(tok_done, 2 + 4 * (b - 1) + 2 * g + t + 1)
                        elif g == 0:
                            pe.wait_ge(tok_done, t + 1)
                    for j in range(CPG):
                        rows_chunk(C_ROWS + g * CPG + j + 1 + 2 * CPG * b, j % SLOTS, hT,
                                   range(CK * j, CK * (j + 1)), GRP,
                                   [(A[2 * g + t], t, 0, GRP) for t in range(TH)], j == 0,
                                   j == CPG - 1, free, tok_full)
                        if not index:
                            continue
                        if g == 0 and j == 3:
                            pe.wait_ge(iq_done, 3 * b)
                            pe.wait_ge(relu_done, 1 + 4 * (b - 1))
                            pe.wait_ge(ikT_done, 2)
                            for p2 in range(2):
                                for t in range(TH):
                                    i = pe.transpose(
                                        B[0][:, (2 * p2 + t) * P:(2 * p2 + t + 1) * P],
                                        iq[:, t, 2 * p2:2 * p2 + 2, :]
                                        .rearrange("p h d -> p (h d)"), ident[:, :])
                            i.then_inc(iqT_full, 1)
                        if (g, j) in ((0, 7), (1, 3)):
                            pair = g
                            at0, at1 = (B[1], B[2]) if pair == 0 else (B[3], B[0])
                            pe.wait_ge(iqT_done, b)
                            mm(at0[:, 0:2 * P], iqT[:, pair, 0:P], ikT[:, :, 0:P], True, True)\
                                .then_inc(sc_full, 1)
                            mm(at1[:, :], iqT[:, pair, P:S], ikT[:, :, :], True, True)\
                                .then_inc(sc_full, 1)

            rows_body(0, False)
            with pe.Fori(1, NB) as b:
                rows_body(b, True)

            pe.wait_ge(relu_done, 1 + NI)

            def heads_body(i):
                def free(ct):
                    pe.wait_ge(col_done, 4 * i - 4 + ct + 1)
                first_group = isinstance(i, int)

                def free0(ct):
                    pe.wait_ge(tok_done, 2 + 4 * NB)
                for j in range(CPG):
                    cols_chunk(C_HEADS + CPG * i + j + 1, j % SLOTS, hT,
                               range(CK * j, CK * (j + 1)), A, j == 0, j == CPG - 1,
                               free0 if first_group else free, col_full)
                    if j == 6:
                        pe.wait_ge(qn_done, i + 1)
                        pe.wait_ge(qkT_done, 2 * i)
                        for r in range(2):
                            for h in range(2):
                                for t in range(TH):
                                    k = pe.transpose(
                                        B[r][:, (2 * h + t) * P:(2 * h + t + 1) * P],
                                        qn[:, 2 * r + t, h, :], ident[:, :])
                            k.then_inc(qn_T, 1)

            heads_body(0)
            with pe.Fori(1, 4) as i:
                heads_body(i)

            with pe.Fori(0, NH) as h:
                def free_gate(ct):
                    pe.wait_ge(col_done, 16 + 4 * h - 4 + ct + 1)
                for j in range(CPG):
                    cols_chunk(C_GATES + CPG * h + j + 1, j % SLOTS, hT,
                               range(CK * j, CK * (j + 1)), A, j == 0, j == CPG - 1,
                               free_gate, col_full)
                    if j == 0:
                        pe.wait_ge(staged_qk, 3 * h + 3)
                        mm(B[0][:, 0:S], sb_k[:, 0:P], sb_q[:, :], True, True)
                        mm(B[0][:, S:KEYS], sb_k[:, P:S], sb_q[:, P:S], False, True)\
                            .then_inc(z_full, 1)
                        mm(B[1][:, 0:P], ds_qk[:, 0:P], ds_qk[:, S:S + P], True, True)
                        mm(B[1][:, P:KEYS], ds_qk[:, P:S], ds_qk[:, S:2 * S], True, True)\
                            .then_inc(logit_full, 1)
                    if j == 3:
                        pe.wait_ge(stay_done, h + 1)
                        mm(B[0][:, S:KEYS], neg_tri[:, :], stay[:, S:KEYS], False, True)
                        mm(B[0][:, P:S], neg_one[:, :], stay[:, S:KEYS], False, True)
                        mm(B[0][:, 0:S], neg_tri[:, :], stay[:, 0:S], False, True)\
                            .then_inc(suffix_full, 1)
                    if j == 4:
                        pe.wait_ge(prob_done, 2 * h + 2)
                        pe.wait_ge(ds_done, 1 + h)
                        for k in range(3):
                            i = pe.transpose(B[3][:, k * P:(k + 1) * P],
                                             prob[:, k * P:(k + 1) * P], ident[:, :])
                        i.then_inc(probT_full, 1)
                    if j in (6, 7):
                        if j == 6:
                            pe.wait_ge(stick_done, h + 1)
                            pe.wait_ge(sb_done, 1 + h)
                        else:
                            pe.wait_ge(probT_done, h + 1)
                        pe.wait_ge(staged_v, 2 * h + 2)
                        bank, v, w, full = ((B[2], sb_v, stick, sb_full),
                                            (B[3], ds_v, probT, ds_full))[j - 6]
                        mm(bank[:, 0:S], v[:, 0, :], w[:, 0:S], True, True)
                        mm(bank[:, P:S], v[:, 1, :], w[:, S:KEYS], False, True).then_inc(full, 1)

            def branch_body(n):
                first_group = isinstance(n, int)

                def free_sb(ct):
                    pe.wait_ge(col_done, 48 + 4 * n - 4 + ct + 1)

                def free_ds(ct):
                    if not first_group:
                        pe.wait_ge(bcol_done, 4 * n - 4 + ct + 1)
                for j in range(CPG):
                    if first_group and j < 4:
                        pe.wait_ge(sb_done, 1 + NH)
                    if first_group and j == 4:
                        pe.wait_ge(ds_done, 1 + NH)
                    cols_chunk(C_BRANCH + CPG * n + j + 1, j % SLOTS, oT,
                               range(CK * j, CK * (j + 1)), (A, B)[j // 4], j % 4 == 0,
                               j % 4 == 3, (free_sb, free_ds)[j // 4],
                               (col_full, bcol_full)[j // 4])

            branch_body(0)
            with pe.Fori(1, 4) as n:
                branch_body(n)

            for m in range(2):
                for g in range(2):
                    def free_row(t):
                        if m == 0:
                            pe.wait_ge(col_done, 64)
                        else:
                            pe.wait_ge(row_done, 4 * (m - 1) + 2 * g + t + 1)
                    for j in range(CPG):
                        if m == 0 and g == 0:
                            pe.wait_ge(mT_done, CK * (j + 1))
                        rows_chunk(C_OUT + CPG * (2 * m + g) + j + 1, j % SLOTS, mT,
                                   range(CK * j, CK * (j + 1)), GRP,
                                   [(A[2 * g + t], t, 0, GRP) for t in range(TH)], j == 0,
                                   j == CPG - 1, free_row, row_full)
            pe.wait_ge(bcol_done, 16)
            transposes(1)

            def up_body(n):
                first_pair = isinstance(n, int)

                def free_a(ct):
                    if first_pair:
                        pe.wait_ge(row_done, 8)
                    else:
                        pe.wait_ge(col_done, 64 + 4 * n - 4 + ct + 1)

                def free_b(ct):
                    if not first_pair:
                        pe.wait_ge(bcol_done, 16 + 4 * n - 4 + ct + 1)
                for b in range(2):
                    for j in range(CPG):
                        if first_pair and b == 0:
                            pe.wait_ge(xT_lo, KT + CK * (j + 1))
                        cols_chunk(C_UP + b * CPG + 2 * CPG * n + j + 1, j % SLOTS, h2T,
                                   range(CK * j, CK * (j + 1)), (A, B)[b], j == 0,
                                   j == CPG - 1, (free_a, free_b)[b],
                                   (col_full, bcol_full)[b])

            up_body(0)
            with pe.Fori(1, NU) as n:
                up_body(n)

            for m in range(2):
                def free_down(o):
                    if m == 0:
                        pe.wait_ge(col_done, 64 + 4 * NU)
                    else:
                        pe.wait_ge(out_ready, 4 * (m - 1) + o + 1)
                for k in range(FT):
                    if m == 0:
                        pe.wait_ge(ffT_done, k + 1)
                    rows_chunk(C_DOWN + FT * m + k + 1, k % SLOTS, ffT, [k], BLOCK,
                               [(A[2 * t + g], t, g * GRP, (g + 1) * GRP)
                                for t in range(TH) for g in range(2)], k == 0,
                               k == FT - 1, free_down, down_full)


_INS = ["x", "positions", "attn_norm_g", "w_in", "q_norm_g", "k_norm_g", "w_branch", "w_out",
        "ffn_norm_g", "w_up", "conv_w", "conv_b", "w_down"]


def kernel(**inputs):
    import concourse.bacc as bacc
    from concourse.bass_utils import run_bass_kernel_spmd

    nc = bacc.Bacc("TRN2", target_bir_lowering=False, num_devices=1)
    arrays, args = {}, []
    for name in _INS:
        a = np.ascontiguousarray(inputs[name])
        arrays[f"in_{name}"] = a
        args.append(nc.dram_tensor(f"in_{name}", a.shape, mybir.dt.from_np(a.dtype),
                                   kind="ExternalInput").ap())
    shape = inputs["x"].shape
    out = nc.dram_tensor("out", shape, mybir.dt.float32, kind="ExternalOutput").ap()
    hybrid_layer(nc, *args, out)
    r = run_bass_kernel_spmd(nc, [arrays], core_ids=[0])
    return r.results[0]["out"]
```

```python
import math

import numpy as np

import concourse.bass as bass
from concourse import mybir
from contextlib import ExitStack


def hybrid_layer(nc, x, positions, attn_norm_g, w_in, q_norm_g, k_norm_g, w_branch, w_out,
                 ffn_norm_g, w_up, conv_w, conv_b, w_down, out):
    f32 = mybir.dt.float32
    f32r = mybir.dt.float32r
    i32 = mybir.dt.int32
    ACT = mybir.ActivationFunctionType
    ALU = mybir.AluOpType
    AX = mybir.AxisListType
    ds = bass.ds

    P = 128
    S, D = x.shape[1], x.shape[2]
    TH = S // P
    KT = D // P
    HD = 128
    NH = 8
    NI, ID = 16, 64
    FF = w_down.shape[0]
    FT = FF // P
    TOPK = min(256, S // 4)
    EPS = 1e-6
    SCALE = HD ** -0.5
    IDX_SCALE = ID ** -0.5 * NI ** -0.5
    HALF = HD // 4 // 2
    IHALF = ID // 4 // 2
    GRP = 512
    CK = 2
    CPG = KT // CK
    BLOCK = 2 * GRP
    SLOTS = 4
    AHEAD = 3
    NB = 5
    TAIL_AT = 7 * BLOCK
    TAIL = ID + NI
    TAIL_CK = 4
    GATE_AT = TAIL_AT + TAIL
    KEYS = P + S

    C_ROWS = KT // TAIL_CK
    C_HEADS = C_ROWS + NB * 2 * CPG
    C_GATES = C_HEADS + 4 * CPG
    C_BRANCH = C_GATES + 8 * CPG
    C_OUT = C_BRANCH + 4 * CPG
    C_UP = C_OUT + 4 * CPG
    NU = FF // GRP
    C_DOWN = C_UP + NU * 2 * CPG
    for first in (C_ROWS, C_HEADS, C_GATES, C_BRANCH, C_OUT, C_UP, C_DOWN):
        assert first % SLOTS == 0

    NONCAUSAL, TAKEN, MASKED = -1e38, -3e38, -1e30
    ROUND = 1.5 * 2.0 ** 23
    TWO_PI_A, TWO_PI_B = 6.28125, 0.00193500518798828125
    TWO_PI_C = 2 * math.pi - TWO_PI_A - TWO_PI_B
    SIN_MAX = 3.1415925
    FREQS = [float(np.float32(500000.0) ** np.float32(-i / HALF)) for i in range(HALF)]

    ctx = ExitStack()
    with ctx:
        KB = 1024
        ARENA = 206 * KB
        arena = ctx.enter_context(nc.sbuf_tensor("arena", [P, ARENA // 4], f32))
        base = nc.lookup_mloc(arena).addr

        def at(name, shape, offset, dtype=f32):
            assert offset + 4 * int(np.prod(shape)) <= ARENA
            return nc.alloc_sbuf_tensor_at(name, [P, *shape], dtype, offset=base + offset)

        def sem(name):
            return ctx.enter_context(nc.semaphore(name))

        hT = at("hT", [KT, 2 * S], 0, f32r)
        mT = at("mT", [KT, 2 * S], 0, f32r)
        tok = at("tok", [NB, TH, BLOCK], 32 * KB)
        gates = at("gates", [2 * KT, S], 72 * KB)
        diag = at("diag", [TH, P], 72 * KB)
        y = at("y", [TH, D], 88 * KB)
        ffT = at("ffT", [FT, 2 * S], 0, f32r)
        qkT = at("qkT", [2 * NH, 2 * S], 104 * KB)
        oT = at("oT", [2 * NH, 2 * S], 104 * KB, f32r)
        h2T = at("h2T", [KT, 2 * S], 104 * KB, f32r)
        raw = [at(f"raw{i}", [2 * GRP], (136 + 4 * i) * KB) for i in range(SLOTS)]
        hi = [at(f"hi{i}", [2 * GRP], (152 + 4 * i) * KB, f32r) for i in range(SLOTS)]
        lo = [at(f"lo{i}", [2 * GRP], (168 + 4 * i) * KB, f32r) for i in range(SLOTS)]
        ident = at("ident", [P], 184 * KB)
        params = at("params", [2 * KT + 4 * 2 * FT], 184 * KB + 512)
        A0 = 186 * KB
        neg_tri = at("neg_tri", [P], A0)
        neg_one = at("neg_one", [P], A0 + 512)
        qk_gain = at("qk_gain", [2, HD], A0 + 1024)
        tail = at("tail", [TH, TAIL], A0 + 2048)
        wix = at("wix", [TH, NI], A0 + 2688)
        cos_d = at("cos_d", [4, 2 * HALF], A0 + 2816)
        sin_d = at("sin_d", [4, 2 * HALF], A0 + 3328)
        cos_i = at("cos_i", [TH, 2 * IHALF], A0 + 3840)
        sin_i = at("sin_i", [TH, 2 * IHALF], A0 + 3968)
        bias = at("bias", [KEYS], A0 + 4096)
        scores = at("scores", [KEYS], A0 + 5632)
        probT = at("probT", [KEYS], A0 + 5632)
        W0 = A0 + 7 * KB
        part = [at(f"part{i}", [S], W0 + i * KB) for i in range(4)]
        sb_q = at("sb_q", [S], W0 + 4 * KB)
        sb_k = at("sb_k", [S], W0 + 5 * KB)
        ds_qk = at("ds_qk", [2 * S], W0 + 6 * KB)
        sb_v = at("sb_v", [TH, HD], W0 + 8 * KB)
        ds_v = at("ds_v", [TH, HD], W0 + 9 * KB)
        partb = [at(f"partb{i}", [S], W0 + (4 + i) * KB) for i in range(4)]
        Z0 = A0 + 19 * KB
        ss = at("ss", [TH, 4], Z0)
        var2 = at("var2", [TH], Z0 + 32)
        inv2 = at("inv2", [TH], Z0 + 64)
        warm = at("warm", [1], Z0 + 288)
        rstd2 = at("rstd2", [TH], Z0 + 96)
        top = at("top", [2], Z0 + 128)
        ntop = at("ntop", [2], Z0 + 160)
        psum_e = at("psum_e", [2], Z0 + 192)
        pinv = at("pinv", [2], Z0 + 224)
        sb_scale = at("sb_scale", [1], Z0 + 256)
        ikT = at("ikT", [2, S], 104 * KB)
        iq = at("iq", [TH, 4, ID], 106 * KB)
        iqT = at("iqT", [2, S], 108 * KB)
        relu = [at(f"relu{i}", [2, KEYS], (110 + 3 * i) * KB) for i in range(2)]
        rot_i = at("rot_i", [2, TH, 4, 2 * IHALF], 116 * KB)
        rows_in = at("rows_in", [6, P], 118 * KB)
        freq = at("freq", [HALF], 121 * KB)
        ang = at("ang", [2, TH, HALF], 121 * KB + 256)
        turn = at("turn", [2, TH, HALF], 121 * KB + 512)
        trig = at("trig", [2, TH, HALF], 121 * KB + 768)
        pos_i = at("pos_i", [TH], 122 * KB, i32)
        pos_f = at("pos_f", [TH], 122 * KB + 64)
        k_ix = at("k_ix", [TH, 2, ID], 123 * KB)
        rot_k = at("rot_k", [2, TH, 2, 2 * IHALF], 124 * KB)
        junk = at("junk", [TH, D], 32 * KB)
        sq = at("sq", [4, 2, HD], 72 * KB)
        qn = at("qn", [4, 2, HD], 76 * KB)
        rot_d = at("rot_d", [2, 4, 2, 2 * HALF], 80 * KB)
        ms = at("ms", [8], 82 * KB)
        inv = at("inv", [8], 82 * KB + 64)
        rstd = at("rstd", [8], 82 * KB + 128)
        best = at("best", [2, 8], 82 * KB + 192)
        soft = at("soft", [KEYS], 64 * KB)
        stay = at("stay", [KEYS], 64 * KB + 1536)
        stick = at("stick", [KEYS], 64 * KB + 3072)
        logit = at("logit", [KEYS], 64 * KB + 4608)
        prob = at("prob", [KEYS], 64 * KB + 6144)
        sig = [[at(f"sig{b}{i}", [S], (32 + 4 * b + i) * KB) for i in range(4)] for b in range(2)]
        br = [[at(f"br{b}{i}", [S], (40 + 4 * b + i) * KB) for i in range(4)] for b in range(2)]
        junk2 = at("junk2", [TH, GRP], 40 * KB)
        U0 = A0
        u = [[at(f"u{b}{i}", [S + 2], U0 + (4 * b + i) * 1056) for i in range(4)]
             for b in range(2)]
        conv = [[at(f"conv{b}{i}", [S], U0 + 9 * KB + (2 * b + i) * KB) for i in range(2)]
                for b in range(2)]
        silu = [at(f"silu{i}", [S], U0 + (13 + i) * KB) for i in range(4)]

        banks = [ctx.enter_context(nc.psum_tensor(f"bank{i}", [P, 512], f32)) for i in range(8)]
        A, B = banks[:4], banks[4:]

        w_landed = [sem(f"w_landed{i}") for i in range(SLOTS)]
        hi_done = sem("hi_done")
        lo_done = sem("lo_done")
        w_used = sem("w_used")
        x_in = [sem(f"x_in{t}") for t in range(TH)]
        pos_in = sem("pos_in")
        small_in = sem("small_in")
        conv_in = sem("conv_in")
        x_again = sem("x_again")
        const_set = sem("const_set")
        const_sel = sem("const_sel")
        scale_set = sem("scale_set")
        rows_zero = sem("rows_zero")
        freq_set = sem("freq_set")
        warm_set = sem("warm_set")
        trig_step = sem("trig_step")
        angle_done = sem("angle_done")
        sin_done = sem("sin_done")
        cos_set = sem("cos_set")
        ss_done = sem("ss_done")
        var_done = sem("var_done")
        inv_done = sem("inv_done")
        rstd_done = sem("rstd_done")
        diag_done = sem("diag_done")
        params_T = sem("params_T")
        params_done = sem("params_done")
        xT_full = sem("xT_full")
        xT_hi = sem("xT_hi")
        xT_lo = sem("xT_lo")
        tok_full = sem("tok_full")
        tok_done = sem("tok_done")
        wix_done = sem("wix_done")
        kix_a = sem("kix_a")
        kix_b = sem("kix_b")
        kix_done = sem("kix_done")
        kixT_full = sem("kixT_full")
        ikT_zero = sem("ikT_zero")
        ikT_done = sem("ikT_done")
        score_zero = sem("score_zero")
        iq_rot = sem("iq_rot")
        iq_done = sem("iq_done")
        iqT_full = sem("iqT_full")
        iqT_done = sem("iqT_done")
        sc_full = sem("sc_full")
        relu_done = sem("relu_done")
        score_add = sem("score_add")
        score_masked = sem("score_masked")
        best_done = sem("best_done")
        taken_done = sem("taken_done")
        bias_raw = sem("bias_raw")
        bias_done = sem("bias_done")
        sq_done = sem("sq_done")
        ms_done = sem("ms_done")
        msv_done = sem("msv_done")
        hinv_done = sem("hinv_done")
        hrstd_done = sem("hrstd_done")
        qn_scaled = sem("qn_scaled")
        qn_gain = sem("qn_gain")
        qn_rot = sem("qn_rot")
        qn_done = sem("qn_done")
        qn_T = sem("qn_T")
        qkT_done = sem("qkT_done")
        col_full = sem("col_full")
        part_done = sem("part_done")
        col_done = sem("col_done")
        bcol_full = sem("bcol_full")
        bpart_done = sem("bpart_done")
        bcol_done = sem("bcol_done")
        staged_qk = sem("staged_qk")
        staged_v = sem("staged_v")
        z_full = sem("z_full")
        logit_full = sem("logit_full")
        abs_done = sem("abs_done")
        exp_done = sem("exp_done")
        ln_done = sem("ln_done")
        stay_raw = sem("stay_raw")
        stay_done = sem("stay_done")
        suffix_full = sem("suffix_full")
        stick_raw = sem("stick_raw")
        stick_done = sem("stick_done")
        logit_done = sem("logit_done")
        top_done = sem("top_done")
        ntop_done = sem("ntop_done")
        prob_raw = sem("prob_raw")
        pinv_done = sem("pinv_done")
        prob_done = sem("prob_done")
        probT_full = sem("probT_full")
        probT_done = sem("probT_done")
        sb_full = sem("sb_full")
        ds_full = sem("ds_full")
        sb_hi = sem("sb_hi")
        ds_hi = sem("ds_hi")
        sb_done = sem("sb_done")
        ds_done = sem("ds_done")
        sig_done = sem("sig_done")
        mix_a = sem("mix_a")
        mix_b = sem("mix_b")
        mix_done = sem("mix_done")
        mT_hi = sem("mT_hi")
        mT_done = sem("mT_done")
        row_full = sem("row_full")
        row_done = sem("row_done")
        pad_zero = sem("pad_zero")
        gate_w2 = sem("gate_w2")
        gate_w1 = sem("gate_w1")
        gate_w0 = sem("gate_w0")
        silu_done = sem("silu_done")
        val_w2 = sem("val_w2")
        val_w1 = sem("val_w1")
        val_w0 = sem("val_w0")
        val_bias = sem("val_bias")
        act_done = sem("act_done")
        ffT_hi = sem("ffT_hi")
        ffT_done = sem("ffT_done")
        down_full = sem("down_full")
        out_ready = sem("out_ready")
        stored = sem("stored")
        passed = sem("passed")

        block = ctx.enter_context(nc.Block())

        def wait_alone(engine, semaphore, value):
            engine.wait_ge(semaphore, value)
            engine.sem_inc(passed, 1)

        def prime(engine, *semaphores):
            for s in semaphores:
                engine.sem_inc(s, 1)

        def wait_full(engine, full, group, count, bank, end):
            if bank < count - 1:
                engine.wait_ge(full, (count - 1) * group + bank + 1)
            else:
                engine.wait_ge(w_used, end)

        @block.sync
        def _(sp):
            def load(slot, dst, src):
                sp.dma_start(dst, src).then_inc(w_landed[slot], 16)

            def load_group(c0, w, step, col, n=CPG, width=GRP, per=CK):
                for j in range(n):
                    wait_alone(sp, lo_done, c0 + j - AHEAD + step)
                    rows = w[j * per * P:(j + 1) * per * P, ds(col, width)]
                    load(j % SLOTS, raw[j % SLOTS][:, :].rearrange("p (k c) -> p k c", k=per),
                         rows.rearrange("(k p) c -> p k c", p=P))

            for t in range(TH):
                for cols in (slice(0, BLOCK), slice(BLOCK, D)):
                    sp.dma_start(y[:, t, cols], x[0, t * P:(t + 1) * P, cols])\
                        .then_inc(x_in[t], 16)
            for c in range(C_ROWS):
                rows = w_in[c * TAIL_CK * P:(c + 1) * TAIL_CK * P, TAIL_AT:TAIL_AT + TAIL]
                load(c, raw[c][:, 0:TAIL_CK * TAIL].rearrange("p (k c) -> p k c", k=TAIL_CK),
                     rows.rearrange("(k p) c -> p k c", p=P))
            with sp.Fori(0, NB) as b:
                for g in range(2):
                    load_group(C_ROWS + g * CPG, w_in, 2 * CPG * b,
                               2 * BLOCK + (NB - 1) * BLOCK + g * GRP - BLOCK * b)
            with sp.Fori(0, 4) as g:
                load_group(C_HEADS, w_in, CPG * g, GRP * g)
            with sp.Fori(0, 8) as g:
                load_group(C_GATES, w_in, CPG * g, GATE_AT + GRP * g)
            with sp.Fori(0, 4) as g:
                load_group(C_BRANCH, w_branch, CPG * g, GRP * g)
            with sp.Fori(0, 4) as g:
                load_group(C_OUT, w_out, CPG * g, GRP * g)
            with sp.Fori(0, NU) as n:
                for b in range(2):
                    load_group(C_UP + b * CPG, w_up, 2 * CPG * n, b * FF + GRP * n)
            with sp.Fori(0, 2) as m:
                load_group(C_DOWN, w_down, FT * m, BLOCK * m, n=FT, width=BLOCK, per=1)
            for m in range(2):
                for t in range(TH):
                    for h in range(2):
                        cols = slice(m * BLOCK + h * GRP, m * BLOCK + (h + 1) * GRP)
                        sp.wait_ge(out_ready, 4 * m + 2 * t + h + 1)
                        sp.dma_start(out[0, t * P:(t + 1) * P, cols], y[:, t, cols])\
                            .then_inc(stored, 16)
            sp.wait_ge(stored, 16 * 4 * TH)

        @block.scalar
        def _(act):
            def split(c0, step=0, slots=1, width=2 * GRP):
                s = c0 % SLOTS
                act.wait_ge(w_landed[s], 16 * (c0 // SLOTS + 1) + 16 * slots * step)
                if c0 >= SLOTS:
                    act.wait_ge(w_used, c0 - SLOTS + 1 + SLOTS * slots * step)
                act.activation(hi[s][:, 0:width], raw[s][:, 0:width], ACT.Copy)\
                    .then_inc(hi_done, 1)

            def norm_rstd(k):
                act.wait_ge(inv_done, k + 1)
                act.activation(rstd2[:, :], inv2[:, :], ACT.Sqrt).then_inc(rstd_done, 1)

            def transposed_hi(dst, gain, k, kts):
                for kt in kts:
                    act.wait_ge(xT_full, k * KT + kt + 1)
                    act.activation(dst[:, kt, 0:S], B[kt % 4][:, 0:S], ACT.Copy,
                                   scale=params[:, gain + kt:gain + kt + 1]).then_inc(xT_hi, 1)

            prime(act, relu_done)
            for t in range(TH):
                act.dma_start(pos_i[:, t:t + 1], positions[0, t * P:(t + 1) * P].unsqueeze(1))\
                    .then_inc(pos_in, 16)
            act.wait_ge(rows_zero, 1)
            act.dma_start(rows_in[0:KT, 0, :], attn_norm_g.rearrange("(t p) -> t p", p=P))\
                .then_inc(small_in, 16)
            act.dma_start(rows_in[0:KT, 1, :], ffn_norm_g.rearrange("(t p) -> t p", p=P))\
                .then_inc(small_in, 16)
            act.wait_ge(warm_set, 1)
            act.activation(warm[:, :], warm[:, :], ACT.Sqrt).then_inc(passed, 1)
            for t in range(TH):
                for half in range(2):
                    act.wait_ge(x_in[t], 16 * 2)
                    act.activation(junk[:, t, half * BLOCK:(half + 1) * BLOCK],
                                   y[:, t, half * BLOCK:(half + 1) * BLOCK], ACT.Square,
                                   accum_out=ss[:, t, half:half + 1]).then_inc(ss_done, 1)
            act.wait_ge(params_T, 1)
            act.activation(params[:, :], B[3][:, 0:2 * KT + 8 * FT], ACT.Copy)\
                .then_inc(params_done, 1)
            norm_rstd(0)
            act.wait_ge(params_done, 1)
            split(0, width=TAIL_CK * TAIL)
            for c in range(C_ROWS):
                if c + 1 < C_ROWS:
                    split(c + 1, width=TAIL_CK * TAIL)
                transposed_hi(hT, 0, 0, range(TAIL_CK * c, TAIL_CK * (c + 1)))
            for c in range(C_ROWS, C_ROWS + AHEAD):
                split(c)
            for t in range(TH):
                wait_full(act, tok_full, 0, TH, t, C_ROWS)
                act.activation(tail[:, t, :], A[2 + t][:, 0:TAIL], ACT.Copy).then_inc(tok_done, 1)
            act.wait_ge(angle_done, 1)
            act.activation(trig[:, :, :, :], ang[:, :, :, :], ACT.Sin).then_inc(sin_done, 1)

            def rows_body(b, index):
                for g in range(2):
                    for j in range(CPG):
                        split(C_ROWS + AHEAD + g * CPG + j, b, 2 * CPG // SLOTS)
                        if not index:
                            if (g, j) == (1, 4):
                                act.wait_ge(kixT_full, 1)
                                act.wait_ge(ikT_zero, 1)
                                for h in range(2):
                                    rows = slice(h * ID, (h + 1) * ID)
                                    act.activation(ikT[rows, h, :], B[0][rows, 0:S], ACT.Copy)\
                                        .then_inc(ikT_done, 1)
                            continue
                        if g == 0 and j == 5:
                            act.wait_ge(iqT_full, 1 + b)
                            act.activation(iqT[:, :, :], B[0][:, :], ACT.Copy)\
                                .then_inc(iqT_done, 1)
                        if g == 1 and j in (1, 5):
                            pair = j // 4
                            at0, at1 = (B[1], B[2]) if pair == 0 else (B[3], B[0])
                            act.wait_ge(sc_full, 4 * (b - 1) + 2 * pair + 1)
                            act.activation(relu[pair][:, :, 0:P],
                                           at0[:, 0:2 * P].rearrange("p (h k) -> p h k", h=2),
                                           ACT.Relu).then_inc(relu_done, 1)
                            act.wait_ge(sc_full, 4 * (b - 1) + 2 * pair + 2)
                            act.activation(relu[pair][:, :, P:KEYS],
                                           at1[:, :].rearrange("p (h k) -> p h k", h=2),
                                           ACT.Relu).then_inc(relu_done, 1)
                    for t in range(TH):
                        wait_full(act, tok_full, 1 + 2 * b + g, TH, t,
                                  C_ROWS + CPG * (g + 1) + 2 * CPG * b)
                        act.activation(tok[:, ds(NB - 1 - b, 1), t, g * GRP:(g + 1) * GRP],
                                       A[2 * g + t][:, :].unsqueeze(1), ACT.Copy)\
                            .then_inc(tok_done, 1)

            rows_body(0, False)
            with act.Fori(1, NB) as b:
                rows_body(b, True)

            def column_halves(full, done, bank, dst, group, end, tiles=range(4)):
                for ct in tiles:
                    wait_full(act, full, group, 4, ct, end)
                    act.activation(dst[ct][:, :], bank[ct][:, S:2 * S], ACT.Copy).then_inc(done, 1)

            def heads_body(qk, half):
                i = 2 * qk + half
                for j in range(CPG):
                    split(C_HEADS + AHEAD + j, i, CPG // SLOTS)
                    if j == 1:
                        act.activation(sq[:, :, :, :].rearrange("p r h d -> p r (h d)"),
                                       tok[:, 1:3, :, ds(2 * HD * i, 2 * HD)]
                                       .rearrange("p b t c -> p (b t) c"),
                                       ACT.Square).then_inc(sq_done, 1)
                    if j == 3:
                        act.wait_ge(hinv_done, i + 1)
                        act.activation(rstd[:, :], inv[:, :], ACT.Sqrt).then_inc(hrstd_done, 1)
                column_halves(col_full, part_done, A, part, i, C_HEADS + CPG + CPG * i)
                for r in range(2):
                    act.wait_ge(qn_T, 2 * i + r + 1)
                    act.activation(qkT[:, ds(NH + 2 * i, 2), r * S:(r + 1) * S],
                                   B[r][:, :].rearrange("p (h s) -> p h s", h=2),
                                   ACT.Copy).then_inc(qkT_done, 1)

            act.wait_ge(tok_done, 2 + 4 * NB)
            with act.Fori(0, 2) as qk:
                with act.Fori(0, 2) as half:
                    heads_body(qk, half)

            def gates_body(h):
                for j in range(CPG):
                    split(C_GATES + AHEAD + j, h, CPG // SLOTS)
                    if j == 1:
                        act.wait_ge(z_full, h + 1)
                        act.activation(soft[:, :], B[0][:, 0:KEYS], ACT.Abs).then_inc(abs_done, 1)
                        act.wait_ge(abs_done, h + 1)
                        act.activation(soft[:, :], soft[:, :], ACT.Exp, scale=-1.0)\
                            .then_inc(exp_done, 1)
                        act.wait_ge(exp_done, h + 1)
                        act.activation(soft[:, :], soft[:, :], ACT.Ln, bias=1.0)\
                            .then_inc(ln_done, 1)
                    if j == 2:
                        act.wait_ge(ntop_done, h + 1)
                        for t, (k0, k1) in enumerate(((0, P), (P, KEYS))):
                            act.activation(prob[:, k0:k1], logit[:, k0:k1], ACT.Exp,
                                           bias=ntop[:, t:t + 1], scale=SCALE,
                                           accum_out=psum_e[:, t:t + 1]).then_inc(prob_raw, 1)
                    if j == 5:
                        act.wait_ge(suffix_full, h + 1)
                        act.activation(stick[:, :], B[0][:, 0:KEYS], ACT.Exp)\
                            .then_inc(stick_raw, 1)
                    if j == 6:
                        act.wait_ge(probT_full, h + 1)
                        act.activation(probT[:, :], B[3][:, 0:KEYS], ACT.Copy)\
                            .then_inc(probT_done, 1)
                column_halves(col_full, part_done, A, part, 4 + h, C_GATES + CPG + CPG * h)
                for full, done, bank, at_head in ((sb_full, sb_hi, B[2], h),
                                                  (ds_full, ds_hi, B[3], NH + h)):
                    act.wait_ge(full, 1 + h + 1)
                    act.activation(oT[:, ds(at_head, 1), 0:S], bank[:, 0:S].unsqueeze(1),
                                   ACT.Copy).then_inc(done, 1)

            with act.Fori(0, NH) as h:
                gates_body(h)

            def merged_hi(n, ct):
                act.wait_ge(mix_done, 4 * n + ct + 1)
                act.activation(mT[:, ds(4 * n + ct, 1), 0:S], br[0][ct][:, :].unsqueeze(1),
                               ACT.Copy).then_inc(mT_hi, 1)

            def branch_body(n, before):
                for j in range(CPG):
                    split(C_BRANCH + AHEAD + j, n, CPG // SLOTS)
                    if before and j < 4:
                        merged_hi(n - 1, j)
                    if j in (4, 5):
                        for ct in (2 * j - 8, 2 * j - 7):
                            column_halves(col_full, part_done, A, part, 12 + n,
                                          C_BRANCH + CPG // 2 + CPG * n, [ct])
                    if j in (5, 6):
                        for ct in (2 * j - 10, 2 * j - 9):
                            act.activation(sig[0][ct][:, :].unsqueeze(1),
                                           gates[:, ds(4 * n + ct, 1), :],
                                           ACT.Sigmoid).then_inc(sig_done, 1)
                    if j in (6, 7):
                        for ct in (2 * j - 12, 2 * j - 11):
                            act.activation(sig[1][ct][:, :].unsqueeze(1),
                                           gates[:, ds(KT + 4 * n + ct, 1), :],
                                           ACT.Sigmoid).then_inc(sig_done, 1)
                column_halves(bcol_full, bpart_done, B, partb, n, C_BRANCH + CPG + CPG * n)

            branch_body(0, False)
            with act.Fori(1, 4) as n:
                branch_body(n, True)

            def out_body(m, first):
                for g in range(2):
                    for j in range(CPG):
                        split(C_OUT + AHEAD + g * CPG + j, m, 2 * CPG // SLOTS)
                        if first and g == 0 and 1 <= j < 5:
                            merged_hi(3, j - 1)
                        if not first and g == 0 and j == 0:
                            act.activation(warm[:, :], warm[:, :], ACT.Sqrt).then_inc(passed, 1)
                    for t in range(TH):
                        act.wait_ge(row_done, 4 * m + 2 * g + t + 1)
                        act.wait_ge(ss_done, 2 * TH + 4 * m + 2 * g + t - 1)
                        act.activation(junk2[:, t, :],
                                       y[:, t, ds(GRP * 2 * m + GRP * g, GRP)], ACT.Square,
                                       accum_out=ss[:, t, ds(2 * m + g, 1)]).then_inc(ss_done, 1)

            out_body(0, True)
            out_body(1, False)
            norm_rstd(1)
            transposed_hi(h2T, KT, 1, range(4))

            def gate_half(n, ct):
                wait_full(act, col_full, 16 + n, 4, ct, C_UP + CPG + 2 * CPG * n)
                act.activation(u[0][ct][:, 2:S + 2], A[ct][:, S:2 * S], ACT.Copy)\
                    .then_inc(part_done, 1)

            def val_half(n, ct):
                wait_full(act, bcol_full, 4 + n, 4, ct, C_UP + 2 * CPG + 2 * CPG * n)
                act.activation(u[1][ct][:, 2:S + 2], B[ct][:, S:2 * S], ACT.Copy)\
                    .then_inc(bpart_done, 1)

            def gate_silu(n, ct):
                e = 4 * n + ct
                act.wait_ge(gate_w0, e + 1)
                act.activation(silu[ct][:, :], conv[0][ct % 2][:, :], ACT.Silu,
                               bias=params[:, ds(2 * KT + 3 * 2 * FT + e, 1)])\
                    .then_inc(silu_done, 1)

            def ff_hi(n, ct):
                e = 4 * n + ct
                act.wait_ge(act_done, e + 1)
                act.activation(ffT[:, ds(e, 1), 0:S], conv[1][ct % 2][:, :].unsqueeze(1),
                               ACT.Copy).then_inc(ffT_hi, 1)

            def up_step(n, j):
                if j < 4:
                    val_half(n - 1, j)
                if j in (3, 5, 7, 9):
                    ff_hi(n - 1, (j - 3) // 2)

            def gate_step(n, j):
                if j < 4:
                    gate_half(n, j)
                if j in (3, 5, 7):
                    gate_silu(n, (j - 3) // 2)
                if j == 7:
                    gate_silu(n, 3)

            def up_body(n, before):
                for j in range(2 * CPG):
                    split(C_UP + AHEAD + j, n, 2 * CPG // SLOTS)
                    if before:
                        up_step(n, j)
                    elif j < CPG - 2:
                        transposed_hi(h2T, KT, 1, range(4 + CK * j, 4 + CK * (j + 1)))
                    if j >= CPG:
                        gate_step(n, j - CPG)

            up_body(0, False)
            with act.Fori(1, NU) as n:
                up_body(n, True)
            LAST = 3 * SLOTS
            for j in range(LAST):
                split(C_DOWN + AHEAD + j)
                up_step(NU, j)
            left = 2 * FT - AHEAD - LAST
            with act.Fori(0, left // SLOTS) as r:
                for j in range(SLOTS):
                    split(C_DOWN + AHEAD + LAST + j, r)
            for j in range(left - left % SLOTS, left):
                split(C_DOWN + AHEAD + LAST + j)

        @block.vector
        def _(dve):
            def split(c0, step=0, slots=1, width=2 * GRP):
                s = c0 % SLOTS
                dve.wait_ge(hi_done, c0 + 1 + SLOTS * slots * step)
                dve.tensor_tensor(lo[s][:, 0:width], raw[s][:, 0:width],
                                  hi[s][:, 0:width].bitcast(f32), ALU.subtract)\
                    .then_inc(lo_done, 1)

            def norm_rows(k, parts):
                dve.wait_ge(ss_done, 2 * TH + 4 * TH * k)
                dve.tensor_reduce(var2[:, :], ss[:, :, 0:parts], AX.X, ALU.add)\
                    .then_inc(var_done, 1)
                dve.wait_ge(var_done, 2 * k + 1)
                dve.tensor_scalar(var2[:, :], var2[:, :], 1.0 / D, EPS, ALU.mult, ALU.add)\
                    .then_inc(var_done, 1)
                dve.wait_ge(var_done, 2 * k + 2)
                dve.reciprocal(inv2[:, :], var2[:, :]).then_inc(inv_done, 1)
                dve.wait_ge(rstd_done, k + 1)
                for t in range(TH):
                    dve.tensor_scalar(diag[:, t, :], ident[:, :], rstd2[:, t:t + 1], None,
                                      ALU.mult).then_inc(diag_done, 1)

            def transposed_lo(dst, gain, k, kts):
                for kt in kts:
                    dve.wait_ge(xT_hi, k * KT + kt + 1)
                    dve.scalar_tensor_tensor(
                        dst[:, kt, S:2 * S], B[kt % 4][:, 0:S],
                        params[:, gain + kt:gain + kt + 1], dst[:, kt, 0:S].bitcast(f32),
                        ALU.mult, ALU.subtract).then_inc(xT_lo, 1)

            prime(dve, score_add, taken_done, sb_done, ds_done)
            steps = [0]

            def then(instruction):
                steps[0] += 1
                instruction.then_inc(trig_step, 1)
                dve.wait_ge(trig_step, steps[0])

            dve.wait_ge(pos_in, 16 * TH)
            dve.wait_ge(freq_set, HALF)
            then(dve.tensor_copy(pos_f[:, :], pos_i[:, :]))
            for q in range(2):
                for t in range(TH):
                    then(dve.tensor_scalar(ang[:, q, t, :], freq[:, :], pos_f[:, t:t + 1], None,
                                           ALU.mult))
            for q in range(2):
                then(dve.tensor_scalar(turn[:, q, :, :], ang[:, q, :, :], 1.0 / (2 * math.pi),
                                       0.25 * q, ALU.mult, ALU.add))
            then(dve.tensor_scalar(turn[:, :, :, :], turn[:, :, :, :], ROUND, None, ALU.add))
            then(dve.tensor_scalar(turn[:, :, :, :], turn[:, :, :, :], -ROUND, None, ALU.add))

            def flat(t):
                return t[:, :, :, :].rearrange("p a b c -> p (a b c)")

            for piece in (TWO_PI_A, TWO_PI_B, TWO_PI_C):
                then(dve.scalar_tensor_tensor(flat(ang), flat(turn), -piece, flat(ang),
                                              ALU.mult, ALU.add))
            then(dve.tensor_scalar(ang[:, 1, :, :], ang[:, 1, :, :], math.pi / 2, None, ALU.add))
            dve.tensor_scalar(flat(ang), flat(ang), SIN_MAX, -SIN_MAX, ALU.min, ALU.max)\
                .then_inc(angle_done, 1)
            dve.wait_ge(const_sel, 2)
            norm_rows(0, 2)
            dve.wait_ge(params_done, 1)
            split(0, width=TAIL_CK * TAIL)
            for c in range(C_ROWS):
                if c + 1 < C_ROWS:
                    split(c + 1, width=TAIL_CK * TAIL)
                transposed_lo(hT, 0, 0, range(TAIL_CK * c, TAIL_CK * (c + 1)))
            for c in range(C_ROWS, C_ROWS + AHEAD):
                split(c)

            def tables():
                dve.wait_ge(sin_done, 1)
                for r in range(4):
                    for e in range(2):
                        dve.tensor_copy(cos_d[:, r, e * HALF:(e + 1) * HALF], trig[:, 1, r % 2, :])\
                            .then_inc(cos_set, 1)
                        dve.tensor_scalar(sin_d[:, r, e * HALF:(e + 1) * HALF], trig[:, 0, r % 2, :],
                                          (-1.0, 1.0)[e], None, ALU.mult).then_inc(cos_set, 1)
                for e in range(2):
                    dve.tensor_copy(cos_i[:, :, e * IHALF:(e + 1) * IHALF], trig[:, 1, :, 0:HALF:2])\
                        .then_inc(cos_set, 1)
                    dve.tensor_scalar(sin_i[:, :, e * IHALF:(e + 1) * IHALF], trig[:, 0, :, 0:HALF:2],
                                      (-1.0, 1.0)[e], None, ALU.mult).then_inc(cos_set, 1)
                dve.wait_ge(tok_done, TH)
                dve.tensor_scalar(wix[:, :, :], tail[:, :, ID:TAIL], IDX_SCALE, None, ALU.mult)\
                    .then_inc(wix_done, 1)

            halves = ((0, 0, P), (1, P, KEYS))

            def rows_body(b, index):
                for g in range(2):
                    for j in range(CPG):
                        split(C_ROWS + AHEAD + g * CPG + j, b, 2 * CPG // SLOTS)
                        if not index and (g, j) == (0, 0):
                            tables()
                        if index and g == 1 and j in (2, 6):
                            pair = j // 4
                            for h in range(2):
                                for t, k0, k1 in halves:
                                    k = 2 * pair + h
                                    dve.wait_ge(relu_done, 1 + 4 * (b - 1) + 2 * pair + t + 1)
                                    dve.wait_ge(score_add, 1 + 8 * (b - 1) + 2 * k + t)
                                    dve.scalar_tensor_tensor(
                                        scores[:, k0:k1], relu[pair][:, h, k0:k1],
                                        wix[:, t, ds(4 * (b - 1) + k, 1)], scores[:, k0:k1],
                                        ALU.mult, ALU.add).then_inc(score_add, 1)

            rows_body(0, False)
            dve.wait_ge(wix_done, 1)
            dve.wait_ge(score_zero, 1)
            with dve.Fori(1, NB) as b:
                rows_body(b, True)

            def column_sums(ready, done, bank, halves_, count, dst, tiles=range(4)):
                for ct in tiles:
                    dve.wait_ge(ready, count + ct + 1)
                    dve.tensor_tensor(dst(ct), bank[ct][:, 0:S].unsqueeze(1),
                                      halves_[ct][:, :].unsqueeze(1), ALU.add).then_inc(done, 1)

            ROUNDS = TOPK // 8 // 4

            def take(i, r):
                for t, k0, k1 in halves:
                    n = 2 * ROUNDS * i + 2 * r + t
                    wait_alone(dve, taken_done, 1 + n)
                    dve.max(best[:, t, :], scores[:, k0:k1]).then_inc(best_done, 1)
                    wait_alone(dve, best_done, n + 1)
                    dve.match_replace(scores[:, k0:k1], best[:, t, :], scores[:, k0:k1], TAKEN)\
                        .then_inc(taken_done, 1)

            def heads_body(qk, half):
                i = 2 * qk + half
                for j in range(CPG):
                    split(C_HEADS + AHEAD + j, i, CPG // SLOTS)
                    if j == 2:
                        dve.wait_ge(sq_done, i + 1)
                        dve.tensor_reduce(ms[:, :], sq[:, :, :, :].rearrange(
                            "p r h d -> p (r h) d"), AX.X, ALU.add).then_inc(ms_done, 1)
                        dve.wait_ge(ms_done, i + 1)
                        dve.tensor_scalar(ms[:, :], ms[:, :], 1.0 / HD, EPS, ALU.mult, ALU.add)\
                            .then_inc(msv_done, 1)
                        dve.wait_ge(msv_done, i + 1)
                        dve.reciprocal(inv[:, :], ms[:, :]).then_inc(hinv_done, 1)
                    if j == 4:
                        dve.wait_ge(hrstd_done, i + 1)
                        for r in range(4):
                            dve.tensor_tensor(
                                qn[:, r, :, :],
                                tok[:, 1 + r // 2, r % 2, ds(2 * HD * i, 2 * HD)]
                                .rearrange("p (h d) -> p h d", h=2),
                                rstd[:, 2 * r:2 * r + 2].unsqueeze(2).to_broadcast([P, 2, HD]),
                                ALU.mult).then_inc(qn_scaled, 1)
                    if j in (3, 5):
                        take(i, j // 4)
                column_sums(part_done, col_done, A, part, 4 * i,
                            lambda ct: qkT[:, ds(4 * half + ct, 1), ds(S * qk, S)])

            dve.wait_ge(score_masked, 1)
            with dve.Fori(0, 2) as qk:
                with dve.Fori(0, 2) as half:
                    heads_body(qk, half)

            dve.wait_ge(taken_done, 1 + 2 * TOPK // 8)
            dve.tensor_scalar(bias[:, :], scores[:, :], (NONCAUSAL + TAKEN) / 2, MASKED,
                              ALU.is_gt, ALU.mult).then_inc(bias_raw, 1)

            def gates_body(h):
                for j in range(CPG):
                    split(C_GATES + AHEAD + j, h, CPG // SLOTS)
                    if j == 1:
                        dve.wait_ge(logit_full, h + 1)
                        dve.wait_ge(bias_done, 1)
                        dve.tensor_tensor(logit[:, :], B[1][:, 0:KEYS], bias[:, :], ALU.add)\
                            .then_inc(logit_done, 1)
                        dve.wait_ge(logit_done, h + 1)
                        for t, k0, k1 in halves:
                            dve.tensor_reduce(top[:, t:t + 1], logit[:, k0:k1], AX.X, ALU.max)\
                                .then_inc(top_done, 1)
                        dve.wait_ge(top_done, 2 * h + 2)
                        dve.tensor_scalar(ntop[:, :], top[:, :], -SCALE, None, ALU.mult)\
                            .then_inc(ntop_done, 1)
                    if j == 2:
                        dve.wait_ge(ln_done, h + 1)
                        dve.scalar_tensor_tensor(stay[:, :], B[0][:, 0:KEYS], 0.0, soft[:, :],
                                                 ALU.max, ALU.add).then_inc(stay_raw, 1)
                    if j == 3:
                        dve.wait_ge(prob_raw, 2 * h + 2)
                        dve.reciprocal(pinv[:, :], psum_e[:, :]).then_inc(pinv_done, 1)
                column_sums(part_done, col_done, A, part, 16 + 4 * h,
                            lambda ct: gates[:, ds(4 * h + ct, 1), :])
                for ready, done, bank, at_head in ((sb_hi, sb_done, B[2], h),
                                                   (ds_hi, ds_done, B[3], NH + h)):
                    dve.wait_ge(ready, h + 1)
                    dve.tensor_tensor(oT[:, ds(at_head, 1), S:2 * S], bank[:, 0:S].unsqueeze(1),
                                      oT[:, ds(at_head, 1), 0:S].bitcast(f32), ALU.subtract)\
                        .then_inc(done, 1)

            with dve.Fori(0, NH) as h:
                gates_body(h)

            def merged_lo(n, ct):
                dve.wait_ge(mT_hi, 4 * n + ct + 1)
                dve.tensor_tensor(mT[:, ds(4 * n + ct, 1), S:2 * S],
                                  br[0][ct][:, :].unsqueeze(1),
                                  mT[:, ds(4 * n + ct, 1), 0:S].bitcast(f32), ALU.subtract)\
                    .then_inc(mT_done, 1)

            def branch_body(n, before):
                for j in range(CPG):
                    split(C_BRANCH + AHEAD + j, n, CPG // SLOTS)
                    if before and j < 4:
                        merged_lo(n - 1, j)
                    if before and j == 4:
                        dve.wait_ge(mT_done, 4 * n)
                    if j in (4, 5):
                        column_sums(part_done, col_done, A, part, 48 + 4 * n,
                                    lambda ct: br[0][ct][:, :].unsqueeze(1),
                                    (2 * j - 8, 2 * j - 7))
                column_sums(bpart_done, bcol_done, B, partb, 4 * n,
                            lambda ct: br[1][ct][:, :].unsqueeze(1))

            branch_body(0, False)
            with dve.Fori(1, 4) as n:
                branch_body(n, True)

            def out_body(m, first):
                for g in range(2):
                    for j in range(CPG):
                        split(C_OUT + AHEAD + g * CPG + j, m, 2 * CPG // SLOTS)
                        if first and g == 0 and 1 <= j < 5:
                            merged_lo(3, j - 1)
                    if first and g == 0:
                        dve.wait_ge(x_again, 16)
                        for b in range(2):
                            for i in range(4):
                                dve.memset(u[b][i][:, 0:2], 0.0).then_inc(pad_zero, 1)
                    for t in range(TH):
                        wait_full(dve, row_full, 2 * m + g, TH, t,
                                  C_OUT + CPG * (g + 1) + 2 * CPG * m)
                        cols = y[:, t, ds(GRP * 2 * m + GRP * g, GRP)]
                        dve.tensor_tensor(cols, A[2 * g + t][:, :], cols, ALU.add)\
                            .then_inc(row_done, 1)

            out_body(0, True)
            out_body(1, False)
            norm_rows(1, 4)
            transposed_lo(h2T, KT, 1, range(4))
            dve.wait_ge(pad_zero, 8)

            def u_sum(b, n, ct):
                ready, full_at, done = ((part_done, 64, col_done), (bpart_done, 16, bcol_done))[b]
                dve.wait_ge(ready, full_at + 4 * n + ct + 1)
                dve.tensor_tensor(u[b][ct][:, 2:S + 2], (A, B)[b][ct][:, 0:S],
                                  u[b][ct][:, 2:S + 2], ALU.add).then_inc(done, 1)

            def neighbours(b, n, ct):
                e = 4 * n + ct
                w2, w1, w0 = ((gate_w2, gate_w1, gate_w0), (val_w2, val_w1, val_w0))[b]
                for k, before, done in ((1, w2, w1), (0, w1, w0)):
                    column = 2 * KT + 2 * FT * k + b * FT
                    dve.wait_ge(before, e + 1)
                    dve.scalar_tensor_tensor(conv[b][ct % 2][:, :], u[b][ct][:, k:k + S],
                                             params[:, ds(column + e, 1)], conv[b][ct % 2][:, :],
                                             ALU.mult, ALU.add).then_inc(done, 1)

            def ff_lo(n, ct):
                e = 4 * n + ct
                dve.wait_ge(ffT_hi, e + 1)
                dve.tensor_tensor(ffT[:, ds(e, 1), S:2 * S], conv[1][ct % 2][:, :].unsqueeze(1),
                                  ffT[:, ds(e, 1), 0:S].bitcast(f32), ALU.subtract)\
                    .then_inc(ffT_done, 1)

            def up_step(n, j):
                if j < 4:
                    u_sum(1, n - 1, j)
                if j in (1, 3, 5, 7):
                    neighbours(1, n - 1, j // 2)
                if j in (4, 6, 8, 10):
                    ff_lo(n - 1, (j - 4) // 2)

            def gate_step(n, j):
                if j < 4:
                    u_sum(0, n, j)
                if j % 2:
                    neighbours(0, n, j // 2)

            def up_body(n, before):
                for j in range(2 * CPG):
                    split(C_UP + AHEAD + j, n, 2 * CPG // SLOTS)
                    if before:
                        up_step(n, j)
                    elif j < CPG - 2:
                        transposed_lo(h2T, KT, 1, range(4 + CK * j, 4 + CK * (j + 1)))
                    if j >= CPG:
                        gate_step(n, j - CPG)

            up_body(0, False)
            with dve.Fori(1, NU) as n:
                up_body(n, True)
            LAST = 3 * SLOTS
            for j in range(LAST):
                split(C_DOWN + AHEAD + j)
                up_step(NU, j)

            def add_rows(m):
                for t in range(TH):
                    for g in range(2):
                        cols = y[:, t, m * BLOCK + g * GRP:m * BLOCK + (g + 1) * GRP]
                        wait_full(dve, down_full, m, 4, 2 * t + g, C_DOWN + FT * (m + 1))
                        dve.tensor_tensor(cols, A[2 * t + g][:, :], cols, ALU.add)\
                            .then_inc(out_ready, 1)

            first = C_DOWN + AHEAD + LAST
            with dve.Fori(0, (FT - LAST) // SLOTS) as r:
                for j in range(SLOTS):
                    split(first + j, r)
            add_rows(0)
            second = first + FT - LAST
            left = FT - AHEAD
            with dve.Fori(0, left // SLOTS) as r:
                for j in range(SLOTS):
                    split(second + j, r)
            for j in range(left - left % SLOTS, left):
                split(second + j)
            add_rows(1)

        @block.gpsimd
        def _(pool):
            pool.memset(rows_in[:, :, :], 0.0).then_inc(rows_zero, 1)
            pool.memset(ident[:, :], 0.0).then_inc(const_set, 1)
            pool.memset(neg_tri[:, :], -1.0).then_inc(const_set, 1)
            pool.memset(neg_one[:, :], -1.0).then_inc(const_set, 1)
            pool.wait_ge(const_set, 3)
            pool.affine_select(out=ident[:, :], in_=ident[:, :], compare_op=ALU.not_equal,
                               fill=1.0, base=0, pattern=[[-1, P]], channel_multiplier=1)\
                .then_inc(const_sel, 1)
            pool.affine_select(out=neg_tri[:, :], in_=neg_tri[:, :], compare_op=ALU.is_ge,
                               fill=0.0, base=0, pattern=[[-1, P]], channel_multiplier=1)\
                .then_inc(const_sel, 1)
            pool.memset(warm[:, :], 1.0).then_inc(warm_set, 1)
            pool.wait_ge(rows_zero, 1)
            pool.dma_start(rows_in[0:2 * FT, 2:5, :], conv_w.rearrange("k (t p) -> t k p", p=P))\
                .then_inc(conv_in, 16)
            pool.dma_start(rows_in[0:2 * FT, 5, :], conv_b.rearrange("(t p) -> t p", p=P))\
                .then_inc(conv_in, 16)
            pool.dma_start(qk_gain[:, 0, :], q_norm_g.partition_broadcast(P))\
                .then_inc(conv_in, 16)
            pool.dma_start(qk_gain[:, 1, :], k_norm_g.partition_broadcast(P))\
                .then_inc(conv_in, 16)
            for i, f in enumerate(FREQS):
                pool.memset(freq[:, i:i + 1], f).then_inc(freq_set, 1)
            pool.memset(sb_scale[:, :], SCALE).then_inc(scale_set, 1)
            pool.memset(ikT[:, :, :], 0.0).then_inc(ikT_zero, 1)
            pool.memset(scores[:, :], 0.0).then_inc(score_zero, 1)

            def rotate(dst, src, rot, cos, sin, heads, half, sem_mid, count, sem_end):
                rows = cos.shape[1]
                c = cos[:, :, :].unsqueeze(2).to_broadcast([P, rows, heads, 2 * half])
                s = sin[:, :, :].unsqueeze(2).to_broadcast([P, rows, heads, 2 * half])
                pool.tensor_tensor(rot[:, 0], src(0, 2 * half), c, ALU.mult).then_inc(sem_mid, 1)
                pool.tensor_tensor(rot[:, 1, :, :, 0:half], src(half, 2 * half),
                                   s[:, :, :, 0:half], ALU.mult).then_inc(sem_mid, 1)
                pool.tensor_tensor(rot[:, 1, :, :, half:2 * half], src(0, half),
                                   s[:, :, :, half:2 * half], ALU.mult).then_inc(sem_mid, 1)
                pool.wait_ge(sem_mid, count)
                pool.tensor_tensor(dst, rot[:, 0], rot[:, 1], ALU.add).then_inc(sem_end, 1)

            pool.wait_ge(tok_done, TH)
            pool.wait_ge(cos_set, 20)
            for e in range(2):
                pool.tensor_copy(k_ix[:, :, e, 2 * IHALF:ID], tail[:, :, 2 * IHALF:ID])\
                    .then_inc(kix_a, 1)
            rotate(k_ix[:, :, :, 0:2 * IHALF],
                   lambda a, b: tail[:, :, a:b].unsqueeze(2).to_broadcast([P, TH, 2, b - a]),
                   rot_k, cos_i, sin_i, 2, IHALF, kix_b, 3, kix_done)

            with pool.Fori(1, NB) as b:
                q4 = tok[:, NB - 1, :, ds(4 * ID * (b - 1), 4 * ID)]\
                    .rearrange("p t (h d) -> p t h d", h=4)
                pool.wait_ge(tok_done, 2 + 4)
                pool.wait_ge(iqT_full, 1 + b - 1)
                for t in range(TH):
                    pool.tensor_copy(iq[:, t, :, 2 * IHALF:ID], q4[:, t, :, 2 * IHALF:ID])\
                        .then_inc(iq_done, 1)
                rotate(iq[:, :, :, 0:2 * IHALF], lambda c0, c1: q4[:, :, :, c0:c1], rot_i, cos_i,
                       sin_i, 4, IHALF, iq_rot, 3 * b, iq_done)

            pool.wait_ge(score_add, 1 + 2 * NI)
            diagonal = lambda t: t[:, :].rearrange("p (b c) -> p b c", b=3)[:, 0:3:2, :]
            pool.affine_select(out=diagonal(scores), in_=diagonal(scores), compare_op=ALU.is_ge,
                               fill=NONCAUSAL, base=0, pattern=[[0, 2], [-1, P]],
                               channel_multiplier=1).then_inc(score_masked, 1)

            with pool.Fori(0, 4) as i:
                pool.wait_ge(qn_scaled, 4 * i + 4)
                for r in range(4):
                    pool.tensor_tensor(
                        qn[:, r, :, :], qn[:, r, :, :],
                        qk_gain[:, r // 2:r // 2 + 1, :].to_broadcast([P, 2, HD]),
                        ALU.mult).then_inc(qn_gain, 1)
                pool.wait_ge(qn_gain, 4 * i + 4)
                rotate(qn[:, :, :, 0:2 * HALF], lambda c0, c1: qn[:, :, :, c0:c1], rot_d, cos_d,
                       sin_d, 2, HALF, qn_rot, 3 * i + 3, qn_done)

            pool.wait_ge(bias_raw, 1)
            pool.affine_select(out=diagonal(bias), in_=diagonal(bias), compare_op=ALU.is_ge,
                               fill=MASKED, base=0, pattern=[[0, 2], [-1, P]],
                               channel_multiplier=1).then_inc(bias_done, 1)

            pool.wait_ge(scale_set, 1)

            def stage_sb(h):
                pool.tensor_tensor(sb_k[:, :].unsqueeze(1), qkT[:, ds(h, 1), S:2 * S],
                                   sb_scale[:, :].unsqueeze(1).to_broadcast([P, 1, S]),
                                   ALU.mult).then_inc(staged_qk, 1)
                pool.tensor_copy(sb_q[:, :].unsqueeze(1), qkT[:, ds(h, 1), 0:S])\
                    .then_inc(staged_qk, 1)

            def stage_ds(h):
                pool.tensor_copy(ds_qk[:, :].unsqueeze(1), qkT[:, ds(NH + h, 1), :])\
                    .then_inc(staged_qk, 1)

            def head_body(h, more):
                pool.wait_ge(ds_full, 1 + h)
                pool.tensor_copy(sb_v[:, :, :], tok[:, 0, :, ds(HD * h, HD)]).then_inc(staged_v, 1)
                pool.tensor_copy(ds_v[:, :, :], tok[:, 3, :, ds(HD * h, HD)]).then_inc(staged_v, 1)
                wait_alone(pool, stay_raw, h + 1)
                pool.affine_select(out=diagonal(stay), in_=diagonal(stay), compare_op=ALU.is_gt,
                                   fill=0.0, base=0, pattern=[[0, 2], [1, P]],
                                   channel_multiplier=-1).then_inc(stay_done, 1)
                wait_alone(pool, pinv_done, h + 1)
                for t, (k0, k1) in enumerate(((0, P), (P, KEYS))):
                    pool.tensor_scalar(prob[:, k0:k1], prob[:, k0:k1], pinv[:, t:t + 1], None,
                                       ALU.mult).then_inc(prob_done, 1)
                if more:
                    pool.wait_ge(logit_full, h + 1)
                    stage_sb(h + 1)
                wait_alone(pool, stick_raw, h + 1)
                pool.affine_select(out=diagonal(stick), in_=diagonal(stick), compare_op=ALU.is_gt,
                                   fill=0.0, base=0, pattern=[[0, 2], [1, P]],
                                   channel_multiplier=-1).then_inc(stick_done, 1)
                if more:
                    stage_ds(h + 1)

            pool.wait_ge(col_done, 16)
            pool.wait_ge(qkT_done, 8)
            stage_sb(0)
            stage_ds(0)
            with pool.Fori(0, NH - 1) as h:
                head_body(h, True)
            head_body(NH - 1, False)

            def mix_body(n, last):
                for ct in range(4):
                    pool.wait_ge(sig_done, 8 * n + ct + 1)
                    pool.wait_ge(col_done, 48 + 4 * n + ct + 1)
                    pool.tensor_tensor(br[0][ct][:, :], br[0][ct][:, :], sig[0][ct][:, :],
                                       ALU.mult).then_inc(mix_a, 1)
                if last:
                    pool.wait_ge(sig_done, 32)
                    pool.dma_start(y[:, :, :], x[0, :, :].rearrange("(t p) d -> p t d", p=P))\
                        .then_inc(x_again, 16)
                for ct in range(4):
                    pool.wait_ge(sig_done, 8 * n + 4 + ct + 1)
                    pool.wait_ge(bcol_done, 4 * n + ct + 1)
                    pool.tensor_tensor(br[1][ct][:, :], br[1][ct][:, :], sig[1][ct][:, :],
                                       ALU.mult).then_inc(mix_b, 1)
                    pool.wait_ge(mix_a, 4 * n + ct + 1)
                    pool.wait_ge(mix_b, 4 * n + ct + 1)
                    pool.tensor_tensor(br[0][ct][:, :], br[0][ct][:, :], br[1][ct][:, :],
                                       ALU.add).then_inc(mix_done, 1)

            with pool.Fori(0, 3) as n:
                mix_body(n, False)
            mix_body(3, True)

            def column(first, e):
                return params[:, ds(first + e, 1)].to_broadcast([P, S])

            CONV_B = 2 * KT + 3 * 2 * FT

            def begin(b, n, ct, ready, at_, done):
                e = 4 * n + ct
                if not isinstance(e, int) or e >= 2:
                    pool.wait_ge((silu_done, ffT_done)[b], e - 1)
                pool.wait_ge(ready, at_ + e + 1)
                pool.tensor_tensor(conv[b][ct % 2][:, :], u[b][ct][:, 2:S + 2],
                                   column(2 * KT + 2 * FT * 2 + b * FT, e), ALU.mult)\
                    .then_inc(done, 1)

            def gate_tiles(n):
                for ct in range(4):
                    begin(0, n, ct, col_done, 64, gate_w2)

            def val_tiles(n):
                for ct in range(4):
                    e = 4 * n + ct
                    c = conv[1][ct % 2][:, :]
                    begin(1, n, ct, bcol_done, 16, val_w2)
                    pool.wait_ge(val_w0, e + 1)
                    pool.tensor_tensor(c, c, column(CONV_B + FT, e), ALU.add)\
                        .then_inc(val_bias, 1)
                    pool.wait_ge(val_bias, e + 1)
                    pool.wait_ge(silu_done, e + 1)
                    pool.tensor_tensor(c, c, silu[ct][:, :], ALU.mult).then_inc(act_done, 1)

            gate_tiles(0)
            val_tiles(0)
            gate_tiles(1)
            with pool.Fori(2, NU) as n:
                val_tiles(n - 1)
                gate_tiles(n)
            val_tiles(NU - 1)

        @block.tensor
        def _(pe):
            def mm(o, l, r, start, stop):
                return pe.matmul(o, l, r, start=start, stop=stop, skip_group_check=True)

            def rows_chunk(c, slot, src, kts, width, outs, first, last, free, full):
                n = len(kts)
                wh = hi[slot][:, 0:n * width].rearrange("p (k c) -> p k c", k=n)
                wl = lo[slot][:, 0:n * width].rearrange("p (k c) -> p k c", k=n)
                pe.wait_ge(lo_done, c)
                for o, (bank, t, c0, c1) in enumerate(outs):
                    if first and free is not None:
                        free(o)
                    out_ = bank[:, 0:c1 - c0]
                    for j, kt in enumerate(kts):
                        xh = src[:, kt, t * P:(t + 1) * P]
                        xl = src[:, kt, S + t * P:S + (t + 1) * P]
                        mm(out_, xh, wh[:, j, c0:c1], first and j == 0, False)
                        mm(out_, xl, wh[:, j, c0:c1], False, False)
                        i = mm(out_, xh, wl[:, j, c0:c1], False, last and j == n - 1)
                    if last and o < len(outs) - 1:
                        i.then_inc(full, 1)
                i.then_inc(w_used, 1)

            def cols_chunk(c, slot, src, kts, bank, first, last, free, full):
                wh = hi[slot][:, :].rearrange("p (k c) -> p k c", k=CK)
                wl = lo[slot][:, :].rearrange("p (k c) -> p k c", k=CK)
                pe.wait_ge(lo_done, c)
                for ct in range(4):
                    if first and free is not None:
                        free(ct)
                    cs = slice(ct * P, (ct + 1) * P)
                    for j, kt in enumerate(kts):
                        if not (first and j == 0):
                            mm(bank[ct][:, 0:S], wl[:, j, cs], src[:, kt, 0:S], False, False)
                        i = mm(bank[ct][:, :], wh[:, j, cs], src[:, kt, :], first and j == 0,
                               last and j == CK - 1)
                        if first and j == 0:
                            mm(bank[ct][:, 0:S], wl[:, j, cs], src[:, kt, 0:S], False, False)
                    if last and ct < 3:
                        i.then_inc(full, 1)
                i.then_inc(w_used, 1)

            def transposes(k, kts):
                for kt in kts:
                    if kt >= 4:
                        pe.wait_ge(xT_lo, k * KT + kt - 3)
                    for t in range(TH):
                        i = mm(B[kt % 4][:, t * P:(t + 1) * P], y[:, t, kt * P:(kt + 1) * P],
                               diag[:, t, :], True, True)
                    i.then_inc(xT_full, 1)

            prime(pe, iqT_full, sb_full, ds_full)
            pe.wait_ge(const_sel, 2)
            pe.wait_ge(small_in, 16 * 2)
            pe.wait_ge(conv_in, 16 * 4)
            for r, (n, at_) in enumerate(((KT, 0), (KT, KT), *((2 * FT, 2 * KT + 2 * FT * k)
                                                               for k in range(4)))):
                i = pe.transpose(B[3][:, at_:at_ + n], rows_in[0:n, r, :], ident[0:n, 0:n])
            i.then_inc(params_T, 1)
            pe.wait_ge(params_done, 1)
            pe.wait_ge(diag_done, TH)
            transposes(0, range(TAIL_CK))
            for c in range(C_ROWS):
                if c + 1 < C_ROWS:
                    transposes(0, range(TAIL_CK * (c + 1), TAIL_CK * (c + 2)))
                pe.wait_ge(xT_lo, TAIL_CK * (c + 1))
                rows_chunk(c + 1, c, hT, range(TAIL_CK * c, TAIL_CK * (c + 1)), TAIL,
                           [(A[2 + t], t, 0, TAIL) for t in range(TH)], c == 0,
                           c == C_ROWS - 1, None, tok_full)
            def rows_body(b, index):
                for g in range(2):
                    def free(t):
                        if index:
                            pe.wait_ge(tok_done, 2 + 4 * (b - 1) + 2 * g + t + 1)
                        elif g == 1:
                            pe.wait_ge(tok_done, t + 1)
                    for j in range(CPG):
                        rows_chunk(C_ROWS + g * CPG + j + 1 + 2 * CPG * b, j % SLOTS, hT,
                                   range(CK * j, CK * (j + 1)), GRP,
                                   [(A[2 * g + t], t, 0, GRP) for t in range(TH)], j == 0,
                                   j == CPG - 1, free, tok_full)
                        if not index:
                            if (g, j) == (1, 3):
                                pe.wait_ge(kix_a, 2)
                                pe.wait_ge(kix_done, 1)
                                for t in range(TH):
                                    i = pe.transpose(
                                        B[0][:, t * P:(t + 1) * P],
                                        k_ix[:, t, :, :].rearrange("p e d -> p (e d)"),
                                        ident[:, :])
                                i.then_inc(kixT_full, 1)
                            continue
                        if g == 0 and j == 3:
                            pe.wait_ge(iq_done, 3 * b)
                            pe.wait_ge(relu_done, 1 + 4 * (b - 1))
                            pe.wait_ge(ikT_done, 2)
                            for p2 in range(2):
                                for t in range(TH):
                                    i = pe.transpose(
                                        B[0][:, (2 * p2 + t) * P:(2 * p2 + t + 1) * P],
                                        iq[:, t, 2 * p2:2 * p2 + 2, :]
                                        .rearrange("p h d -> p (h d)"), ident[:, :])
                            i.then_inc(iqT_full, 1)
                        if (g, j) in ((0, 7), (1, 3)):
                            pair = g
                            at0, at1 = (B[1], B[2]) if pair == 0 else (B[3], B[0])
                            pe.wait_ge(iqT_done, b)
                            mm(at0[:, 0:2 * P], iqT[:, pair, 0:P], ikT[:, :, 0:P], True, True)\
                                .then_inc(sc_full, 1)
                            mm(at1[:, :], iqT[:, pair, P:S], ikT[:, :, :], True, True)\
                                .then_inc(sc_full, 1)

            rows_body(0, False)
            with pe.Fori(1, NB) as b:
                rows_body(b, True)

            pe.wait_ge(relu_done, 1 + NI)

            def heads_body(i):
                def free(ct):
                    pe.wait_ge(col_done, 4 * i - 4 + ct + 1)
                first_group = isinstance(i, int)

                def free0(ct):
                    pe.wait_ge(tok_done, 2 + 4 * NB)
                for j in range(CPG):
                    cols_chunk(C_HEADS + CPG * i + j + 1, j % SLOTS, hT,
                               range(CK * j, CK * (j + 1)), A, j == 0, j == CPG - 1,
                               free0 if first_group else free, col_full)
                    if j == 7:
                        pe.wait_ge(qn_done, i + 1)
                        pe.wait_ge(qkT_done, 2 * i)
                        for r in range(2):
                            for h in range(2):
                                for t in range(TH):
                                    k = pe.transpose(
                                        B[r][:, (2 * h + t) * P:(2 * h + t + 1) * P],
                                        qn[:, 2 * r + t, h, :], ident[:, :])
                            k.then_inc(qn_T, 1)

            heads_body(0)
            with pe.Fori(1, 4) as i:
                heads_body(i)

            with pe.Fori(0, NH) as h:
                def free_gate(ct):
                    pe.wait_ge(col_done, 16 + 4 * h - 4 + ct + 1)
                for j in range(CPG):
                    cols_chunk(C_GATES + CPG * h + j + 1, j % SLOTS, hT,
                               range(CK * j, CK * (j + 1)), A, j == 0, j == CPG - 1,
                               free_gate, col_full)
                    if j == 0:
                        pe.wait_ge(staged_qk, 3 * h + 3)
                        mm(B[0][:, 0:S], sb_k[:, 0:P], sb_q[:, :], True, True)
                        mm(B[0][:, S:KEYS], sb_k[:, P:S], sb_q[:, P:S], False, True)\
                            .then_inc(z_full, 1)
                        mm(B[1][:, 0:P], ds_qk[:, 0:P], ds_qk[:, S:S + P], True, True)
                        mm(B[1][:, P:KEYS], ds_qk[:, P:S], ds_qk[:, S:2 * S], True, True)\
                            .then_inc(logit_full, 1)
                    if j == 3:
                        pe.wait_ge(stay_done, h + 1)
                        mm(B[0][:, S:KEYS], neg_tri[:, :], stay[:, S:KEYS], False, True)
                        mm(B[0][:, P:S], neg_one[:, :], stay[:, S:KEYS], False, True)
                        mm(B[0][:, 0:S], neg_tri[:, :], stay[:, 0:S], False, True)\
                            .then_inc(suffix_full, 1)
                    if j == 4:
                        pe.wait_ge(prob_done, 2 * h + 2)
                        pe.wait_ge(ds_done, 1 + h)
                        for k in range(3):
                            i = pe.transpose(B[3][:, k * P:(k + 1) * P],
                                             prob[:, k * P:(k + 1) * P], ident[:, :])
                        i.then_inc(probT_full, 1)
                for bank, v, w, full, ready, done in (
                        (B[2], sb_v, stick, sb_full, stick_done, sb_done),
                        (B[3], ds_v, probT, ds_full, probT_done, None)):
                        pe.wait_ge(ready, h + 1)
                        if done is not None:
                            pe.wait_ge(done, 1 + h)
                        pe.wait_ge(staged_v, 2 * h + 2)
                        mm(bank[:, 0:S], v[:, 0, :], w[:, 0:S], True, True)
                        mm(bank[:, P:S], v[:, 1, :], w[:, S:KEYS], False, True).then_inc(full, 1)

            def branch_body(n):
                first_group = isinstance(n, int)

                def free_sb(ct):
                    pe.wait_ge(col_done, 48 + 4 * n - 4 + ct + 1)

                def free_ds(ct):
                    if not first_group:
                        pe.wait_ge(bcol_done, 4 * n - 4 + ct + 1)
                for j in range(CPG):
                    if first_group and j < 4:
                        pe.wait_ge(sb_done, 1 + NH)
                    if first_group and j == 4:
                        pe.wait_ge(ds_done, 1 + NH)
                    cols_chunk(C_BRANCH + CPG * n + j + 1, j % SLOTS, oT,
                               range(CK * j, CK * (j + 1)), (A, B)[j // 4], j % 4 == 0,
                               j % 4 == 3, (free_sb, free_ds)[j // 4],
                               (col_full, bcol_full)[j // 4])

            branch_body(0)
            with pe.Fori(1, 4) as n:
                branch_body(n)

            for m in range(2):
                for g in range(2):
                    def free_row(t):
                        if m == 0:
                            pe.wait_ge(col_done, 64)
                        else:
                            pe.wait_ge(row_done, 4 * (m - 1) + 2 * g + t + 1)
                    for j in range(CPG):
                        if m == 0 and g == 0:
                            pe.wait_ge(mT_done, CK * (j + 1))
                        rows_chunk(C_OUT + CPG * (2 * m + g) + j + 1, j % SLOTS, mT,
                                   range(CK * j, CK * (j + 1)), GRP,
                                   [(A[2 * g + t], t, 0, GRP) for t in range(TH)], j == 0,
                                   j == CPG - 1, free_row, row_full)
            pe.wait_ge(bcol_done, 16)
            pe.wait_ge(diag_done, 2 * TH)
            transposes(1, range(4))

            def up_body(n):
                first_pair = isinstance(n, int)

                def free_a(ct):
                    if first_pair:
                        pe.wait_ge(row_done, 8)
                    else:
                        pe.wait_ge(col_done, 64 + 4 * n - 4 + ct + 1)

                def free_b(ct):
                    if not first_pair:
                        pe.wait_ge(bcol_done, 16 + 4 * n - 4 + ct + 1)
                for b in range(2):
                    for j in range(CPG):
                        if first_pair and b == 0:
                            if j < CPG - 2:
                                transposes(1, range(4 + CK * j, 4 + CK * (j + 1)))
                            pe.wait_ge(xT_lo, KT + CK * (j + 1))
                        cols_chunk(C_UP + b * CPG + 2 * CPG * n + j + 1, j % SLOTS, h2T,
                                   range(CK * j, CK * (j + 1)), (A, B)[b], j == 0,
                                   j == CPG - 1, (free_a, free_b)[b],
                                   (col_full, bcol_full)[b])

            up_body(0)
            with pe.Fori(1, NU) as n:
                up_body(n)

            for m in range(2):
                def free_down(o):
                    if m == 0:
                        pe.wait_ge(col_done, 64 + 4 * NU)
                    else:
                        pe.wait_ge(out_ready, 4 * (m - 1) + o + 1)
                for k in range(FT):
                    if m == 0:
                        pe.wait_ge(ffT_done, k + 1)
                    rows_chunk(C_DOWN + FT * m + k + 1, k % SLOTS, ffT, [k], BLOCK,
                               [(A[2 * t + g], t, g * GRP, (g + 1) * GRP)
                                for t in range(TH) for g in range(2)], k == 0,
                               k == FT - 1, free_down, down_full)


_INS = ["x", "positions", "attn_norm_g", "w_in", "q_norm_g", "k_norm_g", "w_branch", "w_out",
        "ffn_norm_g", "w_up", "conv_w", "conv_b", "w_down"]


def kernel(**inputs):
    import concourse.bacc as bacc
    from concourse.bass_utils import run_bass_kernel_spmd

    nc = bacc.Bacc("TRN2", target_bir_lowering=False, num_devices=1)
    arrays, args = {}, []
    for name in _INS:
        a = np.ascontiguousarray(inputs[name])
        arrays[f"in_{name}"] = a
        args.append(nc.dram_tensor(f"in_{name}", a.shape, mybir.dt.from_np(a.dtype),
                                   kind="ExternalInput").ap())
    shape = inputs["x"].shape
    out = nc.dram_tensor("out", shape, mybir.dt.float32, kind="ExternalOutput").ap()
    hybrid_layer(nc, *args, out)
    r = run_bass_kernel_spmd(nc, [arrays], core_ids=[0])
    return r.results[0]["out"]
```

```python
import math

import numpy as np

import concourse.bass as bass
from concourse import mybir
from contextlib import ExitStack


def hybrid_layer(nc, x, positions, attn_norm_g, w_in, q_norm_g, k_norm_g, w_branch, w_out,
                 ffn_norm_g, w_up, conv_w, conv_b, w_down, out):
    f32 = mybir.dt.float32
    f32r = mybir.dt.float32r
    i32 = mybir.dt.int32
    ACT = mybir.ActivationFunctionType
    ALU = mybir.AluOpType
    AX = mybir.AxisListType
    ds = bass.ds

    P = 128
    S, D = x.shape[1], x.shape[2]
    TH = S // P
    KT = D // P
    HD = 128
    NH = 8
    NI, ID = 16, 64
    FF = w_down.shape[0]
    FT = FF // P
    TOPK = min(256, S // 4)
    EPS = 1e-6
    SCALE = HD ** -0.5
    IDX_SCALE = ID ** -0.5 * NI ** -0.5
    HALF = HD // 4 // 2
    IHALF = ID // 4 // 2
    GRP = 512
    CK = 2
    CPG = KT // CK
    BLOCK = 2 * GRP
    SLOTS = 4
    AHEAD = 3
    NB = 5
    TAIL_AT = 7 * BLOCK
    TAIL = ID + NI
    TAIL_CK = 4
    GATE_AT = TAIL_AT + TAIL
    KEYS = P + S

    C_ROWS = KT // TAIL_CK
    C_HEADS = C_ROWS + NB * 2 * CPG
    C_GATES = C_HEADS + 4 * CPG
    C_BRANCH = C_GATES + 8 * CPG
    C_OUT = C_BRANCH + 4 * CPG
    C_UP = C_OUT + 4 * CPG
    NU = FF // GRP
    C_DOWN = C_UP + NU * 2 * CPG
    for first in (C_ROWS, C_HEADS, C_GATES, C_BRANCH, C_OUT, C_UP, C_DOWN):
        assert first % SLOTS == 0

    NONCAUSAL, TAKEN, MASKED = -1e38, -3e38, -1e30
    ROUND = 1.5 * 2.0 ** 23
    TWO_PI_A, TWO_PI_B = 6.28125, 0.00193500518798828125
    TWO_PI_C = 2 * math.pi - TWO_PI_A - TWO_PI_B
    SIN_MAX = 3.1415925
    FREQS = [float(np.float32(500000.0) ** np.float32(-i / HALF)) for i in range(HALF)]

    ctx = ExitStack()
    with ctx:
        KB = 1024
        ARENA = 206 * KB
        arena = ctx.enter_context(nc.sbuf_tensor("arena", [P, ARENA // 4], f32))
        base = nc.lookup_mloc(arena).addr

        def at(name, shape, offset, dtype=f32):
            assert offset + 4 * int(np.prod(shape)) <= ARENA
            return nc.alloc_sbuf_tensor_at(name, [P, *shape], dtype, offset=base + offset)

        def sem(name):
            return ctx.enter_context(nc.semaphore(name))

        hT = at("hT", [KT, 2 * S], 0, f32r)
        mT = at("mT", [KT, 2 * S], 0, f32r)
        tok = at("tok", [NB, TH, BLOCK], 32 * KB)
        gates = at("gates", [2 * KT, S], 72 * KB)
        diag = at("diag", [TH, P], 72 * KB)
        y = at("y", [TH, D], 88 * KB)
        ffT = at("ffT", [FT, 2 * S], 0, f32r)
        qkT = at("qkT", [2 * NH, 2 * S], 104 * KB)
        oT = at("oT", [2 * NH, 2 * S], 104 * KB, f32r)
        h2T = at("h2T", [KT, 2 * S], 104 * KB, f32r)
        raw = [at(f"raw{i}", [2 * GRP], (136 + 4 * i) * KB) for i in range(SLOTS)]
        hi = [at(f"hi{i}", [2 * GRP], (152 + 4 * i) * KB, f32r) for i in range(SLOTS)]
        lo = [at(f"lo{i}", [2 * GRP], (168 + 4 * i) * KB, f32r) for i in range(SLOTS)]
        ident = at("ident", [P], 184 * KB)
        params = at("params", [2 * KT + 4 * 2 * FT], 184 * KB + 512)
        A0 = 186 * KB
        neg_tri = at("neg_tri", [P], A0)
        neg_one = at("neg_one", [P], A0 + 512)
        qk_gain = at("qk_gain", [2, HD], A0 + 1024)
        tail = at("tail", [TH, TAIL], A0 + 2048)
        wix = at("wix", [TH, NI], A0 + 2688)
        cos_d = at("cos_d", [4, 2 * HALF], A0 + 2816)
        sin_d = at("sin_d", [4, 2 * HALF], A0 + 3328)
        cos_i = at("cos_i", [TH, 2 * IHALF], A0 + 3840)
        sin_i = at("sin_i", [TH, 2 * IHALF], A0 + 3968)
        bias = at("bias", [KEYS], A0 + 4096)
        scores = at("scores", [KEYS], A0 + 5632)
        probT = at("probT", [KEYS], A0 + 5632)
        W0 = A0 + 7 * KB
        part = [at(f"part{i}", [S], W0 + i * KB) for i in range(4)]
        sb_q = at("sb_q", [S], W0 + 4 * KB)
        sb_k = at("sb_k", [S], W0 + 5 * KB)
        ds_qk = at("ds_qk", [2 * S], W0 + 6 * KB)
        sb_v = at("sb_v", [TH, HD], W0 + 8 * KB)
        ds_v = at("ds_v", [TH, HD], W0 + 9 * KB)
        partb = [at(f"partb{i}", [S], W0 + (4 + i) * KB) for i in range(4)]
        rms_row = at("rms_row", [S], A0 + 17 * KB)
        one = at("one", [P], A0 + 18 * KB)
        Z0 = A0 + 19 * KB
        ss = at("ss", [TH, 4], Z0)
        var2 = at("var2", [TH], Z0 + 32)
        inv2 = at("inv2", [TH], Z0 + 64)
        warm = at("warm", [1], Z0 + 288)
        rstd2 = at("rstd2", [TH], Z0 + 96)
        top = at("top", [2], Z0 + 128)
        ntop = at("ntop", [2], Z0 + 160)
        psum_e = at("psum_e", [2], Z0 + 192)
        pinv = at("pinv", [2], Z0 + 224)
        sb_scale = at("sb_scale", [1], Z0 + 256)
        ikT = at("ikT", [2, S], 104 * KB, f32r)
        ikT_lo = at("ikT_lo", [2, S], 126 * KB, f32r)
        iqT_lo = at("iqT_lo", [2, S], 128 * KB, f32r)
        iq = at("iq", [TH, 4, ID], 106 * KB)
        iqT = at("iqT", [2, S], 108 * KB, f32r)
        relu = [at(f"relu{i}", [2, KEYS], (110 + 3 * i) * KB) for i in range(2)]
        rot_i = at("rot_i", [2, TH, 4, 2 * IHALF], 116 * KB)
        tailT = at("tailT", [S], 125 * KB)
        rows_in = at("rows_in", [6, P], 118 * KB)
        freq = at("freq", [HALF], 121 * KB)
        ang = at("ang", [2, TH, HALF], 121 * KB + 256)
        turn = at("turn", [2, TH, HALF], 121 * KB + 512)
        trig = at("trig", [2, TH, HALF], 121 * KB + 768)
        pos_i = at("pos_i", [TH], 122 * KB, i32)
        pos_f = at("pos_f", [TH], 122 * KB + 64)
        k_ix = at("k_ix", [TH, 2, ID], 123 * KB)
        rot_k = at("rot_k", [2, TH, 2, 2 * IHALF], 124 * KB)
        junk = at("junk", [TH, D], 32 * KB)
        sq = at("sq", [4, 2, HD], 72 * KB)
        qn = at("qn", [4, 2, HD], 76 * KB)
        rot_d = at("rot_d", [2, 4, 2, 2 * HALF], 80 * KB)
        ms = at("ms", [8], 82 * KB)
        inv = at("inv", [8], 82 * KB + 64)
        rstd = at("rstd", [8], 82 * KB + 128)
        best = at("best", [2, 8], 82 * KB + 192)
        soft = at("soft", [KEYS], 64 * KB)
        stay = at("stay", [KEYS], 64 * KB + 1536)
        stick = at("stick", [KEYS], 64 * KB + 3072)
        logit = at("logit", [KEYS], 64 * KB + 4608)
        prob = at("prob", [KEYS], 64 * KB + 6144)
        sig = [[at(f"sig{b}{i}", [S], (32 + 4 * b + i) * KB) for i in range(4)] for b in range(2)]
        br = [[at(f"br{b}{i}", [S], (40 + 4 * b + i) * KB) for i in range(4)] for b in range(2)]
        junk2 = at("junk2", [TH, GRP], 40 * KB)
        U0 = A0
        u = [[at(f"u{b}{i}", [S + 2], U0 + (4 * b + i) * 1056) for i in range(4)]
             for b in range(2)]
        conv = [[at(f"conv{b}{i}", [S], U0 + 9 * KB + (2 * b + i) * KB) for i in range(2)]
                for b in range(2)]
        silu = [at(f"silu{i}", [S], U0 + (13 + i) * KB) for i in range(4)]

        banks = [ctx.enter_context(nc.psum_tensor(f"bank{i}", [P, 512], f32)) for i in range(8)]
        A, B = banks[:4], banks[4:]

        w_landed = [sem(f"w_landed{i}") for i in range(SLOTS)]
        hi_done = sem("hi_done")
        lo_done = sem("lo_done")
        w_used = sem("w_used")
        x_in = [sem(f"x_in{i}") for i in range(2 * TH)]
        pos_in = sem("pos_in")
        small_in = sem("small_in")
        conv_in = sem("conv_in")
        gain_in = sem("gain_in")
        x_again = sem("x_again")
        const_set = sem("const_set")
        const_sel = sem("const_sel")
        scale_set = sem("scale_set")
        rows_zero = sem("rows_zero")
        freq_set = sem("freq_set")
        warm_set = sem("warm_set")
        trig_step = sem("trig_step")
        angle_done = sem("angle_done")
        sin_done = sem("sin_done")
        cos_set = sem("cos_set")
        ss_done = sem("ss_done")
        var_done = sem("var_done")
        inv_done = sem("inv_done")
        rstd_done = sem("rstd_done")
        params_T = sem("params_T")
        params_done = sem("params_done")
        xT_full = sem("xT_full")
        xT_hi = sem("xT_hi")
        xT_lo = sem("xT_lo")
        tailT_half = sem("tailT_half")
        tailT_done = sem("tailT_done")
        tail_full = sem("tail_full")
        tok_full = sem("tok_full")
        tok_done = sem("tok_done")
        wix_done = sem("wix_done")
        kix_a = sem("kix_a")
        kix_b = sem("kix_b")
        kix_done = sem("kix_done")
        kixT_full = sem("kixT_full")
        ikT_zero = sem("ikT_zero")
        ikT_hi = sem("ikT_hi")
        iqT_hi = sem("iqT_hi")
        ikT_done = sem("ikT_done")
        score_zero = sem("score_zero")
        iq_rot = sem("iq_rot")
        iq_done = sem("iq_done")
        iqT_full = sem("iqT_full")
        iqT_done = sem("iqT_done")
        sc_full = sem("sc_full")
        relu_done = sem("relu_done")
        score_add = sem("score_add")
        score_masked = sem("score_masked")
        best_done = sem("best_done")
        taken_done = sem("taken_done")
        bias_raw = sem("bias_raw")
        bias_done = sem("bias_done")
        sq_done = sem("sq_done")
        ms_done = sem("ms_done")
        msv_done = sem("msv_done")
        hinv_done = sem("hinv_done")
        hrstd_done = sem("hrstd_done")
        qn_scaled = sem("qn_scaled")
        qn_gain = sem("qn_gain")
        qn_rot = sem("qn_rot")
        qn_done = sem("qn_done")
        qn_T = sem("qn_T")
        qkT_done = sem("qkT_done")
        col_full = sem("col_full")
        part_done = sem("part_done")
        col_scaled = sem("col_scaled")
        col_done = sem("col_done")
        bcol_full = sem("bcol_full")
        bpart_done = sem("bpart_done")
        bcol_done = sem("bcol_done")
        staged_qk = sem("staged_qk")
        staged_v = sem("staged_v")
        z_full = sem("z_full")
        logit_full = sem("logit_full")
        abs_done = sem("abs_done")
        exp_done = sem("exp_done")
        ln_done = sem("ln_done")
        stay_raw = sem("stay_raw")
        stay_done = sem("stay_done")
        suffix_full = sem("suffix_full")
        stick_raw = sem("stick_raw")
        stick_done = sem("stick_done")
        logit_done = sem("logit_done")
        top_done = sem("top_done")
        ntop_done = sem("ntop_done")
        prob_raw = sem("prob_raw")
        pinv_done = sem("pinv_done")
        prob_done = sem("prob_done")
        probT_full = sem("probT_full")
        probT_done = sem("probT_done")
        sb_full = sem("sb_full")
        ds_full = sem("ds_full")
        sb_hi = sem("sb_hi")
        ds_hi = sem("ds_hi")
        sb_done = sem("sb_done")
        ds_done = sem("ds_done")
        sig_done = sem("sig_done")
        mix_a = sem("mix_a")
        mix_b = sem("mix_b")
        mix_done = sem("mix_done")
        mT_hi = sem("mT_hi")
        mT_done = sem("mT_done")
        row_full = sem("row_full")
        row_done = sem("row_done")
        diag_done = sem("diag_done")
        rms_full = sem("rms_full")
        rms_done = sem("rms_done")
        gate_scaled = sem("gate_scaled")
        val_scaled = sem("val_scaled")
        pad_zero = sem("pad_zero")
        gate_w2 = sem("gate_w2")
        gate_w1 = sem("gate_w1")
        gate_w0 = sem("gate_w0")
        silu_done = sem("silu_done")
        val_w2 = sem("val_w2")
        val_w1 = sem("val_w1")
        val_w0 = sem("val_w0")
        val_bias = sem("val_bias")
        act_done = sem("act_done")
        ffT_hi = sem("ffT_hi")
        ffT_done = sem("ffT_done")
        down_full = sem("down_full")
        out_ready = sem("out_ready")
        stored = sem("stored")
        passed = sem("passed")

        block = ctx.enter_context(nc.Block())

        def wait_alone(engine, semaphore, value):
            engine.wait_ge(semaphore, value)
            engine.sem_inc(passed, 1)

        def prime(engine, *semaphores):
            for s in semaphores:
                engine.sem_inc(s, 1)

        def wait_full(engine, full, group, count, bank, end):
            if bank < count - 1:
                engine.wait_ge(full, (count - 1) * group + bank + 1)
            else:
                engine.wait_ge(w_used, end)

        @block.sync
        def _(sp):
            def load(slot, dst, src):
                sp.dma_start(dst, src).then_inc(w_landed[slot], 16)

            def load_group(c0, w, step, col, n=CPG, width=GRP, per=CK):
                for j in range(n):
                    wait_alone(sp, lo_done, c0 + j - AHEAD + step)
                    rows = w[j * per * P:(j + 1) * per * P, ds(col, width)]
                    load(j % SLOTS, raw[j % SLOTS][:, :].rearrange("p (k c) -> p k c", k=per),
                         rows.rearrange("(k p) c -> p k c", p=P))

            for half in range(2):
                cols = slice(half * BLOCK, (half + 1) * BLOCK)
                for t in range(TH):
                    sp.dma_start(y[:, t, cols], x[0, t * P:(t + 1) * P, cols])\
                        .then_inc(x_in[2 * half + t], 16)
                for c in range(C_ROWS // 2 * half, C_ROWS // 2 * (half + 1)):
                    rows = w_in[c * TAIL_CK * P:(c + 1) * TAIL_CK * P, TAIL_AT:TAIL_AT + TAIL]
                    load(c, raw[c][:, 0:TAIL_CK * TAIL].rearrange("p (k c) -> p k c", k=TAIL_CK),
                         rows.rearrange("(k p) c -> p k c", p=P))
            with sp.Fori(0, NB) as b:
                for g in range(2):
                    load_group(C_ROWS + g * CPG, w_in, 2 * CPG * b,
                               2 * BLOCK + (NB - 1) * BLOCK + g * GRP - BLOCK * b)
            with sp.Fori(0, 4) as g:
                load_group(C_HEADS, w_in, CPG * g, GRP * g)
            with sp.Fori(0, 8) as g:
                load_group(C_GATES, w_in, CPG * g, GATE_AT + GRP * g)
            with sp.Fori(0, 4) as g:
                load_group(C_BRANCH, w_branch, CPG * g, GRP * g)
            with sp.Fori(0, 4) as g:
                load_group(C_OUT, w_out, CPG * g, GRP * g)
            with sp.Fori(0, NU) as n:
                for b in range(2):
                    load_group(C_UP + b * CPG, w_up, 2 * CPG * n, b * FF + GRP * n)
            with sp.Fori(0, 2) as m:
                load_group(C_DOWN, w_down, FT * m, BLOCK * m, n=FT, width=BLOCK, per=1)
            for m in range(2):
                for t in range(TH):
                    for h in range(2):
                        cols = slice(m * BLOCK + h * GRP, m * BLOCK + (h + 1) * GRP)
                        sp.wait_ge(out_ready, 4 * m + 2 * t + h + 1)
                        sp.dma_start(out[0, t * P:(t + 1) * P, cols], y[:, t, cols])\
                            .then_inc(stored, 16)
            sp.wait_ge(stored, 16 * 4 * TH)

        @block.scalar
        def _(act):
            def split(c0, step=0, slots=1, width=2 * GRP):
                s = c0 % SLOTS
                act.wait_ge(w_landed[s], 16 * (c0 // SLOTS + 1) + 16 * slots * step)
                if c0 >= SLOTS:
                    act.wait_ge(w_used, c0 - SLOTS + 1 + SLOTS * slots * step)
                act.activation(hi[s][:, 0:width], raw[s][:, 0:width], ACT.Copy)\
                    .then_inc(hi_done, 1)

            def norm_rstd(k):
                act.wait_ge(inv_done, k + 1)
                act.activation(rstd2[:, :], inv2[:, :], ACT.Sqrt).then_inc(rstd_done, 1)

            def rms_copy(k):
                act.wait_ge(rms_full, k + 1)
                act.activation(rms_row[:, :], B[0][:, 0:S], ACT.Copy).then_inc(rms_done, 1)

            def transposed_hi(dst, gain, k, kts):
                for kt in kts:
                    act.wait_ge(xT_full, k * KT + kt + 1)
                    act.activation(dst[:, kt, 0:S], B[kt % 4][:, 0:S], ACT.Copy,
                                   scale=params[:, gain + kt:gain + kt + 1]).then_inc(xT_hi, 1)

            prime(act, relu_done)
            act.wait_ge(rows_zero, 1)
            act.dma_start(rows_in[0:KT, 0, :], attn_norm_g.rearrange("(t p) -> t p", p=P))\
                .then_inc(small_in, 16)
            for t in range(TH):
                act.dma_start(pos_i[:, t:t + 1], positions[0, t * P:(t + 1) * P].unsqueeze(1))\
                    .then_inc(pos_in, 16)
            act.wait_ge(warm_set, 1)
            act.activation(warm[:, :], warm[:, :], ACT.Sqrt).then_inc(passed, 1)

            def squares(half, t):
                act.wait_ge(x_in[2 * half + t], 16)
                act.activation(junk[:, t, half * BLOCK:(half + 1) * BLOCK],
                               y[:, t, half * BLOCK:(half + 1) * BLOCK], ACT.Square,
                               accum_out=ss[:, t, half:half + 1]).then_inc(ss_done, 1)

            act.wait_ge(params_T, 1)
            act.activation(params[:, 0:KT], A[3][:, 0:KT], ACT.Copy)\
                .then_inc(params_done, 1)
            act.wait_ge(params_done, 1)
            for c in range(C_ROWS):
                transposed_hi(hT, 0, 0, range(TAIL_CK * c, TAIL_CK * (c + 1)))
                split(c, width=TAIL_CK * TAIL)
                if c == 1:
                    squares(0, 0)
            split(C_ROWS)
            squares(0, 1)
            split(C_ROWS + 1)
            squares(1, 0)
            split(C_ROWS + 2)
            squares(1, 1)
            act.wait_ge(params_T, 2)
            act.activation(params[:, KT:2 * KT + 8 * FT], A[3][:, KT:2 * KT + 8 * FT],
                           ACT.Copy).then_inc(params_done, 1)
            act.wait_ge(w_used, C_ROWS)
            act.activation(tailT[0:TAIL, :], A[2][0:TAIL, S:2 * S], ACT.Copy)\
                .then_inc(tailT_half, 1)

            def rows_body(b, index):
                for g in range(2):
                    for j in range(CPG):
                        split(C_ROWS + AHEAD + g * CPG + j, b, 2 * CPG // SLOTS)
                        if not index:
                            if (g, j) == (0, 1):
                                norm_rstd(0)
                            if (g, j) == (0, 3):
                                act.wait_ge(tail_full, 1)
                                act.wait_ge(rstd_done, 1)
                                for t in range(TH):
                                    act.activation(tail[:, t, :],
                                                   B[1][:, t * TAIL:(t + 1) * TAIL], ACT.Copy,
                                                   scale=rstd2[:, t:t + 1]).then_inc(tok_done, 1)
                            if (g, j) == (0, 5):
                                rms_copy(0)
                            if (g, j) == (0, 6):
                                act.wait_ge(angle_done, 1)
                                act.activation(trig[:, :, :, :], ang[:, :, :, :], ACT.Sin)\
                                    .then_inc(sin_done, 1)
                            if (g, j) == (1, 4):
                                act.wait_ge(kixT_full, 1)
                                act.wait_ge(ikT_zero, 2)
                                for h in range(2):
                                    rows = slice(h * ID, (h + 1) * ID)
                                    act.activation(ikT[rows, h, :], B[0][rows, 0:S], ACT.Copy)\
                                        .then_inc(ikT_hi, 1)
                            continue
                        if g == 0 and j == 5:
                            act.wait_ge(iqT_full, 1 + b)
                            act.activation(iqT[:, :, :].rearrange("p a s -> p (a s)"),
                                           B[0][:, :], ACT.Copy).then_inc(iqT_hi, 1)
                        if g == 1 and j in (1, 5):
                            pair = j // 4
                            at0, at1 = (B[1], B[2]) if pair == 0 else (B[3], B[0])
                            act.wait_ge(sc_full, 4 * (b - 1) + 2 * pair + 1)
                            act.activation(relu[pair][:, :, 0:P],
                                           at0[:, 0:2 * P].rearrange("p (h k) -> p h k", h=2),
                                           ACT.Relu).then_inc(relu_done, 1)
                            act.wait_ge(sc_full, 4 * (b - 1) + 2 * pair + 2)
                            act.activation(relu[pair][:, :, P:KEYS],
                                           at1[:, :].rearrange("p (h k) -> p h k", h=2),
                                           ACT.Relu).then_inc(relu_done, 1)
                    for t in range(TH):
                        wait_full(act, tok_full, 2 * b + g, TH, t,
                                  C_ROWS + CPG * (g + 1) + 2 * CPG * b)
                        act.activation(tok[:, ds(NB - 1 - b, 1), t, g * GRP:(g + 1) * GRP],
                                       A[2 * g + t][:, :].unsqueeze(1), ACT.Copy,
                                       scale=rstd2[:, t:t + 1]).then_inc(tok_done, 1)

            rows_body(0, False)
            with act.Fori(1, NB) as b:
                rows_body(b, True)

            def column_halves(full, done, bank, dst, group, end, tiles=range(4)):
                for ct in tiles:
                    wait_full(act, full, group, 4, ct, end)
                    act.activation(dst[ct][:, :], bank[ct][:, S:2 * S], ACT.Copy).then_inc(done, 1)

            def heads_body(qk, half):
                i = 2 * qk + half
                for j in range(CPG):
                    split(C_HEADS + AHEAD + j, i, CPG // SLOTS)
                    if j == 1:
                        act.activation(sq[:, :, :, :].rearrange("p r h d -> p r (h d)"),
                                       tok[:, 1:3, :, ds(2 * HD * i, 2 * HD)]
                                       .rearrange("p b t c -> p (b t) c"),
                                       ACT.Square).then_inc(sq_done, 1)
                    if j == 3:
                        act.wait_ge(hinv_done, i + 1)
                        act.activation(rstd[:, :], inv[:, :], ACT.Sqrt).then_inc(hrstd_done, 1)
                column_halves(col_full, part_done, A, part, i, C_HEADS + CPG + CPG * i)
                for r in range(2):
                    act.wait_ge(qn_T, 2 * i + r + 1)
                    act.activation(qkT[:, ds(NH + 2 * i, 2), r * S:(r + 1) * S],
                                   B[r][:, :].rearrange("p (h s) -> p h s", h=2),
                                   ACT.Copy).then_inc(qkT_done, 1)

            act.wait_ge(tok_done, 2 + 4 * NB)
            with act.Fori(0, 2) as qk:
                with act.Fori(0, 2) as half:
                    heads_body(qk, half)

            def gates_body(h):
                for j in range(CPG):
                    split(C_GATES + AHEAD + j, h, CPG // SLOTS)
                    if j == 1:
                        act.wait_ge(z_full, h + 1)
                        act.activation(soft[:, :], B[0][:, 0:KEYS], ACT.Abs).then_inc(abs_done, 1)
                        act.wait_ge(abs_done, h + 1)
                        act.activation(soft[:, :], soft[:, :], ACT.Exp, scale=-1.0)\
                            .then_inc(exp_done, 1)
                        act.wait_ge(exp_done, h + 1)
                        act.activation(soft[:, :], soft[:, :], ACT.Ln, bias=1.0)\
                            .then_inc(ln_done, 1)
                    if j == 2:
                        act.wait_ge(ntop_done, h + 1)
                        for t, (k0, k1) in enumerate(((0, P), (P, KEYS))):
                            act.activation(prob[:, k0:k1], logit[:, k0:k1], ACT.Exp,
                                           bias=ntop[:, t:t + 1], scale=SCALE,
                                           accum_out=psum_e[:, t:t + 1]).then_inc(prob_raw, 1)
                    if j == 5:
                        act.wait_ge(suffix_full, h + 1)
                        act.activation(stick[:, :], B[0][:, 0:KEYS], ACT.Exp)\
                            .then_inc(stick_raw, 1)
                    if j == 6:
                        act.wait_ge(probT_full, h + 1)
                        act.activation(probT[:, :], B[3][:, 0:KEYS], ACT.Copy)\
                            .then_inc(probT_done, 1)
                column_halves(col_full, part_done, A, part, 4 + h, C_GATES + CPG + CPG * h)
                for full, done, bank, at_head in ((sb_full, sb_hi, B[2], h),
                                                  (ds_full, ds_hi, B[3], NH + h)):
                    act.wait_ge(full, 1 + h + 1)
                    act.activation(oT[:, ds(at_head, 1), 0:S], bank[:, 0:S].unsqueeze(1),
                                   ACT.Copy).then_inc(done, 1)

            with act.Fori(0, NH) as h:
                gates_body(h)

            def merged_hi(n, ct):
                act.wait_ge(mix_done, 4 * n + ct + 1)
                act.activation(mT[:, ds(4 * n + ct, 1), 0:S], br[0][ct][:, :].unsqueeze(1),
                               ACT.Copy).then_inc(mT_hi, 1)

            def branch_body(n, before):
                for j in range(CPG):
                    split(C_BRANCH + AHEAD + j, n, CPG // SLOTS)
                    if before and j < 4:
                        merged_hi(n - 1, j)
                    if j in (4, 5):
                        for ct in (2 * j - 8, 2 * j - 7):
                            column_halves(col_full, part_done, A, part, 12 + n,
                                          C_BRANCH + CPG // 2 + CPG * n, [ct])
                    if j in (5, 6):
                        for ct in (2 * j - 10, 2 * j - 9):
                            act.activation(sig[0][ct][:, :].unsqueeze(1),
                                           gates[:, ds(4 * n + ct, 1), :],
                                           ACT.Sigmoid).then_inc(sig_done, 1)
                    if j in (6, 7):
                        for ct in (2 * j - 12, 2 * j - 11):
                            act.activation(sig[1][ct][:, :].unsqueeze(1),
                                           gates[:, ds(KT + 4 * n + ct, 1), :],
                                           ACT.Sigmoid).then_inc(sig_done, 1)
                column_halves(bcol_full, bpart_done, B, partb, n, C_BRANCH + CPG + CPG * n)

            act.wait_ge(col_scaled, 12)
            branch_body(0, False)
            with act.Fori(1, 4) as n:
                branch_body(n, True)

            def out_body(m, first):
                for g in range(2):
                    for j in range(CPG):
                        split(C_OUT + AHEAD + g * CPG + j, m, 2 * CPG // SLOTS)
                        if first and g == 0 and 1 <= j < 5:
                            merged_hi(3, j - 1)
                        if not (first and g == 0) and 3 <= j < 7:
                            transposed_hi(h2T, KT, 1, [4 * (2 * m + g) - 4 + j - 3])
                        if not first and g == 0 and j == 0:
                            act.activation(warm[:, :], warm[:, :], ACT.Sqrt).then_inc(passed, 1)
                    for t in range(TH):
                        act.wait_ge(row_done, 4 * m + 2 * g + t + 1)
                        act.wait_ge(ss_done, 2 * TH + 4 * m + 2 * g + t - 1)
                        act.activation(junk2[:, t, :],
                                       y[:, t, ds(GRP * 2 * m + GRP * g, GRP)], ACT.Square,
                                       accum_out=ss[:, t, ds(2 * m + g, 1)]).then_inc(ss_done, 1)

            out_body(0, True)
            out_body(1, False)

            def gate_half(n, ct):
                wait_full(act, col_full, 16 + n, 4, ct, C_UP + CPG + 2 * CPG * n)
                act.activation(u[0][ct][:, 2:S + 2], A[ct][:, S:2 * S], ACT.Copy)\
                    .then_inc(part_done, 1)

            def val_half(n, ct):
                wait_full(act, bcol_full, 4 + n, 4, ct, C_UP + 2 * CPG + 2 * CPG * n)
                act.activation(u[1][ct][:, 2:S + 2], B[ct][:, S:2 * S], ACT.Copy)\
                    .then_inc(bpart_done, 1)

            def gate_silu(n, ct):
                e = 4 * n + ct
                act.wait_ge(gate_w0, e + 1)
                act.activation(silu[ct][:, :], conv[0][ct % 2][:, :], ACT.Silu,
                               bias=params[:, ds(2 * KT + 3 * 2 * FT + e, 1)])\
                    .then_inc(silu_done, 1)

            def ff_hi(n, ct):
                e = 4 * n + ct
                act.wait_ge(act_done, e + 1)
                act.activation(ffT[:, ds(e, 1), 0:S], conv[1][ct % 2][:, :].unsqueeze(1),
                               ACT.Copy).then_inc(ffT_hi, 1)

            def up_step(n, j):
                if j < 4:
                    val_half(n - 1, j)
                if j in (3, 5, 7, 9):
                    ff_hi(n - 1, (j - 3) // 2)

            def gate_step(n, j):
                if j < 4:
                    gate_half(n, j)
                if j in (3, 5, 7):
                    gate_silu(n, (j - 3) // 2)
                if j == 7:
                    gate_silu(n, 3)

            def up_body(n, before):
                for j in range(2 * CPG):
                    split(C_UP + AHEAD + j, n, 2 * CPG // SLOTS)
                    if before:
                        up_step(n, j)
                    elif j == 1:
                        norm_rstd(1)
                    elif 3 <= j < 7:
                        transposed_hi(h2T, KT, 1, [KT - 4 + j - 3])
                    elif j == 7:
                        rms_copy(1)
                    if j >= CPG:
                        gate_step(n, j - CPG)

            up_body(0, False)
            with act.Fori(1, NU) as n:
                up_body(n, True)
            LAST = 3 * SLOTS
            for j in range(LAST):
                split(C_DOWN + AHEAD + j)
                up_step(NU, j)
            left = 2 * FT - AHEAD - LAST
            with act.Fori(0, left // SLOTS) as r:
                for j in range(SLOTS):
                    split(C_DOWN + AHEAD + LAST + j, r)
            for j in range(left - left % SLOTS, left):
                split(C_DOWN + AHEAD + LAST + j)

        @block.vector
        def _(dve):
            def split(c0, step=0, slots=1, width=2 * GRP):
                s = c0 % SLOTS
                dve.wait_ge(hi_done, c0 + 1 + SLOTS * slots * step)
                dve.tensor_tensor(lo[s][:, 0:width], raw[s][:, 0:width],
                                  hi[s][:, 0:width].bitcast(f32), ALU.subtract)\
                    .then_inc(lo_done, 1)

            def mean_squares(k, parts):
                dve.wait_ge(ss_done, 2 * TH + 4 * TH * k)
                dve.tensor_reduce(var2[:, :], ss[:, :, 0:parts], AX.X, ALU.add)\
                    .then_inc(var_done, 1)
                dve.wait_ge(var_done, 2 * k + 1)
                dve.tensor_scalar(var2[:, :], var2[:, :], 1.0 / D, EPS, ALU.mult, ALU.add)\
                    .then_inc(var_done, 1)
                dve.wait_ge(var_done, 2 * k + 2)
                dve.reciprocal(inv2[:, :], var2[:, :]).then_inc(inv_done, 1)

            def rms_diagonal(k):
                dve.wait_ge(rstd_done, k + 1)
                for t in range(TH):
                    dve.tensor_scalar(diag[:, t, :], ident[:, :], rstd2[:, t:t + 1], None,
                                      ALU.mult).then_inc(diag_done, 1)

            def transposed_lo(dst, gain, k, kts):
                for kt in kts:
                    dve.wait_ge(xT_hi, k * KT + kt + 1)
                    dve.scalar_tensor_tensor(
                        dst[:, kt, S:2 * S], B[kt % 4][:, 0:S],
                        params[:, gain + kt:gain + kt + 1], dst[:, kt, 0:S].bitcast(f32),
                        ALU.mult, ALU.subtract).then_inc(xT_lo, 1)

            prime(dve, score_add, taken_done, sb_done, ds_done)
            steps = [0]

            def then(instruction):
                steps[0] += 1
                instruction.then_inc(trig_step, 1)
                dve.wait_ge(trig_step, steps[0])

            def angles():
                dve.wait_ge(pos_in, 16 * TH)
                dve.wait_ge(freq_set, HALF)
                then(dve.tensor_copy(pos_f[:, :], pos_i[:, :]))
                for q in range(2):
                    for t in range(TH):
                        then(dve.tensor_scalar(ang[:, q, t, :], freq[:, :], pos_f[:, t:t + 1], None,
                                               ALU.mult))
                for q in range(2):
                    then(dve.tensor_scalar(turn[:, q, :, :], ang[:, q, :, :], 1.0 / (2 * math.pi),
                                           0.25 * q, ALU.mult, ALU.add))
                then(dve.tensor_scalar(turn[:, :, :, :], turn[:, :, :, :], ROUND, None, ALU.add))
                then(dve.tensor_scalar(turn[:, :, :, :], turn[:, :, :, :], -ROUND, None, ALU.add))

                def flat(t):
                    return t[:, :, :, :].rearrange("p a b c -> p (a b c)")

                for piece in (TWO_PI_A, TWO_PI_B, TWO_PI_C):
                    then(dve.scalar_tensor_tensor(flat(ang), flat(turn), -piece, flat(ang),
                                                  ALU.mult, ALU.add))
                then(dve.tensor_scalar(ang[:, 1, :, :], ang[:, 1, :, :], math.pi / 2, None,
                                       ALU.add))
                dve.tensor_scalar(flat(ang), flat(ang), SIN_MAX, -SIN_MAX, ALU.min, ALU.max)\
                    .then_inc(angle_done, 1)

            dve.wait_ge(params_done, 1)
            for c in range(C_ROWS):
                transposed_lo(hT, 0, 0, range(TAIL_CK * c, TAIL_CK * (c + 1)))
                split(c, width=TAIL_CK * TAIL)
            for c in range(C_ROWS, C_ROWS + AHEAD):
                split(c)
            dve.wait_ge(tailT_half, 1)
            dve.tensor_tensor(tailT[0:TAIL, :], A[2][0:TAIL, 0:S], tailT[0:TAIL, :], ALU.add)\
                .then_inc(tailT_done, 1)

            def tables():
                dve.wait_ge(sin_done, 1)
                for r in range(4):
                    for e in range(2):
                        dve.tensor_copy(cos_d[:, r, e * HALF:(e + 1) * HALF], trig[:, 1, r % 2, :])\
                            .then_inc(cos_set, 1)
                        dve.tensor_scalar(sin_d[:, r, e * HALF:(e + 1) * HALF],
                                          trig[:, 0, r % 2, :], (-1.0, 1.0)[e], None, ALU.mult)\
                            .then_inc(cos_set, 1)
                for e in range(2):
                    cols = slice(e * IHALF, (e + 1) * IHALF)
                    dve.tensor_copy(cos_i[:, :, cols], trig[:, 1, :, 0:HALF:2])\
                        .then_inc(cos_set, 1)
                    dve.tensor_scalar(sin_i[:, :, cols], trig[:, 0, :, 0:HALF:2],
                                      (-1.0, 1.0)[e], None, ALU.mult).then_inc(cos_set, 1)

            halves = ((0, 0, P), (1, P, KEYS))

            def rows_body(b, index):
                for g in range(2):
                    for j in range(CPG):
                        split(C_ROWS + AHEAD + g * CPG + j, b, 2 * CPG // SLOTS)
                        if not index and (g, j) == (0, 0):
                            dve.wait_ge(const_sel, 2)
                            mean_squares(0, 2)
                        if not index and (g, j) == (0, 2):
                            rms_diagonal(0)
                        if not index and (g, j) == (0, 3):
                            angles()
                        if not index and (g, j) == (0, 6):
                            tables()
                        if not index and (g, j) == (0, 4):
                            dve.wait_ge(tok_done, TH)
                            dve.tensor_scalar(wix[:, :, :], tail[:, :, ID:TAIL], IDX_SCALE, None,
                                              ALU.mult).then_inc(wix_done, 1)
                        if not index and (g, j) == (1, 4):
                            dve.wait_ge(ikT_hi, 2)
                            for h in range(2):
                                rows = slice(h * ID, (h + 1) * ID)
                                dve.tensor_tensor(ikT_lo[rows, h, :], B[0][rows, 0:S],
                                                  ikT[rows, h, :].bitcast(f32), ALU.subtract)\
                                    .then_inc(ikT_done, 1)
                        if index and g == 0 and j == 5:
                            dve.wait_ge(iqT_hi, b)
                            dve.tensor_tensor(iqT_lo[:, :, :].rearrange("p a s -> p (a s)"),
                                              B[0][:, :], iqT[:, :, :].bitcast(f32)
                                              .rearrange("p a s -> p (a s)"),
                                              ALU.subtract).then_inc(iqT_done, 1)
                        if index and g == 1 and j in (2, 6):
                            pair = j // 4
                            for h in range(2):
                                for t, k0, k1 in halves:
                                    k = 2 * pair + h
                                    dve.wait_ge(relu_done, 1 + 4 * (b - 1) + 2 * pair + t + 1)
                                    dve.wait_ge(score_add, 1 + 8 * (b - 1) + 2 * k + t)
                                    dve.scalar_tensor_tensor(
                                        scores[:, k0:k1], relu[pair][:, h, k0:k1],
                                        wix[:, t, ds(4 * (b - 1) + k, 1)], scores[:, k0:k1],
                                        ALU.mult, ALU.add).then_inc(score_add, 1)

            rows_body(0, False)
            dve.wait_ge(wix_done, 1)
            dve.wait_ge(score_zero, 1)
            with dve.Fori(1, NB) as b:
                rows_body(b, True)

            def column_sums(ready, done, bank, halves_, count, dst, tiles=range(4)):
                for ct in tiles:
                    dve.wait_ge(ready, count + ct + 1)
                    dve.tensor_tensor(dst(ct), bank[ct][:, 0:S].unsqueeze(1),
                                      halves_[ct][:, :].unsqueeze(1), ALU.add).then_inc(done, 1)

            def scale_columns(tiles, count):
                dve.wait_ge(col_done, count)
                dve.tensor_tensor(tiles, tiles, rms_row[:, :].unsqueeze(1)
                                  .to_broadcast([P, 4, S]), ALU.mult).then_inc(col_scaled, 1)

            ROUNDS = TOPK // 8 // 4

            def take(i, r):
                for t, k0, k1 in halves:
                    n = 2 * ROUNDS * i + 2 * r + t
                    wait_alone(dve, taken_done, 1 + n)
                    dve.max(best[:, t, :], scores[:, k0:k1]).then_inc(best_done, 1)
                    wait_alone(dve, best_done, n + 1)
                    dve.match_replace(scores[:, k0:k1], best[:, t, :], scores[:, k0:k1], TAKEN)\
                        .then_inc(taken_done, 1)

            def heads_body(qk, half):
                i = 2 * qk + half
                for j in range(CPG):
                    split(C_HEADS + AHEAD + j, i, CPG // SLOTS)
                    if j == 2:
                        dve.wait_ge(sq_done, i + 1)
                        dve.tensor_reduce(ms[:, :], sq[:, :, :, :].rearrange(
                            "p r h d -> p (r h) d"), AX.X, ALU.add).then_inc(ms_done, 1)
                        dve.wait_ge(ms_done, i + 1)
                        dve.tensor_scalar(ms[:, :], ms[:, :], 1.0 / HD, EPS, ALU.mult, ALU.add)\
                            .then_inc(msv_done, 1)
                        dve.wait_ge(msv_done, i + 1)
                        dve.reciprocal(inv[:, :], ms[:, :]).then_inc(hinv_done, 1)
                    if j == 4:
                        dve.wait_ge(hrstd_done, i + 1)
                        for r in range(4):
                            dve.tensor_tensor(
                                qn[:, r, :, :],
                                tok[:, 1 + r // 2, r % 2, ds(2 * HD * i, 2 * HD)]
                                .rearrange("p (h d) -> p h d", h=2),
                                rstd[:, 2 * r:2 * r + 2].unsqueeze(2).to_broadcast([P, 2, HD]),
                                ALU.mult).then_inc(qn_scaled, 1)
                    if j in (3, 5):
                        take(i, j // 4)
                column_sums(part_done, col_done, A, part, 4 * i,
                            lambda ct: qkT[:, ds(4 * half + ct, 1), ds(S * qk, S)])
                scale_columns(qkT[:, ds(4 * half, 4), ds(S * qk, S)], 4 * i + 4)

            dve.wait_ge(rms_done, 1)
            dve.wait_ge(score_masked, 1)
            with dve.Fori(0, 2) as qk:
                with dve.Fori(0, 2) as half:
                    heads_body(qk, half)

            dve.wait_ge(taken_done, 1 + 2 * TOPK // 8)
            dve.tensor_scalar(bias[:, :], scores[:, :], (NONCAUSAL + TAKEN) / 2, MASKED,
                              ALU.is_gt, ALU.mult).then_inc(bias_raw, 1)

            def gates_body(h):
                for j in range(CPG):
                    split(C_GATES + AHEAD + j, h, CPG // SLOTS)
                    if j == 1:
                        dve.wait_ge(logit_full, h + 1)
                        dve.wait_ge(bias_done, 1)
                        dve.tensor_tensor(logit[:, :], B[1][:, 0:KEYS], bias[:, :], ALU.add)\
                            .then_inc(logit_done, 1)
                        dve.wait_ge(logit_done, h + 1)
                        for t, k0, k1 in halves:
                            dve.tensor_reduce(top[:, t:t + 1], logit[:, k0:k1], AX.X, ALU.max)\
                                .then_inc(top_done, 1)
                        dve.wait_ge(top_done, 2 * h + 2)
                        dve.tensor_scalar(ntop[:, :], top[:, :], -SCALE, None, ALU.mult)\
                            .then_inc(ntop_done, 1)
                    if j == 2:
                        dve.wait_ge(ln_done, h + 1)
                        dve.scalar_tensor_tensor(stay[:, :], B[0][:, 0:KEYS], 0.0, soft[:, :],
                                                 ALU.max, ALU.add).then_inc(stay_raw, 1)
                    if j == 3:
                        dve.wait_ge(prob_raw, 2 * h + 2)
                        dve.reciprocal(pinv[:, :], psum_e[:, :]).then_inc(pinv_done, 1)
                column_sums(part_done, col_done, A, part, 16 + 4 * h,
                            lambda ct: gates[:, ds(4 * h + ct, 1), :])
                scale_columns(gates[:, ds(4 * h, 4), :], 16 + 4 * h + 4)
                for ready, done, bank, at_head in ((sb_hi, sb_done, B[2], h),
                                                   (ds_hi, ds_done, B[3], NH + h)):
                    dve.wait_ge(ready, h + 1)
                    dve.tensor_tensor(oT[:, ds(at_head, 1), S:2 * S], bank[:, 0:S].unsqueeze(1),
                                      oT[:, ds(at_head, 1), 0:S].bitcast(f32), ALU.subtract)\
                        .then_inc(done, 1)

            with dve.Fori(0, NH) as h:
                gates_body(h)

            def merged_lo(n, ct):
                dve.wait_ge(mT_hi, 4 * n + ct + 1)
                dve.tensor_tensor(mT[:, ds(4 * n + ct, 1), S:2 * S],
                                  br[0][ct][:, :].unsqueeze(1),
                                  mT[:, ds(4 * n + ct, 1), 0:S].bitcast(f32), ALU.subtract)\
                    .then_inc(mT_done, 1)

            def branch_body(n, before):
                for j in range(CPG):
                    split(C_BRANCH + AHEAD + j, n, CPG // SLOTS)
                    if before and j < 4:
                        merged_lo(n - 1, j)
                    if before and j == 4:
                        dve.wait_ge(mT_done, 4 * n)
                    if j in (4, 5):
                        column_sums(part_done, col_done, A, part, 48 + 4 * n,
                                    lambda ct: br[0][ct][:, :].unsqueeze(1),
                                    (2 * j - 8, 2 * j - 7))
                column_sums(bpart_done, bcol_done, B, partb, 4 * n,
                            lambda ct: br[1][ct][:, :].unsqueeze(1))

            branch_body(0, False)
            with dve.Fori(1, 4) as n:
                branch_body(n, True)

            def out_body(m, first):
                for g in range(2):
                    for j in range(CPG):
                        split(C_OUT + AHEAD + g * CPG + j, m, 2 * CPG // SLOTS)
                        if first and g == 0 and 1 <= j < 5:
                            merged_lo(3, j - 1)
                        if not (first and g == 0) and 3 <= j < 7:
                            transposed_lo(h2T, KT, 1, [4 * (2 * m + g) - 4 + j - 3])
                    if first and g == 0:
                        dve.wait_ge(x_again, 16)
                        for b in range(2):
                            for i in range(4):
                                dve.memset(u[b][i][:, 0:2], 0.0).then_inc(pad_zero, 1)
                    for t in range(TH):
                        wait_full(dve, row_full, 2 * m + g, TH, t,
                                  C_OUT + CPG * (g + 1) + 2 * CPG * m)
                        cols = y[:, t, ds(GRP * 2 * m + GRP * g, GRP)]
                        dve.tensor_tensor(cols, A[2 * g + t][:, :], cols, ALU.add)\
                            .then_inc(row_done, 1)

            out_body(0, True)
            out_body(1, False)
            dve.wait_ge(pad_zero, 8)

            def u_sum(b, n, ct):
                ready, full_at, done = ((part_done, 64, col_done), (bpart_done, 16, bcol_done))[b]
                dve.wait_ge(ready, full_at + 4 * n + ct + 1)
                dve.tensor_tensor(u[b][ct][:, 2:S + 2], (A, B)[b][ct][:, 0:S],
                                  u[b][ct][:, 2:S + 2], ALU.add).then_inc(done, 1)

            def neighbours(b, n, ct):
                e = 4 * n + ct
                w2, w1, w0 = ((gate_w2, gate_w1, gate_w0), (val_w2, val_w1, val_w0))[b]
                for k, before, done in ((1, w2, w1), (0, w1, w0)):
                    column = 2 * KT + 2 * FT * k + b * FT
                    dve.wait_ge(before, e + 1)
                    dve.scalar_tensor_tensor(conv[b][ct % 2][:, :], u[b][ct][:, k:k + S],
                                             params[:, ds(column + e, 1)], conv[b][ct % 2][:, :],
                                             ALU.mult, ALU.add).then_inc(done, 1)

            def ff_lo(n, ct):
                e = 4 * n + ct
                dve.wait_ge(ffT_hi, e + 1)
                dve.tensor_tensor(ffT[:, ds(e, 1), S:2 * S], conv[1][ct % 2][:, :].unsqueeze(1),
                                  ffT[:, ds(e, 1), 0:S].bitcast(f32), ALU.subtract)\
                    .then_inc(ffT_done, 1)

            def up_step(n, j):
                if j < 4:
                    u_sum(1, n - 1, j)
                if j in (1, 3, 5, 7):
                    neighbours(1, n - 1, j // 2)
                if j in (4, 6, 8, 10):
                    ff_lo(n - 1, (j - 4) // 2)

            def gate_step(n, j):
                if j < 4:
                    u_sum(0, n, j)
                if j % 2:
                    neighbours(0, n, j // 2)

            def up_body(n, before):
                for j in range(2 * CPG):
                    split(C_UP + AHEAD + j, n, 2 * CPG // SLOTS)
                    if before:
                        up_step(n, j)
                    elif j == 0:
                        mean_squares(1, 4)
                    elif j == 2:
                        rms_diagonal(1)
                    elif 3 <= j < 7:
                        transposed_lo(h2T, KT, 1, [KT - 4 + j - 3])
                    if j >= CPG:
                        gate_step(n, j - CPG)

            up_body(0, False)
            with dve.Fori(1, NU) as n:
                up_body(n, True)
            LAST = 3 * SLOTS
            for j in range(LAST):
                split(C_DOWN + AHEAD + j)
                up_step(NU, j)

            def add_rows(m):
                for t in range(TH):
                    for g in range(2):
                        cols = y[:, t, m * BLOCK + g * GRP:m * BLOCK + (g + 1) * GRP]
                        wait_full(dve, down_full, m, 4, 2 * t + g, C_DOWN + FT * (m + 1))
                        dve.tensor_tensor(cols, A[2 * t + g][:, :], cols, ALU.add)\
                            .then_inc(out_ready, 1)

            first = C_DOWN + AHEAD + LAST
            with dve.Fori(0, (FT - LAST) // SLOTS) as r:
                for j in range(SLOTS):
                    split(first + j, r)
            add_rows(0)
            second = first + FT - LAST
            left = FT - AHEAD
            with dve.Fori(0, left // SLOTS) as r:
                for j in range(SLOTS):
                    split(second + j, r)
            for j in range(left - left % SLOTS, left):
                split(second + j)
            add_rows(1)

        @block.gpsimd
        def _(pool):
            pool.memset(rows_in[:, :, :], 0.0).then_inc(rows_zero, 1)
            pool.memset(ident[:, :], 0.0).then_inc(const_set, 1)
            pool.memset(neg_tri[:, :], -1.0).then_inc(const_set, 1)
            pool.memset(neg_one[:, :], -1.0).then_inc(const_set, 1)
            pool.wait_ge(const_set, 3)
            pool.affine_select(out=ident[:, :], in_=ident[:, :], compare_op=ALU.not_equal,
                               fill=1.0, base=0, pattern=[[-1, P]], channel_multiplier=1)\
                .then_inc(const_sel, 1)
            pool.affine_select(out=neg_tri[:, :], in_=neg_tri[:, :], compare_op=ALU.is_ge,
                               fill=0.0, base=0, pattern=[[-1, P]], channel_multiplier=1)\
                .then_inc(const_sel, 1)
            pool.memset(warm[:, :], 1.0).then_inc(warm_set, 1)
            pool.wait_ge(rows_zero, 1)
            pool.dma_start(rows_in[0:KT, 1, :], ffn_norm_g.rearrange("(t p) -> t p", p=P))\
                .then_inc(conv_in, 16)
            pool.dma_start(rows_in[0:2 * FT, 2:5, :], conv_w.rearrange("k (t p) -> t k p", p=P))\
                .then_inc(conv_in, 16)
            pool.dma_start(rows_in[0:2 * FT, 5, :], conv_b.rearrange("(t p) -> t p", p=P))\
                .then_inc(conv_in, 16)
            pool.dma_start(qk_gain[:, 0, :], q_norm_g.partition_broadcast(P))\
                .then_inc(gain_in, 16)
            pool.dma_start(qk_gain[:, 1, :], k_norm_g.partition_broadcast(P))\
                .then_inc(gain_in, 16)
            for i, f in enumerate(FREQS):
                pool.memset(freq[:, i:i + 1], f).then_inc(freq_set, 1)
            pool.memset(one[:, :], 1.0).then_inc(scale_set, 1)
            pool.memset(sb_scale[:, :], SCALE).then_inc(scale_set, 1)
            pool.memset(ikT[:, :, :].bitcast(f32), 0.0).then_inc(ikT_zero, 1)
            pool.memset(ikT_lo[:, :, :].bitcast(f32), 0.0).then_inc(ikT_zero, 1)
            pool.memset(scores[:, :], 0.0).then_inc(score_zero, 1)

            def rotate(dst, src, rot, cos, sin, heads, half, sem_mid, count, sem_end):
                rows = cos.shape[1]
                c = cos[:, :, :].unsqueeze(2).to_broadcast([P, rows, heads, 2 * half])
                s = sin[:, :, :].unsqueeze(2).to_broadcast([P, rows, heads, 2 * half])
                pool.tensor_tensor(rot[:, 0], src(0, 2 * half), c, ALU.mult).then_inc(sem_mid, 1)
                pool.tensor_tensor(rot[:, 1, :, :, 0:half], src(half, 2 * half),
                                   s[:, :, :, 0:half], ALU.mult).then_inc(sem_mid, 1)
                pool.tensor_tensor(rot[:, 1, :, :, half:2 * half], src(0, half),
                                   s[:, :, :, half:2 * half], ALU.mult).then_inc(sem_mid, 1)
                pool.wait_ge(sem_mid, count)
                pool.tensor_tensor(dst, rot[:, 0], rot[:, 1], ALU.add).then_inc(sem_end, 1)

            pool.wait_ge(tok_done, TH)
            pool.wait_ge(cos_set, 20)
            for e in range(2):
                pool.tensor_copy(k_ix[:, :, e, 2 * IHALF:ID], tail[:, :, 2 * IHALF:ID])\
                    .then_inc(kix_a, 1)
            rotate(k_ix[:, :, :, 0:2 * IHALF],
                   lambda a, b: tail[:, :, a:b].unsqueeze(2).to_broadcast([P, TH, 2, b - a]),
                   rot_k, cos_i, sin_i, 2, IHALF, kix_b, 3, kix_done)

            with pool.Fori(1, NB) as b:
                q4 = tok[:, NB - 1, :, ds(4 * ID * (b - 1), 4 * ID)]\
                    .rearrange("p t (h d) -> p t h d", h=4)
                pool.wait_ge(tok_done, 2 + 4)
                pool.wait_ge(iqT_full, 1 + b - 1)
                for t in range(TH):
                    pool.tensor_copy(iq[:, t, :, 2 * IHALF:ID], q4[:, t, :, 2 * IHALF:ID])\
                        .then_inc(iq_done, 1)
                rotate(iq[:, :, :, 0:2 * IHALF], lambda c0, c1: q4[:, :, :, c0:c1], rot_i, cos_i,
                       sin_i, 4, IHALF, iq_rot, 3 * b, iq_done)

            pool.wait_ge(score_add, 1 + 2 * NI)
            diagonal = lambda t: t[:, :].rearrange("p (b c) -> p b c", b=3)[:, 0:3:2, :]
            pool.affine_select(out=diagonal(scores), in_=diagonal(scores), compare_op=ALU.is_ge,
                               fill=NONCAUSAL, base=0, pattern=[[0, 2], [-1, P]],
                               channel_multiplier=1).then_inc(score_masked, 1)

            pool.wait_ge(gain_in, 16 * 2)

            def gains_body(i):
                pool.wait_ge(qn_scaled, 4 * i + 4)
                for r in range(4):
                    pool.tensor_tensor(
                        qn[:, r, :, :], qn[:, r, :, :],
                        qk_gain[:, r // 2:r // 2 + 1, :].to_broadcast([P, 2, HD]),
                        ALU.mult).then_inc(qn_gain, 1)
                pool.wait_ge(qn_gain, 4 * i + 4)
                rotate(qn[:, :, :, 0:2 * HALF], lambda c0, c1: qn[:, :, :, c0:c1], rot_d, cos_d,
                       sin_d, 2, HALF, qn_rot, 3 * i + 3, qn_done)

            pool.wait_ge(scale_set, 2)

            def stage_sb(h):
                pool.tensor_tensor(sb_k[:, :].unsqueeze(1), qkT[:, ds(h, 1), S:2 * S],
                                   sb_scale[:, :].unsqueeze(1).to_broadcast([P, 1, S]),
                                   ALU.mult).then_inc(staged_qk, 1)
                pool.tensor_copy(sb_q[:, :].unsqueeze(1), qkT[:, ds(h, 1), 0:S])\
                    .then_inc(staged_qk, 1)

            def stage_ds(h):
                pool.tensor_copy(ds_qk[:, :].unsqueeze(1), qkT[:, ds(NH + h, 1), :])\
                    .then_inc(staged_qk, 1)

            with pool.Fori(0, 3) as i:
                gains_body(i)
            pool.wait_ge(col_scaled, 3)
            pool.wait_ge(qkT_done, 2)
            stage_sb(0)
            stage_ds(0)
            gains_body(3)

            pool.wait_ge(bias_raw, 1)
            pool.affine_select(out=diagonal(bias), in_=diagonal(bias), compare_op=ALU.is_ge,
                               fill=MASKED, base=0, pattern=[[0, 2], [-1, P]],
                               channel_multiplier=1).then_inc(bias_done, 1)

            def head_body(h, more):
                pool.wait_ge(ds_full, 1 + h)
                pool.tensor_copy(sb_v[:, :, :], tok[:, 0, :, ds(HD * h, HD)]).then_inc(staged_v, 1)
                pool.tensor_copy(ds_v[:, :, :], tok[:, 3, :, ds(HD * h, HD)]).then_inc(staged_v, 1)
                wait_alone(pool, stay_raw, h + 1)
                pool.affine_select(out=diagonal(stay), in_=diagonal(stay), compare_op=ALU.is_gt,
                                   fill=0.0, base=0, pattern=[[0, 2], [1, P]],
                                   channel_multiplier=-1).then_inc(stay_done, 1)
                wait_alone(pool, pinv_done, h + 1)
                for t, (k0, k1) in enumerate(((0, P), (P, KEYS))):
                    pool.tensor_scalar(prob[:, k0:k1], prob[:, k0:k1], pinv[:, t:t + 1], None,
                                       ALU.mult).then_inc(prob_done, 1)
                if more:
                    pool.wait_ge(logit_full, h + 1)
                    stage_sb(h + 1)
                wait_alone(pool, stick_raw, h + 1)
                pool.affine_select(out=diagonal(stick), in_=diagonal(stick), compare_op=ALU.is_gt,
                                   fill=0.0, base=0, pattern=[[0, 2], [1, P]],
                                   channel_multiplier=-1).then_inc(stick_done, 1)
                if more:
                    stage_ds(h + 1)

            pool.wait_ge(col_scaled, 4)
            pool.wait_ge(qkT_done, 8)
            with pool.Fori(0, NH - 1) as h:
                head_body(h, True)
            head_body(NH - 1, False)

            def mix_body(n, last):
                for ct in range(4):
                    pool.wait_ge(sig_done, 8 * n + ct + 1)
                    pool.wait_ge(col_done, 48 + 4 * n + ct + 1)
                    pool.tensor_tensor(br[0][ct][:, :], br[0][ct][:, :], sig[0][ct][:, :],
                                       ALU.mult).then_inc(mix_a, 1)
                if last:
                    pool.wait_ge(sig_done, 32)
                    pool.dma_start(y[:, :, :], x[0, :, :].rearrange("(t p) d -> p t d", p=P))\
                        .then_inc(x_again, 16)
                for ct in range(4):
                    pool.wait_ge(sig_done, 8 * n + 4 + ct + 1)
                    pool.wait_ge(bcol_done, 4 * n + ct + 1)
                    pool.tensor_tensor(br[1][ct][:, :], br[1][ct][:, :], sig[1][ct][:, :],
                                       ALU.mult).then_inc(mix_b, 1)
                    pool.wait_ge(mix_a, 4 * n + ct + 1)
                    pool.wait_ge(mix_b, 4 * n + ct + 1)
                    pool.tensor_tensor(br[0][ct][:, :], br[0][ct][:, :], br[1][ct][:, :],
                                       ALU.add).then_inc(mix_done, 1)

            with pool.Fori(0, 3) as n:
                mix_body(n, False)
            mix_body(3, True)

            def column(first, e):
                return params[:, ds(first + e, 1)].to_broadcast([P, S])

            CONV_B = 2 * KT + 3 * 2 * FT

            def begin(b, n, ct, ready, at_, done):
                e = 4 * n + ct
                if not isinstance(e, int) or e >= 2:
                    pool.wait_ge((silu_done, ffT_done)[b], e - 1)
                pool.wait_ge(ready, at_ + e + 1)
                pool.tensor_tensor(u[b][ct][:, 2:S + 2], u[b][ct][:, 2:S + 2], rms_row[:, :],
                                   ALU.mult).then_inc((gate_scaled, val_scaled)[b], 1)
                pool.wait_ge((gate_scaled, val_scaled)[b], e + 1)
                pool.tensor_tensor(conv[b][ct % 2][:, :], u[b][ct][:, 2:S + 2],
                                   column(2 * KT + 2 * FT * 2 + b * FT, e), ALU.mult)\
                    .then_inc(done, 1)

            def gate_tiles(n):
                for ct in range(4):
                    begin(0, n, ct, col_done, 64, gate_w2)

            def val_tiles(n):
                for ct in range(4):
                    e = 4 * n + ct
                    c = conv[1][ct % 2][:, :]
                    begin(1, n, ct, bcol_done, 16, val_w2)
                    pool.wait_ge(val_w0, e + 1)
                    pool.tensor_tensor(c, c, column(CONV_B + FT, e), ALU.add)\
                        .then_inc(val_bias, 1)
                    pool.wait_ge(val_bias, e + 1)
                    pool.wait_ge(silu_done, e + 1)
                    pool.tensor_tensor(c, c, silu[ct][:, :], ALU.mult).then_inc(act_done, 1)

            pool.wait_ge(rms_done, 2)
            gate_tiles(0)
            val_tiles(0)
            gate_tiles(1)
            with pool.Fori(2, NU) as n:
                val_tiles(n - 1)
                gate_tiles(n)
            val_tiles(NU - 1)

        @block.tensor
        def _(pe):
            def mm(o, l, r, start, stop):
                return pe.matmul(o, l, r, start=start, stop=stop, skip_group_check=True)

            def rows_chunk(c, slot, src, kts, width, outs, first, last, free, full):
                n = len(kts)
                wh = hi[slot][:, 0:n * width].rearrange("p (k c) -> p k c", k=n)
                wl = lo[slot][:, 0:n * width].rearrange("p (k c) -> p k c", k=n)
                pe.wait_ge(lo_done, c)
                for o, (bank, t, c0, c1) in enumerate(outs):
                    if first and free is not None:
                        free(o)
                    out_ = bank[:, 0:c1 - c0]
                    for j, kt in enumerate(kts):
                        xh = src[:, kt, t * P:(t + 1) * P]
                        xl = src[:, kt, S + t * P:S + (t + 1) * P]
                        mm(out_, xh, wh[:, j, c0:c1], first and j == 0, False)
                        mm(out_, xl, wh[:, j, c0:c1], False, False)
                        i = mm(out_, xh, wl[:, j, c0:c1], False, last and j == n - 1)
                    if last and o < len(outs) - 1:
                        i.then_inc(full, 1)
                i.then_inc(w_used, 1)

            def cols_chunk(c, slot, src, kts, bank, first, last, free, full):
                wh = hi[slot][:, :].rearrange("p (k c) -> p k c", k=CK)
                wl = lo[slot][:, :].rearrange("p (k c) -> p k c", k=CK)
                pe.wait_ge(lo_done, c)
                for ct in range(4):
                    if first and free is not None:
                        free(ct)
                    cs = slice(ct * P, (ct + 1) * P)
                    for j, kt in enumerate(kts):
                        if not (first and j == 0):
                            mm(bank[ct][:, 0:S], wl[:, j, cs], src[:, kt, 0:S], False, False)
                        i = mm(bank[ct][:, :], wh[:, j, cs], src[:, kt, :], first and j == 0,
                               last and j == CK - 1)
                        if first and j == 0:
                            mm(bank[ct][:, 0:S], wl[:, j, cs], src[:, kt, 0:S], False, False)
                    if last and ct < 3:
                        i.then_inc(full, 1)
                i.then_inc(w_used, 1)

            def transposes(k, kts, src):
                for kt in kts:
                    if kt >= 4:
                        pe.wait_ge(xT_lo, k * KT + kt - 3)
                    for t in range(TH):
                        i = pe.transpose(B[kt % 4][:, t * P:(t + 1) * P],
                                         src[:, t, kt * P:(kt + 1) * P], ident[:, :])
                    i.then_inc(xT_full, 1)

            def spread_rms(k):
                pe.wait_ge(scale_set, 1)
                pe.wait_ge(diag_done, TH * (k + 1))
                pe.wait_ge(xT_lo, KT * (k + 1) - 3)
                for t in range(TH):
                    i = mm(B[0][:, t * P:(t + 1) * P], one[:, :], diag[:, t, :], True, True)
                i.then_inc(rms_full, 1)

            prime(pe, iqT_full, sb_full, ds_full)

            def keep_warm(count):
                for _ in range(count):
                    pe.transpose(A[0][:, 0:P], ident[:, :], ident[:, :])

            pe.wait_ge(const_sel, 2)
            keep_warm(14)
            pe.wait_ge(small_in, 16)
            pe.transpose(A[3][:, 0:KT], rows_in[0:KT, 0, :], ident[0:KT, 0:KT])\
                .then_inc(params_T, 1)
            for t in range(TH):
                pe.wait_ge(x_in[t], 16)
            transposes(0, range(TAIL_CK), y)
            for c in range(C_ROWS):
                if c == 1:
                    for t in range(TH):
                        pe.wait_ge(x_in[2 + t], 16)
                if c + 1 < C_ROWS:
                    transposes(0, range(TAIL_CK * (c + 1), TAIL_CK * (c + 2)), y)
                pe.wait_ge(xT_lo, TAIL_CK * (c + 1))
                wh = hi[c][:, 0:TAIL_CK * TAIL].rearrange("p (k c) -> p k c", k=TAIL_CK)
                wl = lo[c][:, 0:TAIL_CK * TAIL].rearrange("p (k c) -> p k c", k=TAIL_CK)
                pe.wait_ge(lo_done, c + 1)
                for j in range(TAIL_CK):
                    kt = TAIL_CK * c + j
                    mm(A[2][0:TAIL, :], wh[:, j, :], hT[:, kt, :], kt == 0, False)
                    i = mm(A[2][0:TAIL, 0:S], wl[:, j, :], hT[:, kt, 0:S], False, kt == KT - 1)
                i.then_inc(w_used, 1)
            pe.wait_ge(conv_in, 16 * 3)
            pe.wait_ge(params_done, 1)
            pe.transpose(A[3][:, KT:2 * KT], rows_in[0:KT, 1, :], ident[0:KT, 0:KT])
            for k in range(4):
                at_ = 2 * KT + 2 * FT * k
                i = pe.transpose(A[3][:, at_:at_ + 2 * FT], rows_in[0:2 * FT, 2 + k, :],
                                 ident[0:2 * FT, 0:2 * FT])
            i.then_inc(params_T, 1)

            def rows_body(b, index):
                for g in range(2):
                    def free(t):
                        if index:
                            pe.wait_ge(tok_done, 2 + 4 * (b - 1) + 2 * g + t + 1)
                        elif g == 1:
                            pe.wait_ge(params_done, 2)
                    for j in range(CPG):
                        rows_chunk(C_ROWS + g * CPG + j + 1 + 2 * CPG * b, j % SLOTS, hT,
                                   range(CK * j, CK * (j + 1)), GRP,
                                   [(A[2 * g + t], t, 0, GRP) for t in range(TH)], j == 0,
                                   j == CPG - 1, free, tok_full)
                        if not index:
                            if (g, j) == (0, 2):
                                pe.wait_ge(tailT_done, 1)
                                for t in range(TH):
                                    i = pe.transpose(B[1][:, t * TAIL:(t + 1) * TAIL],
                                                     tailT[0:TAIL, t * P:(t + 1) * P],
                                                     ident[0:TAIL, 0:TAIL])
                                i.then_inc(tail_full, 1)
                            if (g, j) == (0, 4):
                                spread_rms(0)
                            if (g, j) == (1, 3):
                                pe.wait_ge(kix_a, 2)
                                pe.wait_ge(kix_done, 1)
                                for t in range(TH):
                                    i = pe.transpose(
                                        B[0][:, t * P:(t + 1) * P],
                                        k_ix[:, t, :, :].rearrange("p e d -> p (e d)"),
                                        ident[:, :])
                                i.then_inc(kixT_full, 1)
                            continue
                        if g == 0 and j == 3:
                            pe.wait_ge(iq_done, 3 * b)
                            pe.wait_ge(relu_done, 1 + 4 * (b - 1))
                            pe.wait_ge(ikT_done, 2)
                            for p2 in range(2):
                                for t in range(TH):
                                    i = pe.transpose(
                                        B[0][:, (2 * p2 + t) * P:(2 * p2 + t + 1) * P],
                                        iq[:, t, 2 * p2:2 * p2 + 2, :]
                                        .rearrange("p h d -> p (h d)"), ident[:, :])
                            i.then_inc(iqT_full, 1)
                        if (g, j) in ((0, 7), (1, 3)):
                            pair = g
                            at0, at1 = (B[1], B[2]) if pair == 0 else (B[3], B[0])
                            pe.wait_ge(iqT_done, b)
                            for out_, q, k in ((at0[:, 0:2 * P], slice(0, P), slice(0, P)),
                                               (at1[:, :], slice(P, S), slice(0, S))):
                                mm(out_, iqT[:, pair, q], ikT[:, :, k], True, False)
                                mm(out_, iqT_lo[:, pair, q], ikT[:, :, k], False, False)
                                mm(out_, iqT[:, pair, q], ikT_lo[:, :, k], False, True)\
                                    .then_inc(sc_full, 1)

            rows_body(0, False)
            with pe.Fori(1, NB) as b:
                rows_body(b, True)

            def heads_body(i):
                def free(ct):
                    pe.wait_ge(col_done, 4 * i - 4 + ct + 1)
                first_group = isinstance(i, int)

                def free0(ct):
                    pe.wait_ge(tok_done, 4 * NB + max(0, ct - 1))
                for j in range(CPG):
                    cols_chunk(C_HEADS + CPG * i + j + 1, j % SLOTS, hT,
                               range(CK * j, CK * (j + 1)), A, j == 0, j == CPG - 1,
                               free0 if first_group else free, col_full)
                    if j == 7:
                        if first_group:
                            pe.wait_ge(relu_done, 1 + NI)
                        pe.wait_ge(qn_done, i + 1)
                        pe.wait_ge(qkT_done, 2 * i)
                        for r in range(2):
                            for h in range(2):
                                for t in range(TH):
                                    k = pe.transpose(
                                        B[r][:, (2 * h + t) * P:(2 * h + t + 1) * P],
                                        qn[:, 2 * r + t, h, :], ident[:, :])
                            k.then_inc(qn_T, 1)

            heads_body(0)
            with pe.Fori(1, 4) as i:
                heads_body(i)

            with pe.Fori(0, NH) as h:
                def free_gate(ct):
                    pe.wait_ge(col_done, 16 + 4 * h - 4 + ct + 1)
                for j in range(CPG):
                    cols_chunk(C_GATES + CPG * h + j + 1, j % SLOTS, hT,
                               range(CK * j, CK * (j + 1)), A, j == 0, j == CPG - 1,
                               free_gate, col_full)
                    if j == 0:
                        pe.wait_ge(staged_qk, 3 * h + 3)
                        pe.wait_ge(qkT_done, 8)
                        mm(B[0][:, 0:S], sb_k[:, 0:P], sb_q[:, :], True, True)
                        mm(B[0][:, S:KEYS], sb_k[:, P:S], sb_q[:, P:S], False, True)\
                            .then_inc(z_full, 1)
                        mm(B[1][:, 0:P], ds_qk[:, 0:P], ds_qk[:, S:S + P], True, True)
                        mm(B[1][:, P:KEYS], ds_qk[:, P:S], ds_qk[:, S:2 * S], True, True)\
                            .then_inc(logit_full, 1)
                    if j == 3:
                        pe.wait_ge(stay_done, h + 1)
                        mm(B[0][:, S:KEYS], neg_tri[:, :], stay[:, S:KEYS], False, True)
                        mm(B[0][:, P:S], neg_one[:, :], stay[:, S:KEYS], False, True)
                        mm(B[0][:, 0:S], neg_tri[:, :], stay[:, 0:S], False, True)\
                            .then_inc(suffix_full, 1)
                    if j == 4:
                        pe.wait_ge(prob_done, 2 * h + 2)
                        pe.wait_ge(ds_done, 1 + h)
                        for k in range(3):
                            i = pe.transpose(B[3][:, k * P:(k + 1) * P],
                                             prob[:, k * P:(k + 1) * P], ident[:, :])
                        i.then_inc(probT_full, 1)
                for bank, v, w, full, ready, done in (
                        (B[2], sb_v, stick, sb_full, stick_done, sb_done),
                        (B[3], ds_v, probT, ds_full, probT_done, None)):
                        pe.wait_ge(ready, h + 1)
                        if done is not None:
                            pe.wait_ge(done, 1 + h)
                        pe.wait_ge(staged_v, 2 * h + 2)
                        mm(bank[:, 0:S], v[:, 0, :], w[:, 0:S], True, True)
                        mm(bank[:, P:S], v[:, 1, :], w[:, S:KEYS], False, True).then_inc(full, 1)

            def branch_body(n):
                first_group = isinstance(n, int)

                def free_sb(ct):
                    pe.wait_ge(col_done, 48 + 4 * n - 4 + ct + 1)

                def free_ds(ct):
                    if not first_group:
                        pe.wait_ge(bcol_done, 4 * n - 4 + ct + 1)
                for j in range(CPG):
                    if first_group and j < 4:
                        pe.wait_ge(sb_done, 1 + CK * (j + 1))
                    if first_group and j == 4:
                        pe.wait_ge(ds_done, 1 + NH)
                    cols_chunk(C_BRANCH + CPG * n + j + 1, j % SLOTS, oT,
                               range(CK * j, CK * (j + 1)), (A, B)[j // 4], j % 4 == 0,
                               j % 4 == 3, (free_sb, free_ds)[j // 4],
                               (col_full, bcol_full)[j // 4])

            branch_body(0)
            with pe.Fori(1, 4) as n:
                branch_body(n)

            for m in range(2):
                for g in range(2):
                    def free_row(t):
                        if m == 0:
                            pe.wait_ge(col_done, 64)
                        else:
                            pe.wait_ge(row_done, 4 * (m - 1) + 2 * g + t + 1)
                    for j in range(CPG):
                        if m == 0 and g == 0:
                            pe.wait_ge(mT_done, CK * (j + 1))
                        rows_chunk(C_OUT + CPG * (2 * m + g) + j + 1, j % SLOTS, mT,
                                   range(CK * j, CK * (j + 1)), GRP,
                                   [(A[2 * g + t], t, 0, GRP) for t in range(TH)], j == 0,
                                   j == CPG - 1, free_row, row_full)
                        if (m, g) != (0, 0) and 1 <= j < 5:
                            pe.wait_ge(row_done, TH * (2 * m + g))
                            pe.wait_ge(bcol_done, 16)
                            transposes(1, [4 * (2 * m + g) - 4 + j - 1], y)

            def up_body(n):
                first_pair = isinstance(n, int)

                def free_a(ct):
                    if first_pair:
                        pe.wait_ge(row_done, 6 + max(0, ct - 1))
                    else:
                        pe.wait_ge(col_done, 64 + 4 * n - 4 + ct + 1)

                def free_b(ct):
                    if first_pair:
                        pe.wait_ge(rms_done, 2)
                    else:
                        pe.wait_ge(bcol_done, 16 + 4 * n - 4 + ct + 1)
                for b in range(2):
                    for j in range(CPG):
                        if first_pair and b == 0:
                            pe.wait_ge(xT_lo, KT + CK * (j + 1))
                        cols_chunk(C_UP + b * CPG + 2 * CPG * n + j + 1, j % SLOTS, h2T,
                                   range(CK * j, CK * (j + 1)), (A, B)[b], j == 0,
                                   j == CPG - 1, (free_a, free_b)[b],
                                   (col_full, bcol_full)[b])
                        if first_pair and b == 0 and 1 <= j < 5:
                            pe.wait_ge(row_done, 4 * TH)
                            transposes(1, [KT - 4 + j - 1], y)
                        if first_pair and b == 0 and j == 5:
                            spread_rms(1)

            up_body(0)
            with pe.Fori(1, NU) as n:
                up_body(n)

            for m in range(2):
                def free_down(o):
                    if m == 0:
                        pe.wait_ge(col_done, 64 + 4 * NU)
                    else:
                        pe.wait_ge(out_ready, 4 * (m - 1) + o + 1)
                for k in range(FT):
                    if m == 0:
                        pe.wait_ge(ffT_done, k + 1)
                    rows_chunk(C_DOWN + FT * m + k + 1, k % SLOTS, ffT, [k], BLOCK,
                               [(A[2 * t + g], t, g * GRP, (g + 1) * GRP)
                                for t in range(TH) for g in range(2)], k == 0,
                               k == FT - 1, free_down, down_full)


_INS = ["x", "positions", "attn_norm_g", "w_in", "q_norm_g", "k_norm_g", "w_branch", "w_out",
        "ffn_norm_g", "w_up", "conv_w", "conv_b", "w_down"]


def kernel(**inputs):
    import concourse.bacc as bacc
    from concourse.bass_utils import run_bass_kernel_spmd

    nc = bacc.Bacc("TRN2", target_bir_lowering=False, num_devices=1)
    arrays, args = {}, []
    for name in _INS:
        a = np.ascontiguousarray(inputs[name])
        arrays[f"in_{name}"] = a
        args.append(nc.dram_tensor(f"in_{name}", a.shape, mybir.dt.from_np(a.dtype),
                                   kind="ExternalInput").ap())
    shape = inputs["x"].shape
    out = nc.dram_tensor("out", shape, mybir.dt.float32, kind="ExternalOutput").ap()
    hybrid_layer(nc, *args, out)
    r = run_bass_kernel_spmd(nc, [arrays], core_ids=[0])
    return r.results[0]["out"]
```
